# Optimizing a Trainium2 kernel written in Bass

```python
import math
import jax, jax.numpy as jnp
from jax import lax
import numpy as np
import jax
import jax.numpy as jnp

D_MODEL = 1024
BATCH = 1
SEQ = 256
DEPTH = 2

D_MIX = D_MODEL
D_FF = 2816
NORM_EPS = 1e-6
CONV_W = 4
A_WIDTH = 384
A_HEADS = 6
A_HEAD_DIM = A_WIDTH // A_HEADS
LRU_C = 8.0
B_WIDTH = 384
B_HEADS = 6
B_HEAD_DIM = B_WIDTH // B_HEADS
B_GROUPS = 2
B_STATE = 128
B_CHUNK = 128
B_CONV_DIM = B_WIDTH + 2 * B_GROUPS * B_STATE
B_IN = B_WIDTH + B_CONV_DIM + B_HEADS
C_WIDTH = 256
C_GROUPS = 4
C_GROUP_DIM = C_WIDTH // C_GROUPS
C_CHUNK = 128
IN_COLS = 2 * A_WIDTH + B_IN + 2 * C_WIDTH


def rms_norm(x, g):
    xf = x.astype(jnp.float32)
    y = xf * lax.rsqrt(jnp.mean(xf * xf, axis=-1, keepdims=True) + NORM_EPS)
    return (y * g.astype(jnp.float32)).astype(x.dtype)

def layer_norm(x, g, b):
    xf = x.astype(jnp.float32)
    mu = jnp.mean(xf, axis=-1, keepdims=True)
    xc = xf - mu
    y = xc * lax.rsqrt(jnp.mean(xc * xc, axis=-1, keepdims=True) + NORM_EPS)
    return (y * g.astype(jnp.float32) + b.astype(jnp.float32)).astype(x.dtype)

def swiglu(x, w_gu, w_down):
    g, u = jnp.split(x @ w_gu, 2, axis=-1)
    return (jax.nn.silu(g) * u) @ w_down

def causal_dwconv(x, w, b):
    c = x.shape[-1]
    y = lax.conv_general_dilated(
        x, w[:, None, :].astype(x.dtype), window_strides=(1,),
        padding=((CONV_W - 1, 0),), dimension_numbers=("NWC", "WIO", "NWC"),
        feature_group_count=c)
    return y + b

def rg_lru(x, w_r, b_r, w_i, b_i, lam):
    bsz, s, _ = x.shape
    xh = x.reshape(bsz, s, A_HEADS, A_HEAD_DIM)
    r = jax.nn.sigmoid(jnp.einsum("bshi,hij->bshj", xh, w_r).reshape(bsz, s, A_WIDTH) + b_r)
    i = jax.nn.sigmoid(jnp.einsum("bshi,hij->bshj", xh, w_i).reshape(bsz, s, A_WIDTH) + b_i)
    log_a = -LRU_C * r.astype(jnp.float32) * jax.nn.softplus(-lam.astype(jnp.float32))
    a = jnp.exp(log_a)
    mult = jnp.sqrt(-jnp.expm1(2.0 * log_a))
    u = mult * (i * x).astype(jnp.float32)

    def combine(left, right):
        a1, b1 = left
        a2, b2 = right
        return a1 * a2, a2 * b1 + b2

    _, h = lax.associative_scan(combine, (a, u), axis=1)
    return h.astype(x.dtype)

def segsum(a):
    t = a.shape[-1]
    cs = jnp.cumsum(a, axis=-1)
    diff = cs[..., :, None] - cs[..., None, :]
    mask = jnp.tril(jnp.ones((t, t), dtype=bool))
    return jnp.where(mask, diff, -jnp.inf)

def ssd_mixer(zxbcdt, conv_w, conv_b, dt_bias, a_log, d_skip, norm_g):
    bsz, s, _ = zxbcdt.shape
    f32 = jnp.float32
    nc = s // B_CHUNK
    hpg = B_HEADS // B_GROUPS
    z, xbc, dt = jnp.split(zxbcdt, [B_WIDTH, B_WIDTH + B_CONV_DIM], axis=-1)
    xbc = jax.nn.silu(causal_dwconv(xbc, conv_w, conv_b))
    xs, bm, cm = jnp.split(xbc, [B_WIDTH, B_WIDTH + B_GROUPS * B_STATE], axis=-1)
    dt = jax.nn.softplus(dt.astype(f32) + dt_bias.astype(f32))
    a = -jnp.exp(a_log.astype(f32))
    x_c = xs.astype(f32).reshape(bsz, nc, B_CHUNK, B_GROUPS, hpg, B_HEAD_DIM)
    dt_c = dt.reshape(bsz, nc, B_CHUNK, B_GROUPS, hpg)
    xdt = x_c * dt_c[..., None]
    ad = jnp.moveaxis((dt * a).reshape(bsz, nc, B_CHUNK, B_GROUPS, hpg), 2, -1)
    b_c = bm.astype(f32).reshape(bsz, nc, B_CHUNK, B_GROUPS, B_STATE)
    c_c = cm.astype(f32).reshape(bsz, nc, B_CHUNK, B_GROUPS, B_STATE)
    a_cs = jnp.cumsum(ad, axis=-1)
    lmat = jnp.exp(segsum(ad))
    cb = jnp.einsum("bclgn,bcsgn->bcgls", c_c, b_c)
    y_diag = jnp.einsum("bcgjls,bcsgjp->bclgjp", cb[:, :, :, None] * lmat, xdt)
    decay_states = jnp.exp(a_cs[..., -1:] - a_cs)
    chunk_states = jnp.einsum("bclgn,bcgjl,bclgjp->bcgjpn", b_c, decay_states, xdt)
    chunk_decay = jnp.exp(a_cs[..., -1])

    def step(h, inp):
        st, dc = inp
        return dc[..., None, None] * h + st, h

    h0 = jnp.zeros((bsz, B_GROUPS, hpg, B_HEAD_DIM, B_STATE), f32)
    _, prev = lax.scan(step, h0, (jnp.moveaxis(chunk_states, 1, 0), jnp.moveaxis(chunk_decay, 1, 0)))
    prev = jnp.moveaxis(prev, 0, 1)
    y_off = jnp.einsum("bclgn,bcgjpn,bcgjl->bclgjp", c_c, prev, jnp.exp(a_cs))
    y = y_diag + y_off + x_c * d_skip.astype(f32).reshape(B_GROUPS, hpg)[:, :, None]
    y = y.reshape(bsz, s, B_WIDTH)
    y = rms_norm(y * jax.nn.silu(z.astype(f32)), norm_g)
    return y.astype(zxbcdt.dtype)

def chunk_sgu(uv, ln_g, ln_b, w_s, b_s):
    bsz, s, _ = uv.shape
    nc = s // C_CHUNK
    u, v = jnp.split(jax.nn.gelu(uv), 2, axis=-1)
    v = layer_norm(v, ln_g, ln_b)
    vc = v.reshape(bsz, nc, C_CHUNK, C_GROUPS, C_GROUP_DIM)
    mask = jnp.tril(jnp.ones((C_CHUNK, C_CHUNK), dtype=bool))
    w = jnp.where(mask, w_s, jnp.zeros_like(w_s))
    mixed = jnp.einsum("gts,bcsgd->bctgd", w, vc) + jnp.swapaxes(b_s, 0, 1)[:, :, None]
    return u * mixed.reshape(bsz, s, C_WIDTH)

def hybrid_mixer(h, w_in, w_out, lru_conv_w, lru_conv_b, lru_w_r, lru_b_r, lru_w_i, lru_b_i, lru_lambda,
                 ssd_conv_w, ssd_conv_b, ssd_dt_bias, ssd_a_log, ssd_d, ssd_norm_g,
                 sgu_ln_g, sgu_ln_b, sgu_w_s, sgu_b_s):
    proj = h @ w_in
    pa, pb, pc = jnp.split(proj, [2 * A_WIDTH, 2 * A_WIDTH + B_IN], axis=-1)
    gate_a, rec_a = jnp.split(pa, 2, axis=-1)
    rec = causal_dwconv(rec_a, lru_conv_w, lru_conv_b)
    ya = rg_lru(rec, lru_w_r, lru_b_r, lru_w_i, lru_b_i, lru_lambda) * jax.nn.gelu(gate_a)
    yb = ssd_mixer(pb, ssd_conv_w, ssd_conv_b, ssd_dt_bias, ssd_a_log, ssd_d, ssd_norm_g)
    yc = chunk_sgu(pc, sgu_ln_g, sgu_ln_b, sgu_w_s, sgu_b_s)
    return jnp.concatenate([ya, yb, yc], axis=-1) @ w_out

def first_inputs(seed: int = 0) -> dict:
    key = jax.random.key(seed)
    ks = iter(jax.random.split(key, 40))
    f32 = jnp.float32
    L = DEPTH

    def nrm(shape, scale):
        return jax.random.normal(next(ks), shape, f32) * scale

    def gain(shape):
        return 1.0 + 0.05 * jax.random.normal(next(ks), shape, f32)

    x = jax.random.normal(next(ks), (BATCH, SEQ, D_MODEL), f32)
    ffn1_pre_g = gain((L, D_MODEL))
    ffn1_post_g = gain((L, D_MODEL))
    ffn1_w_gu = nrm((L, D_MODEL, 2 * D_FF), D_MODEL ** -0.5)
    ffn1_w_down = nrm((L, D_FF, D_MODEL), D_FF ** -0.5)
    mix_pre_g = gain((L, D_MODEL))
    mix_post_g = gain((L, D_MODEL))
    mix_w_in = nrm((L, D_MODEL, IN_COLS), D_MODEL ** -0.5)
    mix_w_out = nrm((L, D_MIX, D_MODEL), D_MIX ** -0.5)
    lru_conv_w = nrm((L, CONV_W, A_WIDTH), CONV_W ** -0.5)
    lru_conv_b = nrm((L, A_WIDTH), 0.02)
    lru_w_r = nrm((L, A_HEADS, A_HEAD_DIM, A_HEAD_DIM), A_HEAD_DIM ** -0.5)
    lru_b_r = nrm((L, A_WIDTH), 0.02)
    lru_w_i = nrm((L, A_HEADS, A_HEAD_DIM, A_HEAD_DIM), A_HEAD_DIM ** -0.5)
    lru_b_i = nrm((L, A_WIDTH), 0.02)
    a_c = jax.random.uniform(next(ks), (L, A_WIDTH), f32, 0.9, 0.999)
    a0 = a_c ** (1.0 / LRU_C)
    lru_lambda = jnp.log(a0) - jnp.log1p(-a0)
    ssd_conv_w = nrm((L, CONV_W, B_CONV_DIM), CONV_W ** -0.5)
    ssd_conv_b = nrm((L, B_CONV_DIM), 0.02)
    dt0 = jnp.exp(jax.random.uniform(next(ks), (L, B_HEADS), f32, math.log(1e-3), math.log(1e-1)))
    ssd_dt_bias = dt0 + jnp.log(-jnp.expm1(-dt0))
    ssd_a_log = jnp.log(jax.random.uniform(next(ks), (L, B_HEADS), f32, 1.0, 16.0))
    ssd_d = 1.0 + 0.1 * jax.random.normal(next(ks), (L, B_HEADS), f32)
    ssd_norm_g = gain((L, B_WIDTH))
    sgu_ln_g = gain((L, C_WIDTH))
    sgu_ln_b = nrm((L, C_WIDTH), 0.02)
    sgu_w_s = nrm((L, C_GROUPS, C_CHUNK, C_CHUNK), C_CHUNK ** -0.5)
    sgu_b_s = 1.0 + 0.1 * jax.random.normal(next(ks), (L, C_GROUPS, C_CHUNK), f32)
    ffn2_pre_g = gain((L, D_MODEL))
    ffn2_post_g = gain((L, D_MODEL))
    ffn2_w_gu = nrm((L, D_MODEL, 2 * D_FF), D_MODEL ** -0.5)
    ffn2_w_down = nrm((L, D_FF, D_MODEL), D_FF ** -0.5)
    return {
        "x": x,
        "ffn1_pre_g": ffn1_pre_g, "ffn1_post_g": ffn1_post_g,
        "ffn1_w_gu": ffn1_w_gu, "ffn1_w_down": ffn1_w_down,
        "mix_pre_g": mix_pre_g, "mix_post_g": mix_post_g,
        "mix_w_in": mix_w_in, "mix_w_out": mix_w_out,
        "lru_conv_w": lru_conv_w, "lru_conv_b": lru_conv_b,
        "lru_w_r": lru_w_r, "lru_b_r": lru_b_r,
        "lru_w_i": lru_w_i, "lru_b_i": lru_b_i, "lru_lambda": lru_lambda,
        "ssd_conv_w": ssd_conv_w, "ssd_conv_b": ssd_conv_b,
        "ssd_dt_bias": ssd_dt_bias, "ssd_a_log": ssd_a_log,
        "ssd_d": ssd_d, "ssd_norm_g": ssd_norm_g,
        "sgu_ln_g": sgu_ln_g, "sgu_ln_b": sgu_ln_b,
        "sgu_w_s": sgu_w_s, "sgu_b_s": sgu_b_s,
        "ffn2_pre_g": ffn2_pre_g, "ffn2_post_g": ffn2_post_g,
        "ffn2_w_gu": ffn2_w_gu, "ffn2_w_down": ffn2_w_down,
    }

def first_block(x, ffn1_pre_g, ffn1_post_g, ffn1_w_gu, ffn1_w_down,
              mix_pre_g, mix_post_g, mix_w_in, mix_w_out,
              lru_conv_w, lru_conv_b, lru_w_r, lru_b_r, lru_w_i, lru_b_i, lru_lambda,
              ssd_conv_w, ssd_conv_b, ssd_dt_bias, ssd_a_log, ssd_d, ssd_norm_g,
              sgu_ln_g, sgu_ln_b, sgu_w_s, sgu_b_s,
              ffn2_pre_g, ffn2_post_g, ffn2_w_gu, ffn2_w_down):
    for l in range(DEPTH):
        f = swiglu(rms_norm(x, ffn1_pre_g[l]), ffn1_w_gu[l], ffn1_w_down[l])
        x = x + 0.5 * rms_norm(f, ffn1_post_g[l])
        m = hybrid_mixer(rms_norm(x, mix_pre_g[l]), mix_w_in[l], mix_w_out[l],
                         lru_conv_w[l], lru_conv_b[l], lru_w_r[l], lru_b_r[l],
                         lru_w_i[l], lru_b_i[l], lru_lambda[l],
                         ssd_conv_w[l], ssd_conv_b[l], ssd_dt_bias[l], ssd_a_log[l],
                         ssd_d[l], ssd_norm_g[l],
                         sgu_ln_g[l], sgu_ln_b[l], sgu_w_s[l], sgu_b_s[l])
        x = x + rms_norm(m, mix_post_g[l])
        f = swiglu(rms_norm(x, ffn2_pre_g[l]), ffn2_w_gu[l], ffn2_w_down[l])
        x = x + 0.5 * rms_norm(f, ffn2_post_g[l])
    return x


DEPTH_2 = 1

SSM_WIDTH = D_MODEL // 2
SSM_GROUP = 16
SSM_GROUPS = SSM_WIDTH // SSM_GROUP
SSM_STATE = 64
DT_MIN = 1e-3
DT_MAX = 1e-1
CONV_CH = D_MODEL // 2
CONV_K = 3
HEAD_DIM = 64
N_HEADS = (D_MODEL // 2) // HEAD_DIM
N_KV_HEADS = 2
GQA = N_HEADS // N_KV_HEADS
ATTN_WIDTH = N_HEADS * HEAD_DIM
KV_WIDTH = N_KV_HEADS * HEAD_DIM
CMP_BLOCK = 32
SEL_BLOCK = 64
N_SELECT = 16
WINDOW = 512
CMP_HIDDEN = 256
Q_CHUNK = 64
FORCE_SCORE = 1e4
NSA_BRANCHES = 3
MIX_BRANCHES = 3
D_FF_2 = -(-8 * D_MODEL // (3 * 256)) * 256
RMS_EPS = 1e-6
IN_WIDTH = SSM_WIDTH + 3 * CONV_CH + ATTN_WIDTH + 6 * KV_WIDTH + N_HEADS * NSA_BRANCHES + MIX_BRANCHES * D_MODEL


def rms_norm_2(x, g):
    xf = x.astype(jnp.float32)
    y = xf * lax.rsqrt(jnp.mean(xf * xf, axis=-1, keepdims=True) + RMS_EPS)
    return (y * g.astype(jnp.float32)).astype(x.dtype)

def masked_softmax(s, mask):
    s = jnp.where(mask, s, -jnp.inf)
    m = jnp.max(s, axis=-1, keepdims=True)
    m = jnp.where(jnp.isfinite(m), m, 0.0)
    e = jnp.exp(s - m)
    return e / jnp.maximum(jnp.sum(e, axis=-1, keepdims=True), 1e-30)

def split_projection(z):
    sizes = ([SSM_WIDTH, CONV_CH, CONV_CH, CONV_CH, ATTN_WIDTH] + [KV_WIDTH] * 6
             + [N_HEADS * NSA_BRANCHES, MIX_BRANCHES * D_MODEL])
    return jnp.split(z, np.cumsum(sizes)[:-1].tolist(), axis=-1)

def s5_mixer(u, lam_re, lam_im, b_re, b_im, c_re, c_im, d_skip, log_dt, w_glu):
    bsz, seq, _ = u.shape
    f32 = jnp.float32
    uf = u.astype(f32).reshape(bsz, seq, SSM_GROUPS, SSM_GROUP)
    lam = lax.complex(lam_re.astype(f32), lam_im.astype(f32))
    dt = jnp.exp(log_dt.astype(f32))[:, None]
    lam_bar = jnp.exp(lam * dt)
    b = lax.complex(b_re.astype(f32), b_im.astype(f32))
    b_bar = ((lam_bar - 1.0) / lam)[..., None] * b
    c = lax.complex(c_re.astype(f32), c_im.astype(f32))
    bu = jnp.einsum('bsgh,gph->bsgp', uf.astype(jnp.complex64), b_bar)
    a = jnp.broadcast_to(lam_bar, bu.shape)

    def combine(left, right):
        a_l, b_l = left
        a_r, b_r = right
        return a_r * a_l, a_r * b_l + b_r

    _, states = lax.associative_scan(combine, (a, bu), axis=1)
    y = jnp.einsum('bsgp,ghp->bsgh', states, c).real + d_skip.astype(f32).reshape(SSM_GROUPS, SSM_GROUP) * uf
    y = jax.nn.gelu(y.reshape(bsz, seq, SSM_WIDTH)).astype(u.dtype)
    y_lin, y_gate = jnp.split(y @ w_glu, 2, axis=-1)
    return y_lin * jax.nn.sigmoid(y_gate)

def short_conv_mixer(xin, gate_b, gate_c, conv_w, w_out):
    z = gate_c * xin
    z = lax.conv_general_dilated(z, conv_w[:, None, :], window_strides=(1,), padding=[(CONV_K - 1, 0)],
                                 dimension_numbers=('NWC', 'WIO', 'NWC'), feature_group_count=CONV_CH)
    return (gate_b * z) @ w_out

def nsa_mixer(q, k_cmp, v_cmp, k_sel, v_sel, k_win, v_win, gate_logits,
              q_norm_g, k_norm_g, cmp_pe, cmp_w1, cmp_w2, w_o):
    bsz, seq, _ = q.shape
    f32 = jnp.float32
    scale = HEAD_DIM ** -0.5
    pos = jnp.arange(seq)

    def heads(t, n):
        return t.reshape(bsz, seq, n, HEAD_DIM)

    q = rms_norm_2(heads(q, N_HEADS), q_norm_g).reshape(bsz, seq, N_KV_HEADS, GQA, HEAD_DIM)

    n_cmp = seq // CMP_BLOCK

    def compress(t, which):
        blocks = heads(t, N_KV_HEADS).reshape(bsz, n_cmp, CMP_BLOCK, N_KV_HEADS, HEAD_DIM) + cmp_pe[which][:, None, :]
        blocks = blocks.transpose(0, 1, 3, 2, 4).reshape(bsz, n_cmp, N_KV_HEADS, CMP_BLOCK * HEAD_DIM)
        return jax.nn.gelu(blocks @ cmp_w1[which]) @ cmp_w2[which]

    kc = rms_norm_2(compress(k_cmp, 0), k_norm_g[0])
    vc = compress(v_cmp, 1)
    s = jnp.einsum('bqhgd,bchd->bhgqc', q, kc).astype(f32) * scale
    cmp_end = (jnp.arange(n_cmp) + 1) * CMP_BLOCK - 1
    p_cmp = masked_softmax(s, cmp_end[None, :] <= pos[:, None])
    o_cmp = jnp.einsum('bhgqc,bchd->bqhgd', p_cmp.astype(vc.dtype), vc)

    n_blocks = seq // SEL_BLOCK
    n_top = min(N_SELECT, n_blocks)
    imp = jnp.sum(p_cmp, axis=2).reshape(bsz, N_KV_HEADS, seq, n_blocks, SEL_BLOCK // CMP_BLOCK).sum(-1)
    blk = jnp.arange(n_blocks)[None, :]
    cur = (pos // SEL_BLOCK)[:, None]
    forced = (blk == 0) | (blk == cur) | (blk == cur - 1)
    visible = blk * SEL_BLOCK <= pos[:, None]
    imp = jnp.where(forced, FORCE_SCORE, jnp.where(visible, imp, -jnp.inf))
    _, sel_idx = lax.top_k(imp, n_top)

    ks_blocks = rms_norm_2(heads(k_sel, N_KV_HEADS), k_norm_g[1]).reshape(
        bsz, n_blocks, SEL_BLOCK, N_KV_HEADS, HEAD_DIM).transpose(0, 3, 1, 2, 4)
    vs_blocks = heads(v_sel, N_KV_HEADS).reshape(
        bsz, n_blocks, SEL_BLOCK, N_KV_HEADS, HEAD_DIM).transpose(0, 3, 1, 2, 4)
    pad = ((0, 0), (WINDOW, 0), (0, 0), (0, 0))
    kw_pad = jnp.pad(rms_norm_2(heads(k_win, N_KV_HEADS), k_norm_g[2]), pad)
    vw_pad = jnp.pad(heads(v_win, N_KV_HEADS), pad)
    b_ix = jnp.arange(bsz)[:, None, None, None]
    h_ix = jnp.arange(N_KV_HEADS)[None, :, None, None]
    n_sel_keys = n_top * SEL_BLOCK

    def query_chunk(c):
        start = c * Q_CHUNK
        t = start + jnp.arange(Q_CHUNK)
        qc = lax.dynamic_slice_in_dim(q, start, Q_CHUNK, axis=1)
        idx = lax.dynamic_slice_in_dim(sel_idx, start, Q_CHUNK, axis=2)
        kg = ks_blocks[b_ix, h_ix, idx].reshape(bsz, N_KV_HEADS, Q_CHUNK, n_sel_keys, HEAD_DIM)
        vg = vs_blocks[b_ix, h_ix, idx].reshape(bsz, N_KV_HEADS, Q_CHUNK, n_sel_keys, HEAD_DIM)
        key_pos = (idx[..., None] * SEL_BLOCK + jnp.arange(SEL_BLOCK)).reshape(bsz, N_KV_HEADS, Q_CHUNK, n_sel_keys)
        s_sel = jnp.einsum('bqhgd,bhqkd->bhgqk', qc, kg).astype(f32) * scale
        p_sel = masked_softmax(s_sel, (key_pos <= t[:, None])[:, :, None])
        o_sel = jnp.einsum('bhgqk,bhqkd->bqhgd', p_sel.astype(vg.dtype), vg)
        kwc = lax.dynamic_slice_in_dim(kw_pad, start, Q_CHUNK + WINDOW, axis=1)
        vwc = lax.dynamic_slice_in_dim(vw_pad, start, Q_CHUNK + WINDOW, axis=1)
        wpos = (start - WINDOW + jnp.arange(Q_CHUNK + WINDOW))[None, :]
        wmask = (wpos <= t[:, None]) & (wpos > t[:, None] - WINDOW) & (wpos >= 0)
        s_win = jnp.einsum('bqhgd,bkhd->bhgqk', qc, kwc).astype(f32) * scale
        p_win = masked_softmax(s_win, wmask)
        o_win = jnp.einsum('bhgqk,bkhd->bqhgd', p_win.astype(vwc.dtype), vwc)
        return o_sel, o_win

    o_sel, o_win = lax.map(query_chunk, jnp.arange(seq // Q_CHUNK))

    def unchunk(o):
        return jnp.moveaxis(o, 0, 1).reshape(bsz, seq, N_KV_HEADS, GQA, HEAD_DIM)

    g = jax.nn.sigmoid(gate_logits.astype(f32)).reshape(bsz, seq, N_KV_HEADS, GQA, NSA_BRANCHES).astype(q.dtype)
    o = g[..., 0:1] * o_cmp + g[..., 1:2] * unchunk(o_sel) + g[..., 2:3] * unchunk(o_win)
    return o.reshape(bsz, seq, ATTN_WIDTH) @ w_o

def second_inputs(seed: int = 0) -> dict:
    key = jax.random.key(seed)
    ks = jax.random.split(key, 24)
    f32 = jnp.float32
    nl, G, P, H = DEPTH_2, SSM_GROUPS, SSM_STATE, SSM_GROUP

    def nrm(k, shape, scale):
        return scale * jax.random.normal(k, shape, f32)

    return {
        'x': nrm(ks[0], (BATCH, SEQ, D_MODEL), 1.0),
        'mix_norm_g': 1.0 + nrm(ks[1], (nl, D_MODEL), 0.02),
        'w_in': nrm(ks[2], (nl, D_MODEL, IN_WIDTH), D_MODEL ** -0.5),
        'ssm_lam_re': -0.5 + nrm(ks[3], (nl, G, P), 0.01),
        'ssm_lam_im': jnp.pi * jnp.arange(P, dtype=f32) + nrm(ks[4], (nl, G, P), 0.01),
        'ssm_b_re': nrm(ks[5], (nl, G, P, H), (2 * H) ** -0.5),
        'ssm_b_im': nrm(ks[6], (nl, G, P, H), (2 * H) ** -0.5),
        'ssm_c_re': nrm(ks[7], (nl, G, H, P), 0.5 ** 0.5),
        'ssm_c_im': nrm(ks[8], (nl, G, H, P), 0.5 ** 0.5),
        'ssm_d': nrm(ks[9], (nl, SSM_WIDTH), 1.0),
        'ssm_log_dt': jax.random.uniform(ks[10], (nl, G), f32, float(np.log(DT_MIN)), float(np.log(DT_MAX))),
        'ssm_w_glu': nrm(ks[11], (nl, SSM_WIDTH, 2 * D_MODEL), SSM_WIDTH ** -0.5),
        'conv_w': nrm(ks[12], (nl, CONV_K, CONV_CH), CONV_K ** -0.5),
        'conv_w_out': nrm(ks[13], (nl, CONV_CH, D_MODEL), CONV_CH ** -0.5),
        'q_norm_g': 1.0 + nrm(ks[14], (nl, HEAD_DIM), 0.02),
        'k_norm_g': 1.0 + nrm(ks[15], (nl, NSA_BRANCHES, HEAD_DIM), 0.02),
        'cmp_pe': nrm(ks[16], (nl, 2, CMP_BLOCK, HEAD_DIM), 0.1),
        'cmp_w1': nrm(ks[17], (nl, 2, CMP_BLOCK * HEAD_DIM, CMP_HIDDEN), (CMP_BLOCK * HEAD_DIM) ** -0.5),
        'cmp_w2': nrm(ks[18], (nl, 2, CMP_HIDDEN, HEAD_DIM), CMP_HIDDEN ** -0.5),
        'nsa_w_o': nrm(ks[19], (nl, ATTN_WIDTH, D_MODEL), ATTN_WIDTH ** -0.5),
        'w_out': nrm(ks[20], (nl, D_MODEL, D_MODEL), D_MODEL ** -0.5),
        'ffn_norm_g': 1.0 + nrm(ks[21], (nl, D_MODEL), 0.02),
        'ffn_w_gate_up': nrm(ks[22], (nl, D_MODEL, 2 * D_FF_2), D_MODEL ** -0.5),
        'ffn_w_down': nrm(ks[23], (nl, D_FF_2, D_MODEL), D_FF_2 ** -0.5),
    }

def second_block(x, mix_norm_g, w_in, ssm_lam_re, ssm_lam_im, ssm_b_re, ssm_b_im, ssm_c_re, ssm_c_im,
              ssm_d, ssm_log_dt, ssm_w_glu, conv_w, conv_w_out, q_norm_g, k_norm_g, cmp_pe, cmp_w1,
              cmp_w2, nsa_w_o, w_out, ffn_norm_g, ffn_w_gate_up, ffn_w_down):
    bsz, seq, _ = x.shape
    for i in range(DEPTH_2):
        h = rms_norm_2(x, mix_norm_g[i])
        (u, c_b, c_c, c_x, q, k_c, v_c, k_s, v_s, k_w, v_w, nsa_gates, mix_gates) = split_projection(h @ w_in[i])
        y_ssm = s5_mixer(u, ssm_lam_re[i], ssm_lam_im[i], ssm_b_re[i], ssm_b_im[i], ssm_c_re[i], ssm_c_im[i],
                         ssm_d[i], ssm_log_dt[i], ssm_w_glu[i])
        y_conv = short_conv_mixer(c_x, c_b, c_c, conv_w[i], conv_w_out[i])
        y_attn = nsa_mixer(q, k_c, v_c, k_s, v_s, k_w, v_w, nsa_gates, q_norm_g[i], k_norm_g[i],
                           cmp_pe[i], cmp_w1[i], cmp_w2[i], nsa_w_o[i])
        gates = jax.nn.sigmoid(mix_gates.astype(jnp.float32)).astype(x.dtype).reshape(bsz, seq, MIX_BRANCHES, D_MODEL)
        mixed = gates[:, :, 0] * y_ssm + gates[:, :, 1] * y_conv + gates[:, :, 2] * y_attn
        x = x + mixed @ w_out[i]
        h = rms_norm_2(x, ffn_norm_g[i])
        f_gate, f_up = jnp.split(h @ ffn_w_gate_up[i], 2, axis=-1)
        x = x + (jax.nn.silu(f_gate) * f_up) @ ffn_w_down[i]
    return x


def setup_inputs(seed=0):
    out = dict(first_inputs(seed))
    for name, value in second_inputs(seed + 1).items():
        if name != "x":
            out[name + "_2"] = value
    return out


def reference(
    x, ffn1_pre_g, ffn1_post_g, ffn1_w_gu, ffn1_w_down, mix_pre_g, mix_post_g, mix_w_in,
    mix_w_out, lru_conv_w, lru_conv_b, lru_w_r, lru_b_r, lru_w_i, lru_b_i, lru_lambda,
    ssd_conv_w, ssd_conv_b, ssd_dt_bias, ssd_a_log, ssd_d, ssd_norm_g, sgu_ln_g, sgu_ln_b,
    sgu_w_s, sgu_b_s, ffn2_pre_g, ffn2_post_g, ffn2_w_gu, ffn2_w_down, mix_norm_g_2, w_in_2,
    ssm_lam_re_2, ssm_lam_im_2, ssm_b_re_2, ssm_b_im_2, ssm_c_re_2, ssm_c_im_2, ssm_d_2,
    ssm_log_dt_2, ssm_w_glu_2, conv_w_2, conv_w_out_2, q_norm_g_2, k_norm_g_2, cmp_pe_2,
    cmp_w1_2, cmp_w2_2, nsa_w_o_2, w_out_2, ffn_norm_g_2, ffn_w_gate_up_2, ffn_w_down_2,
):
    x = first_block(
        x, ffn1_pre_g, ffn1_post_g, ffn1_w_gu, ffn1_w_down, mix_pre_g, mix_post_g, mix_w_in,
        mix_w_out, lru_conv_w, lru_conv_b, lru_w_r, lru_b_r, lru_w_i, lru_b_i, lru_lambda,
        ssd_conv_w, ssd_conv_b, ssd_dt_bias, ssd_a_log, ssd_d, ssd_norm_g, sgu_ln_g, sgu_ln_b,
        sgu_w_s, sgu_b_s, ffn2_pre_g, ffn2_post_g, ffn2_w_gu, ffn2_w_down,
    )
    return second_block(
        x, mix_norm_g_2, w_in_2, ssm_lam_re_2, ssm_lam_im_2, ssm_b_re_2, ssm_b_im_2, ssm_c_re_2,
        ssm_c_im_2, ssm_d_2, ssm_log_dt_2, ssm_w_glu_2, conv_w_2, conv_w_out_2, q_norm_g_2,
        k_norm_g_2, cmp_pe_2, cmp_w1_2, cmp_w2_2, nsa_w_o_2, w_out_2, ffn_norm_g_2,
        ffn_w_gate_up_2, ffn_w_down_2,
    )


_drawn_inputs = setup_inputs


def setup_inputs(seed=0):
    import zlib

    import numpy as np

    out = dict(_drawn_inputs(seed))
    spreads = {}
    factors = {'lru_b_r': 26.412,
     'lru_b_i': 8.0,
     'sgu_ln_g': 3.511,
     'sgu_ln_b': 8.0,
     'mix_norm_g_2': 5.507,
     'ssm_lam_re_2': 200.0,
     'q_norm_g_2': 64.0,
     'k_norm_g_2': 64.0,
     'cmp_pe_2': 49.232,
     'ffn_norm_g_2': 45.578,
     'ssm_lam_im_2': 64.0,
     'ssm_b_re_2': 64.0,
     'ssm_b_im_2': 64.0,
     'ssm_c_re_2': 64.0,
     'ssm_c_im_2': 64.0,
     'ssm_d_2': 4.507,
     'ssm_log_dt_2': 64.0,
     'ssm_w_glu_2': 3.823,
     'cmp_w1_2': 4.454,
     'cmp_w2_2': 4.01}
    for name, (base, spread) in spreads.items():
        noise = np.random.default_rng([zlib.crc32(name.encode()), seed]).standard_normal(out[name].shape)
        drawn = base * np.exp(spread * noise) if base else spread * noise
        out[name] = jnp.asarray(drawn.astype(out[name].dtype))
    for name, factor in factors.items():
        out[name] = (out[name] * factor).astype(out[name].dtype)
    return out
```

```python
import concourse.bass as bass
from concourse import mybir
from concourse.alu_op_type import AluOpType as ALU
from contextlib import ExitStack

F32 = mybir.dt.float32
F32R = mybir.dt.float32r
ACT = mybir.ActivationFunctionType
AX = mybir.AxisListType

P = 128
S = 256
T = S // P
D = 1024
KD = D // P
FF = 2816
FT = FF // P
CH = 1024
RING = 6
EPS = 1e-6
NEG = -1e30
LAYERS = 2

AW, BW, CW = 384, 384, 256
AB = AW // P
XB = 7
HEADS = 6
HD = 64
VSTEPS = 63

FFN_CHUNKS = 3 * FT
MIX_CHUNKS = 30
LAYER_CHUNKS = 2 * FFN_CHUNKS + MIX_CHUNKS
MIX2_CHUNKS = 89
MIX2_BASE = LAYERS * LAYER_CHUNKS
FFN3_BASE = MIX2_BASE + MIX2_CHUNKS
TOTAL = FFN3_BASE + FFN_CHUNKS
FFN_BASES = [0, FFN_CHUNKS + MIX_CHUNKS]
MIX_BASE = FFN_CHUNKS + 1

C_REC, C_XBC, C_DT, C_GATE0, C_UV, C_GATE1, C_Z, C_OUT = 0, 3, 10, 11, 12, 16, 18, 21
OUT_ORDER = [6, 7, 0, 1, 2, 3, 4, 5]


D_Q, D_KVC, D_NG, D_U, D_KV, D_U3, D_W1, D_MIX, D_OUT = 0, 4, 8, 9, 12, 16, 17, 41, 81
D_CONV = [25, 26, 27, 29, 30, 31, 32, 34, 35, 36, 37, 39]
D_B = [28, 33, 38, 40]
SPLIT_AFTER = {0: [31], 1: [32], 2: [33], 3: [34, 35], 4: [36], 5: [37], 6: [38], 7: [39, 40], 8: [41], 9: [42],
               10: [43], 11: [44, 45], 15: [46]}
TWO_PI_EXACT = 6.283185307179586
TWO_PI = 6.283185
TWO_PI_PARTS = [6.28125, 2.0 ** -9 * 0.990234375, TWO_PI_EXACT - 6.28125 - 2.0 ** -9 * 0.990234375]
MAGIC = 1.5 * 2.0 ** 23


def columns(*widths):
    at, out = 0, {}
    for name, w in widths:
        out[name] = slice(at, at + w)
        at += w
    return out, at


PM, NPM = columns(("pre_g", KD), ("rec_w", AB * 4), ("rec_b", AB), ("xbc_w", XB * 4), ("xbc_b", XB),
                  ("b_r", AB), ("b_i", AB), ("lam", AB), ("w_r", AB * P), ("w_i", AB * P),
                  ("post_g", D), ("norm_g", BW), ("ln_g", CW), ("ln_b", CW), ("dt_bias", HEADS),
                  ("a_log", HEADS), ("d_skip", HEADS), ("b_s", 4), ("w_s", 4 * P))
PF, NPF = columns(("pre_g", KD), ("post_g", D))


PN, NPN = columns(("mix_g", KD), ("cw", 12), ("ssm_d", 4), ("lre", 16), ("lim", 16), ("ldt", 16), ("c", 1024), ("q_g", HD),
                  ("k_g", 3 * HD), ("pe", 32), ("w2", 4 * HD))


class Signal:

    def __init__(self, sem, per):
        self.sem, self.per, self.k = sem, per, 0

    def begin(self, round_):
        self.base, self.k = round_ * self.per, 0

    def inc(self, ins):
        ins.then_inc(self.sem, 1)
        self.k += 1

    def wait(self, eng, k):
        eng.wait_ge(self.sem, self.base + k)

    def end(self, name=""):
        assert self.k == self.per, (name, self.k, self.per)


class Place:

    def __init__(self, rounds, base):
        self.rounds, self.base = rounds, base

    def slot(self, c):
        return (self.base + c) % RING

    def count(self, c):
        return self.rounds * RING + (self.base + c + 1)

    def loaded(self, c):
        return (self.rounds + ((self.base + c) // RING + 1)) * 16

    def later(self, rounds):
        return Place(self.rounds + rounds, self.base)


BANKED = ([f"rec{b}" for b in range(AB)] + [f"xbc{b}" for b in range(XB)] + ["dt", "gate0", "uv0", "uv1", "gate1", "gate2"]
          + [f"lru{b}" for b in range(AB)] + ["z0", "z1", "xtok0", "xtok1", "cs", "sgu0", "sgu1", "yct0", "yct1"]
          + [f"csb{h}" for h in range(HEADS)] + ["ybt0", "ybt1", "ybt2"])
JOBS = ["uv0"] + [f"lru{b}" for b in range(AB)] + ["z0", "xtok0", "xtok1", "cs", "cbt", "sgu0", "sgu1", "yct0", "yct1", "csb0"]
for _h in range(HEADS):
    JOBS += ([f"csb{_h + 1}"] if _h + 1 < HEADS else []) + [f"y{_h}"]
JOBS += ["ybt0", "ybt1", "ybt2"]
JOB = {name: k + 1 for k, name in enumerate(JOBS)}
BANK = {name: k % 4 for k, name in enumerate(BANKED)}
BY_ACT = BANKED[:BANKED.index("xtok0")]
BY_DVE = ["xtok0", "xtok1", "cs", "sgu0", "sgu1"] + [f"csb{h}" for h in range(HEADS)]
Y_ORDER = ["yct0", "yct1", "ya", "ybt0", "ybt1", "ybt2"]


ROUNDS = 16
BANKED2 = (["q0", "q1"] + [f"kvc{i}" for i in range(4)] + ["ng", "u0", "u1", "u2", "kv0", "kv1", "u3", "hid0", "hid1", "hidt0", "hidt1",
           "cmp0", "cmp1", "qt00", "qt01", "qt10", "qt11", "kt0", "kt1", "kct"])
BY_ACT2, BY_DVE2 = list(BANKED2), ["cs0", "cs1"]
JOBS2 = ["q0", "kv0"] + BANKED2[BANKED2.index("hidt0"):] + ["cs0", "cs1"]
BANKED2 += ["cs0", "cs1"]
for _r in range(ROUNDS + 1):
    _turn = [f"pt{_r - 1}"] if _r else []
    _new = [f"sc{_r}", f"bu{_r}"] if _r < ROUNDS else []
    _conv = [f"cv{_r}"] if _r < 12 else []
    BANKED2 += _turn + _new + _conv
    BY_ACT2 += _turn + (_conv if _r % 3 != 1 else [])
    BY_DVE2 += _new + (_conv if _r % 3 == 1 else [])
    JOBS2 += _turn + (_new if _r % 4 != 3 else _new[:1]) + ([f"y5{_r - 1}", f"pv{_r - 1}"] if _r else [])
_ots = [f"ot{b}" for b in range(4)]
BANKED2 += _ots
BY_DVE2 += _ots
JOBS2 += _ots
for _i in range(KD):
    BANKED2 += [f"g{_i}0", f"g{_i}1", f"g{_i}2", f"lin{_i}", f"br{_i}"]
    BY_ACT2 += [f"g{_i}0", f"g{_i}1", f"g{_i}2"]
    BY_DVE2 += [f"lin{_i}", f"br{_i}"]
JOB2 = {name: k + 1 for k, name in enumerate(JOBS2)}
BANK2 = {name: k % 4 for k, name in enumerate(BANKED2)}


def block_program(nc, stream, x_in, pf_a, pf_b, pm, pm2, out):
    ctx = ExitStack()
    with ctx:
        def sb(name, shape, dt=F32):
            return ctx.enter_context(nc.sbuf_tensor(name, shape, dt))

        def sem(name):
            return ctx.enter_context(nc.semaphore(name))

        raw = sb("raw", [P, RING * CH])
        whi = sb("whi", [P, RING * CH], F32R)
        wlo = sb("wlo", [P, RING * CH], F32R)
        x = sb("x", [P, T, D])
        xn = sb("xn", [P, T, D])
        xg = sb("xg", [P, 2, 4, P])
        xhi = sb("xhi", [P, KD, S], F32R)
        xlo = sb("xlo", [P, KD, S], F32R)
        yhi, ylo = xhi, xlo
        sg = sb("sg", [P, 2, S])
        h32 = sb("h32", [P, 2, S])
        hhi = sb("hhi", [P, 2, S], F32R)
        hlo = sb("hlo", [P, 2, S], F32R)
        pfa = sb("pfa", [P, NPF])
        pfb = sb("pfb", [P, NPF])
        par = sb("par", [P, NPM])
        ident = sb("ident", [P, P])
        upper = sb("upper", [P, S])
        maskadd = sb("maskadd", [P, S])
        ss = sb("ss", [P, 4 * T])
        ms = sb("ms", [P, 4 * T])
        rstd = sb("rstd", [P, 4 * T])
        small = sb("small", [P, 3])

        scope = ExitStack()

        def m1(name, shape, dt=F32):
            return scope.enter_context(nc.sbuf_tensor(name, shape, dt))

        recpad = m1("recpad", [P, AB, S + 3])
        xbcpad = m1("xbcpad", [P, XB, S + 3])
        recc = m1("recc", [P, AB, S])
        xbcc = m1("xbcc", [P, XB, S])
        gateT = m1("gateT", [P, AB, S])
        rg = m1("rg", [P, AB, S])
        ig = m1("ig", [P, AB, S])
        aa = m1("aa", [P, AB, S])
        th = m1("th", [P, AB, S])
        uv = m1("uv", [P, T, 2 * CW])
        zs = m1("zs", [P, T, BW])
        xtok = m1("xtok", [P, T, BW])
        spin = m1("spin", [P, T * HEADS + AB])
        spe = m1("spe", [P, T * HEADS + AB])
        sp_ = m1("sp_", [P, T * HEADS + AB])
        dtraw = m1("dtraw", [P, T, HEADS])
        ea = m1("ea", [P, HEADS])
        ad = m1("ad", [P, T, HEADS])
        ncs = m1("ncs", [P, T, HEADS])
        psp = m1("psp", [P, 2, AB])
        dm = m1("dm", [P, 2, 384])
        mm = m1("mm", [P, 2, 384])
        yb = m1("yb", [P, T, BW])
        yc = m1("yc", [P, T, CW])
        vx = m1("vx", [P, T, CW])
        lnm = m1("lnm", [P, 2, T])


        scope.close()
        y5hi, y5lo = sb("y5hi", [P, 4, S], F32R), sb("y5lo", [P, 4, S], F32R)
        cvhi, cvlo = sb("cvhi", [P, 4, S], F32R), sb("cvlo", [P, 4, S], F32R)
        scope = ExitStack()
        qT = m1("qT", [HD, 8, S])
        kT = m1("kT", [HD, 4, S])
        xchi, xclo = m1("xchi", [P, 2, 16, 16], F32R), m1("xclo", [P, 2, 16, 16], F32R)
        hidT = m1("hidT", [P, 2, 2, 16])
        kcn, vcs = m1("kcn", [16, HD]), m1("vcs", [16, HD])
        kcT = m1("kcT", [HD, 16])
        zpad = m1("zpad", [P, S + 2])
        cc, cb, cvt = m1("cc", [P, S]), m1("cb", [P, S]), m1("cvt", [P, S])
        sm = m1("sm", [P, 2, 2, S])
        pT = m1("pT", [P, 2, 512])
        pcT = m1("pcT", [16, 2, P])
        pc = m1("pc", [P, T, 8, 16])
        ce = m1("ce", [P, T, 8, 8])
        cst = m1("cst", [P, 8])
        table = m1("table", [P, 2, 3, S])
        frac = m1("frac", [P, 2, S])
        v2, g2 = m1("v2", [P, 2, S]), m1("g2", [P, 2, S])
        q1, q2 = m1("q1", [P, 2, S]), m1("q2", [P, 2, S])
        y5t = m1("y5t", [P, S])
        tokens_f = m1("tokens_f", [P, S])
        qmask = m1("qmask", [P, S])
        cmask = m1("cmask", [P, T, 2, 8])
        ngate = m1("ngate", [P, T * 24])
        s5p = m1("s5p", [P, 8, 16])
        qk_ms, qk_rstd = m1("qk_ms", [P, 24]), m1("qk_rstd", [P, 24])
        kc_st = m1("kc_st", [P, 2])
        halves = m1("halves", [P, 24])
        magic = m1("magic", [P, 2])
        nm, rs = m1("nm", [P, 2, 2]), m1("rs", [P, 2, 2])
        uT = xg[:, :, :, :].rearrange("p a b n -> p (a b n)").rearrange("p (k n) -> p k n", k=4)
        xc = v2[:, :, :].rearrange("p w (j n) -> p w j n", j=16)
        hid = g2
        otok = sm[:, :, :, :].rearrange("p t b n -> p t (b n)")
        scope.close()
        ohi, olo = sb("ohi", [P, 4, S], F32R), sb("olo", [P, 4, S], F32R)
        mxhi, mxlo = sb("mxhi", [P, KD, S], F32R), sb("mxlo", [P, KD, S], F32R)
        gsg, sgl = sb("gsg", [P, 2, 3, S]), sb("sgl", [P, 2, S])
        mt = sb("mt", [P, 3, S])

        acc = ctx.enter_context(nc.psum_tensor("acc", [P, T, D], F32))
        W = [ctx.enter_context(nc.psum_tensor(f"work{i}", [P, 512], F32)) for i in range(4)]

        arrived = [sem(f"arrived{i}") for i in range(RING)]
        hi_ready = sem("hi_ready")
        lo_ready = sem("lo_ready")
        consumed = sem("consumed")
        credits = sem("credits")
        consts = sem("consts")
        x_loaded = sem("x_loaded")
        pfa_loaded, pfb_loaded, par_loaded = sem("pfa_loaded"), sem("pfb_loaded"), sem("par_loaded")
        x_ready = sem("x_ready")
        ss_ready = sem("ss_ready")
        ms_ready = sem("ms_ready")
        rstd_ready = sem("rstd_ready")
        xn_ready = sem("xn_ready")
        xt_ready = sem("xt_ready")
        xg_ready = sem("xg_ready")
        xhi_ready = sem("xhi_ready")
        xlo_ready = sem("xlo_ready")
        acc_ready = sem("acc_ready")
        pss_ready = sem("pss_ready")
        pms_ready = sem("pms_ready")
        prstd_ready = sem("prstd_ready")
        upd_ready = sem("upd_ready")
        sg_ready = sem("sg_ready")
        h32_ready = sem("h32_ready")
        hhi_ready = sem("hhi_ready")
        hlo_ready = sem("hlo_ready")
        out_stored = sem("out_stored")
        pads = sem("pads")

        mixsigs = {}

        def mixsig(name, per):
            mixsigs[name] = Signal(sem("m_" + name), per)
            return mixsigs[name]

        job = mixsig("job", len(JOBS))
        evac = mixsig("evac", len(BY_ACT))
        vec = mixsig("vec", len(BY_DVE))
        y_hi = mixsig("y_hi", len(Y_ORDER))
        y_lo = mixsig("y_lo", len(Y_ORDER))
        rec_conv = mixsig("rec_conv", AB)
        xbc_conv = mixsig("xbc_conv", XB)
        xbc_act = mixsig("xbc_act", XB)
        spin_ready = mixsig("spin", 1)
        soft = mixsig("soft", 3)
        ea_ready = mixsig("ea", 1)
        psp_ready = mixsig("psp", 1)
        ad_ready = mixsig("ad", 1)
        a_ready = mixsig("a", AB)
        th_ready = mixsig("th", AB)
        mult2 = mixsig("mult2", 1)
        mult_ready = mixsig("mult", 1)
        ya32 = mixsig("ya32", 1)
        dexp = mixsig("dexp", HEADS)
        m_ready = mixsig("m", HEADS)
        ysum = mixsig("ysum", T)
        yss = mixsig("yss", T)
        yms = mixsig("yms", T)
        yrstd = mixsig("yrstd", T)
        ybn = mixsig("ybn", T)
        vcen = mixsig("vcen", T)
        vss = mixsig("vss", T)
        vms = mixsig("vms", T)
        vrstd = mixsig("vrstd", T)
        vln = mixsig("vln", T)
        yc_ready = mixsig("yc", T)
        wst = mixsig("wst", 1)
        vstep = mixsig("vstep", VSTEPS)

        def one(name):
            s = Signal(sem("n_" + name), 0)
            s.begin(0)
            return s

        job2, evac2, vec2 = one("job"), one("evac"), one("vec")
        (s5a, s5v, s5m, nrm, ucopy, uhl_ready, xc32, xcs, xc_ready, qn_ready, kcn_ready, wc_ready, csm, cexp, pc_ready, tab_k, tab,
         frac_ready, smax, sexp, pscaled, rot_ready, y5sum, y5g, y5_hi, y5_split, cz, cv32, cv_hi, cv_split, otok_ready, o_hi, sgl_ready,
         mix32, mix_hi, mix_lo, vstep2) = [one(n) for n in (
             "s5a s5v s5m nrm ucopy uhl xc32 xcs xc qn kcn wc csm cexp pc tabk tab frac smax sexp pscaled rot y5sum y5g y5hi y5split "
             "cz cv32 cvhi cvsplit otok ohi sgl mix32 mixhi mixlo vstep2").split()]
        consts2 = sem("consts2")

        block = ctx.enter_context(nc.Block())

        def chunk(tensor, place, c, n=1):
            at = place.slot(c)
            assert at + n <= RING
            return tensor[:, at * CH:(at + n) * CH]

        def split_hi(act, place, cs):
            for c in cs:
                act.wait_ge(arrived[place.slot(c)], place.loaded(c))
                act.wait_ge(consumed, place.count(c))
                nc.scalar.activation(chunk(whi, place, c), chunk(raw, place, c), ACT.Copy).then_inc(hi_ready, 1)

        def split_lo(dve, place, cs):
            for c in cs:
                dve.wait_ge(hi_ready, place.count(c))
                nc.vector.tensor_tensor(chunk(wlo, place, c), chunk(raw, place, c), chunk(whi, place, c).bitcast(F32),
                                        ALU.subtract).then_inc(lo_ready, 1)

        def product(o, lhi, llo, rhi, rlo, start, stop):
            return [nc.tensor.matmul(o, lhi, rhi, start=start, stop=False),
                    nc.tensor.matmul(o, lhi, rlo, start=False, stop=False),
                    nc.tensor.matmul(o, llo, rhi, start=False, stop=stop)]

        def bc(ap, n):
            return ap.unsqueeze(2).broadcast_to([P, ap.shape[1], n])

        def prenorm_act(act, q):
            for t in range(T):
                act.wait_ge(x_ready, q * T + (t + 1))
                nc.scalar.activation(xn[:, t, :], x[:, t, :], ACT.Square, scale=D ** -0.5, accum_out=ss[:, t:t + 1]).then_inc(ss_ready, 1)
            for i in range(2 * T):
                t, b = i // 2, i % 2
                act.wait_ge(xg_ready, q * 2 * T + (i + 1))
                nc.scalar.activation(xhi[:, 4 * b:4 * b + 4, t * P:(t + 1) * P], xg[:, i % 2], ACT.Copy).then_inc(xhi_ready, 1)

        def rsqrt_pool(pool, given, g, between, b, done, d, at, eps):
            pool.wait_ge(given, g)
            nc.gpsimd.tensor_tensor(ms[:, at:at + 1], ss[:, at:at + 1], small[:, eps:eps + 1], ALU.add).then_inc(between, 1)
            pool.wait_ge(between, b)
            nc.gpsimd.tensor_tensor(rstd[:, at:at + 1], ms[:, at:at + 1], small[:, 0:1], ALU.pow).then_inc(done, 1)

        def prenorm_pool(pool, q):
            for t in range(T):
                n = q * T + (t + 1)
                rsqrt_pool(pool, ss_ready, n, ms_ready, n, rstd_ready, n, t, 1)

        def prenorm_dve(dve, q, g):
            for t in range(T):
                dve.wait_ge(rstd_ready, q * T + (t + 1))
                nc.vector.tensor_scalar(xn[:, t, :], x[:, t, :], rstd[:, t:t + 1], None, ALU.mult).then_inc(xn_ready, 1)
            for i in range(2 * T):
                t, b = i // 2, i % 2
                cols = slice(4 * b, 4 * b + 4)
                dve.wait_ge(xt_ready, q * 2 * T + (i + 1))
                if i >= 2:
                    dve.wait_ge(xlo_ready, q * 2 * T + (i - 1))
                nc.vector.tensor_tensor(xg[:, i % 2], W[2 + b][:, :].rearrange("p (a n) -> p a n", n=P), bc(g[:, cols], P),
                                        ALU.mult).then_inc(xg_ready, 1)
                dve.wait_ge(xhi_ready, q * 2 * T + (i + 1))
                nc.vector.tensor_tensor(xlo[:, cols, t * P:(t + 1) * P], xg[:, i % 2],
                                        xhi[:, cols, t * P:(t + 1) * P].bitcast(F32), ALU.subtract).then_inc(xlo_ready, 1)

        def prenorm_pe(pe, q, padding=False):
            for i in range(2 * T):
                t, b = i // 2, i % 2
                pe.wait_ge(xn_ready, q * T + (t + 1))
                if i >= 2:
                    pe.wait_ge(xg_ready, q * 2 * T + (i - 1))
                for a in range(4):
                    k = 4 * b + a
                    m = nc.tensor.transpose(W[2 + b][:, a * P:(a + 1) * P], xn[:, t, k * P:(k + 1) * P], ident[:, :])
                    if padding and i == 0 and a == 0:
                        m.then_inc(consumed, 1)
                m.then_inc(xt_ready, 1)

        def acc_wait(eng, q, t, end):
            if t == 0:
                eng.wait_ge(acc_ready, q + 1)
            else:
                eng.wait_ge(consumed, end + RING)

        def postnorm_act(act, q, end, c):
            for t in range(T):
                acc_wait(act, q, t, end)
                nc.scalar.activation(xn[:, t, :], acc[:, t, :], ACT.Square, scale=D ** -0.5 / c, accum_out=ss[:, t:t + 1]).then_inc(pss_ready, 1)

        def postnorm_pool(pool, p, c):
            for t in range(T):
                n = p * T + (t + 1)
                rsqrt_pool(pool, pss_ready, n, pms_ready, n, prstd_ready, n, t, 1 if c == 1 else 2)

        def postnorm_dve(dve, p, g):
            for t in range(T):
                dve.wait_ge(prstd_ready, p * T + (t + 1))
                nc.vector.scalar_tensor_tensor(out=xn[:, t, :], in0=acc[:, t, :], scalar=rstd[:, t:t + 1],
                                               in1=g, op0=ALU.mult, op1=ALU.mult).then_inc(upd_ready, 1)
                dve.wait_ge(upd_ready, p * T + (t + 1))
                nc.vector.tensor_tensor(x[:, t, :], x[:, t, :], xn[:, t, :], ALU.add).then_inc(x_ready, 1)

        def ffn_pe(pe, n, q, place):
            def gate_up(at, c, j, drained=None):
                for i in range(2):
                    pe.wait_ge(lo_ready, at.count(c + i))
                    if i == 0 and drained is not None:
                        pe.wait_ge(h32_ready, drained)
                    hi, lo = chunk(whi, at, c + i), chunk(wlo, at, c + i)
                    for k in range(KD):
                        m = product(W[j][:, i * S:(i + 1) * S], hi[:, k * P:(k + 1) * P], lo[:, k * P:(k + 1) * P],
                                    xhi[:, k, :], xlo[:, k, :], k == 0, k == KD - 1)[-1]
                    m.then_inc(consumed, 1)

            def down(at, c, j, hidden, first=False, last=False):
                pe.wait_ge(lo_ready, at.count(c))
                pe.wait_ge(hlo_ready, hidden)
                hi, lo = chunk(whi, at, c), chunk(wlo, at, c)
                for t in range(T):
                    for h in range(2):
                        cols = slice(h * 512, (h + 1) * 512)
                        m = product(acc[:, t, cols], hhi[:, j, t * P:(t + 1) * P], hlo[:, j, t * P:(t + 1) * P],
                                    hi[:, cols], lo[:, cols], first, last)[-1]
                    if last and t == 0:
                        m.then_inc(acc_ready, 1)
                m.then_inc(consumed, 1)

            pe.wait_ge(xlo_ready, q * 2 * T + 2 * T)
            gate_up(place, 0, 0)
            gate_up(place, 2, 1)
            down(place, 4, 0, n * FT + 1, first=True)
            with pe.Fori(0, (FT - 2) // 2) as i:
                for u in range(2):
                    gate_up(place.later(i), 5 + 3 * u, u, drained=n * FT + i * 2 + (u + 1))
                    down(place.later(i), 7 + 3 * u, 1 - u, n * FT + i * 2 + (u + 2))
            down(place, FFN_CHUNKS - 1, 1, n * FT + FT, last=True)

        def ffn_act(act, n, place, last=False):
            def tile(at, j, c, split):
                act.wait_ge(consumed, at.count(c) + RING)
                nc.scalar.activation(sg[:, j, :], W[j][:, 0:S], ACT.Silu).then_inc(sg_ready, 1)
                split_hi(act, at, split)

            tile(place, 0, 1, range(4, 7))
            tile(place, 1, 3, range(7, 10))
            with act.Fori(1, FT // 2 - last) as i:
                for u in range(2):
                    tile(place.later(i), u, 3 * u, range(4 + 3 * u, 7 + 3 * u))
            if last:
                tile(place, 0, 3 * (FT - 2), range(FFN_CHUNKS - 2, FFN_CHUNKS))
                tile(place, 1, 3 * (FT - 1), [])

        def ffn_dve(dve, n, place, last=False):
            def tile(at, m, j, c, split, free=None):
                dve.wait_ge(consumed, at.count(c) + RING)
                dve.wait_ge(sg_ready, m + 1)
                nc.vector.tensor_tensor(h32[:, j, :], sg[:, j, :], W[j][:, S:2 * S], ALU.mult).then_inc(h32_ready, 1)
                if free is not None:
                    dve.wait_ge(consumed, at.count(free) + RING)
                dve.wait_ge(h32_ready, m + 1)
                nc.vector.tensor_copy(hhi[:, j, :], h32[:, j, :]).then_inc(hhi_ready, 1)
                dve.wait_ge(hhi_ready, m + 1)
                nc.vector.tensor_tensor(hlo[:, j, :], h32[:, j, :], hhi[:, j, :].bitcast(F32), ALU.subtract).then_inc(hlo_ready, 1)
                split_lo(dve, at, split)

            tile(place, n * FT, 0, 1, range(4, 7))
            tile(place, n * FT + 1, 1, 3, range(7, 10))
            with dve.Fori(1, FT // 2 - last) as i:
                for u in range(2):
                    tile(place.later(i), n * FT + i * 2 + u, u, 3 * u, range(4 + 3 * u, 7 + 3 * u), free=3 * u - 2)
            if last:
                tile(place, n * FT + FT - 2, 0, 3 * (FT - 2), range(FFN_CHUNKS - 2, FFN_CHUNKS), free=3 * (FT - 2) - 2)
                tile(place, n * FT + FT - 1, 1, 3 * (FT - 1), [], free=3 * (FT - 1) - 2)

        def bank(name, cols=slice(0, 512)):
            return W[BANK[name]][:, cols]

        def begin(pe, banked, name):
            i = banked.index(name)
            if i < 4:
                return
            before = banked[i - 4]
            if before in BY_ACT:
                evac.wait(pe, BY_ACT.index(before) + 1)
            elif before in BY_DVE:
                vec.wait(pe, BY_DVE.index(before) + 1)
            else:
                y_lo.wait(pe, Y_ORDER.index(before) + 1)

        def mix_pe(pe, q, place):
            def done(name, ins):
                job.inc(ins)
                assert job.k == JOB[name], name

            def channels(name, c):
                begin(pe, BANKED, name)
                pe.wait_ge(lo_ready, place.count(c))
                hi, lo = chunk(whi, place, c), chunk(wlo, place, c)
                for k in range(KD):
                    m = product(bank(name, slice(0, S)), hi[:, k * P:(k + 1) * P], lo[:, k * P:(k + 1) * P],
                                xhi[:, k, :], xlo[:, k, :], k == 0, k == KD - 1)
                m[-1].then_inc(consumed, 1)

            def tokens(name, t, c, n, at=0):
                chunks = -(-KD * n // CH)
                pe.wait_ge(lo_ready, place.count(c + chunks - 1))
                hi, lo = chunk(whi, place, c, chunks), chunk(wlo, place, c, chunks)
                recent = []
                for k in range(KD):
                    recent += product(bank(name, slice(at, at + n)), xhi[:, k, t * P:(t + 1) * P], xlo[:, k, t * P:(t + 1) * P],
                                      hi[:, k * n:(k + 1) * n], lo[:, k * n:(k + 1) * n], k == 0, k == KD - 1)
                return recent[-4:]

            def release(matmuls, n):
                for m in matmuls[-n:]:
                    m.then_inc(consumed, 1)

            pe.wait_ge(xlo_ready, q * 2 * T + 2 * T)
            for b in range(AB):
                channels(f"rec{b}", C_REC + b)
            for b in range(XB):
                channels(f"xbc{b}", C_XBC + b)
            begin(pe, BANKED, "dt")
            tokens("dt", 0, C_DT, HEADS)
            release(tokens("dt", 1, C_DT, HEADS, at=8), 1)
            channels("gate0", C_GATE0)
            begin(pe, BANKED, "uv0")
            done("uv0", tokens("uv0", 0, C_UV, 2 * CW)[-1])
            begin(pe, BANKED, "uv1")
            release(tokens("uv1", 1, C_UV, 2 * CW), 4)
            channels("gate1", C_GATE1)
            channels("gate2", C_GATE1 + 1)
            for b in range(AB):
                begin(pe, BANKED, f"lru{b}")
                rec_conv.wait(pe, b + 1)
                for i, w in enumerate(("w_r", "w_i")):
                    m = nc.tensor.matmul(bank(f"lru{b}", slice(i * S, (i + 1) * S)), par[:, PM[w]][:, b * P:(b + 1) * P],
                                         recc[:, b, :], start=True, stop=True)
                done(f"lru{b}", m)
            begin(pe, BANKED, "z0")
            done("z0", tokens("z0", 0, C_Z, BW)[-1])
            begin(pe, BANKED, "z1")
            release(tokens("z1", 1, C_Z, BW), 3)
            xbc_act.wait(pe, AB)
            for t in range(T):
                begin(pe, BANKED, f"xtok{t}")
                for b in range(AB):
                    m = nc.tensor.transpose(bank(f"xtok{t}", slice(b * P, (b + 1) * P)), xbcc[:, b, t * P:(t + 1) * P], ident[:, :])
                done(f"xtok{t}", m)
            begin(pe, BANKED, "cs")
            ad_ready.wait(pe, 1)
            tri, ones = upper[:, 0:P], upper[:, P:S]
            nc.tensor.matmul(bank("cs", slice(0, HEADS)), tri, ad[:, 0, :], start=True, stop=True)
            nc.tensor.matmul(bank("cs", slice(8, 8 + HEADS)), ones, ad[:, 0, :], start=True, stop=False)
            done("cs", nc.tensor.matmul(bank("cs", slice(8, 8 + HEADS)), tri, ad[:, 1, :], start=False, stop=True))
            xbc_act.wait(pe, XB)
            for g in range(2):
                bT, cT, o = xbcc[:, AB + g, :], xbcc[:, AB + 2 + g, :], acc[:, 1, g * 512:g * 512 + 384]
                nc.tensor.matmul(o[:, 0:S], bT[:, 0:P], cT, start=True, stop=True)
                m = nc.tensor.matmul(o[:, S:384], bT[:, P:S], cT[:, P:S], start=True, stop=True)
            done("cbt", m)
            wst.wait(pe, 1)
            for t in range(T):
                begin(pe, BANKED, f"sgu{t}")
                vln.wait(pe, t + 1)
                for g in range(4):
                    m = nc.tensor.matmul(bank(f"sgu{t}", slice(g * HD, (g + 1) * HD)), par[:, PM["w_s"]][:, g * P:(g + 1) * P],
                                         vx[:, t, g * HD:(g + 1) * HD], start=True, stop=True)
                done(f"sgu{t}", m)
            yc_ready.wait(pe, T)
            for b in range(2):
                begin(pe, BANKED, f"yct{b}")
                for t in range(T):
                    m = nc.tensor.transpose(bank(f"yct{b}", slice(t * P, (t + 1) * P)), yc[:, t, b * P:(b + 1) * P], ident[:, :])
                done(f"yct{b}", m)

            def sums(h):
                begin(pe, BANKED, f"csb{h}")
                o = bank(f"csb{h}", slice(0, S))
                nc.tensor.matmul(o, ad[:, 0, h:h + 1].broadcast_to([P, P]), upper[:, :], start=True, stop=False)
                done(f"csb{h}", nc.tensor.matmul(o[:, P:S], ad[:, 1, h:h + 1].broadcast_to([P, P]), tri, start=False, stop=True))

            sums(0)
            vec.wait(pe, BY_DVE.index("xtok1") + 1)
            for h in range(HEADS):
                if h + 1 < HEADS:
                    sums(h + 1)
                m_ready.wait(pe, h + 1)
                w, cols = mm[:, h % 2], slice(h * HD, (h + 1) * HD)
                o1 = acc[:, 0, 512 + h * HD:512 + (h + 1) * HD]
                nc.tensor.matmul(acc[:, 0, cols], w[:, 0:P], xtok[:, 0, cols], start=True, stop=True)
                nc.tensor.matmul(o1, w[:, P:S], xtok[:, 0, cols], start=True, stop=False)
                done(f"y{h}", nc.tensor.matmul(o1, w[:, S:384], xtok[:, 1, cols], start=False, stop=True))
            ybn.wait(pe, T)
            for b in range(AB):
                begin(pe, BANKED, f"ybt{b}")
                for t in range(T):
                    m = nc.tensor.transpose(bank(f"ybt{b}", slice(t * P, (t + 1) * P)), yb[:, t, b * P:(b + 1) * P], ident[:, :])
                done(f"ybt{b}", m)
            need = [1, 2, 3, 3, 3, 4, 5, 6]
            for i, k in enumerate(OUT_ORDER):
                pe.wait_ge(lo_ready, place.count(C_OUT + i))
                y_lo.wait(pe, need[i])
                hi, lo = chunk(whi, place, C_OUT + i), chunk(wlo, place, C_OUT + i)
                for t in range(T):
                    for h in range(2):
                        cols = slice(h * 512, (h + 1) * 512)
                        m = product(acc[:, t, cols], yhi[:, k, t * P:(t + 1) * P], ylo[:, k, t * P:(t + 1) * P],
                                    hi[:, cols], lo[:, cols], i == 0, i == KD - 1)[-1]
                    if t == 0 and i == KD - 1:
                        m.then_inc(acc_ready, 1)
                m.then_inc(consumed, 1)

        def mix_act(act, place):
            def emptied(name, ins):
                evac.inc(ins)
                assert BY_ACT[evac.k - 1] == name, name

            def projected(c):
                act.wait_ge(consumed, place.count(c) + RING)

            split_hi(act, place, [3, 4, 5])
            for b in range(AB):
                projected(C_REC + b)
                emptied(f"rec{b}", nc.scalar.activation(recpad[:, b, 3:], bank(f"rec{b}", slice(0, S)), ACT.Copy))
                split_hi(act, place, [C_REC + b + 6])
            for b in range(XB):
                projected(C_XBC + b)
                emptied(f"xbc{b}", nc.scalar.activation(xbcpad[:, b, 3:], bank(f"xbc{b}", slice(0, S)), ACT.Copy))
                split_hi(act, place, [C_XBC + b + 6])
            projected(C_DT)
            emptied("dt", nc.scalar.activation(dtraw[:, :, :], bank("dt", slice(0, 16)).rearrange("p (t h) -> p t h", t=T)[:, :, 0:HEADS], ACT.Copy))
            split_hi(act, place, [C_DT + 6])
            act.wait_ge(par_loaded, mixround(1) * 16)
            spin_ready.wait(act, 1)
            soft.inc(nc.scalar.activation(spe[:, :], spin[:, :], ACT.Abs))
            soft.wait(act, 1)
            soft.inc(nc.scalar.activation(sp_[:, :], spe[:, :], ACT.Exp, scale=-1.0))
            soft.wait(act, 2)
            soft.inc(nc.scalar.activation(spe[:, :], sp_[:, :], ACT.Ln, bias=1.0))
            ea_ready.inc(nc.scalar.activation(ea[:, :], par[:, PM["a_log"]], ACT.Exp))
            projected(C_GATE0)
            emptied("gate0", nc.scalar.activation(gateT[:, 0, :], bank("gate0", slice(0, S)), ACT.Gelu_apprx_tanh))
            split_hi(act, place, [C_GATE0 + 6])
            job.wait(act, JOB["uv0"])
            emptied("uv0", nc.scalar.activation(uv[:, 0, :], bank("uv0"), ACT.Gelu_apprx_tanh))
            projected(C_UV + 3)
            emptied("uv1", nc.scalar.activation(uv[:, 1, :], bank("uv1"), ACT.Gelu_apprx_tanh))
            split_hi(act, place, range(C_UV + 6, C_UV + 10))
            for b in range(2):
                projected(C_GATE1 + b)
                emptied(f"gate{b + 1}", nc.scalar.activation(gateT[:, b + 1, :], bank(f"gate{b + 1}", slice(0, S)), ACT.Gelu_apprx_tanh))
                split_hi(act, place, [C_GATE1 + b + 6])
            for b in range(AB):
                job.wait(act, JOB[f"lru{b}"])
                nc.scalar.activation(rg[:, b, :], bank(f"lru{b}", slice(0, S)), ACT.Sigmoid, bias=par[:, PM["b_r"]][:, b:b + 1])
                emptied(f"lru{b}", nc.scalar.activation(ig[:, b, :], bank(f"lru{b}", slice(S, 2 * S)), ACT.Sigmoid, bias=par[:, PM["b_i"]][:, b:b + 1]))
            job.wait(act, JOB["z0"])
            emptied("z0", nc.scalar.activation(zs[:, 0, :], bank("z0", slice(0, BW)), ACT.Silu))
            projected(C_Z + 2)
            emptied("z1", nc.scalar.activation(zs[:, 1, :], bank("z1", slice(0, BW)), ACT.Silu))
            split_hi(act, place, range(C_Z + 6, C_Z + 9))
            for b in range(XB):
                xbc_conv.wait(act, b + 1)
                xbc_act.inc(nc.scalar.activation(xbcc[:, b, :], xbcc[:, b, :], ACT.Silu))
            psp_ready.wait(act, 1)
            evac.wait(act, BY_ACT.index(f"lru{AB - 1}") + 1)
            for b in range(AB):
                a_ready.inc(nc.scalar.activation(aa[:, b, :], rg[:, b, :], ACT.Exp, scale=psp[:, 1, b:b + 1]))
                th_ready.inc(nc.scalar.activation(th[:, b, :], rg[:, b, :], ACT.Tanh, scale=psp[:, 0, b:b + 1]))
            for t in range(T):
                vcen.wait(act, t + 1)
                vss.inc(nc.scalar.activation(yc[:, t, :], vx[:, t, :], ACT.Square, scale=CW ** -0.5, accum_out=ss[:, 2 + t:3 + t]))
            mult2.wait(act, 1)
            mult_ready.inc(nc.scalar.activation(th[:, :, :], th[:, :, :], ACT.Sqrt))
            for i in range(2):
                job.wait(act, JOB[f"yct{i}"])
                y_hi.inc(nc.scalar.activation(yhi[:, 6 + i, :], bank(f"yct{i}", slice(0, S)), ACT.Copy))
            ya32.wait(act, 1)
            y_hi.inc(nc.scalar.activation(yhi[:, 0:AB, :], rg[:, :, :], ACT.Copy))
            for h in range(HEADS):
                vec.wait(act, BY_DVE.index(f"csb{h}") + 1)
                dexp.inc(nc.scalar.activation(dm[:, h % 2, :], dm[:, h % 2, :], ACT.Exp))
            for t in range(T):
                ysum.wait(act, t + 1)
                yss.inc(nc.scalar.activation(dm[:, t, :], yb[:, t, :], ACT.Square, scale=BW ** -0.5, accum_out=ss[:, 4 + t:5 + t]))
            for b in range(AB):
                job.wait(act, JOB[f"ybt{b}"])
                y_hi.inc(nc.scalar.activation(yhi[:, 3 + b, :], bank(f"ybt{b}", slice(0, S)), ACT.Copy))
            split_hi(act, place, range(C_OUT + 6, MIX_CHUNKS - 1 + 4))

        def mix_pool(pool):
            pool.wait_ge(par_loaded, mixround(1) * 16)
            w_s = par[:, PM["w_s"]].rearrange("p (g n) -> p g n", g=4)
            wst.inc(nc.gpsimd.tensor_tensor(w_s, w_s, upper[:, 0:P].unsqueeze(1).broadcast_to([P, 4, P]), ALU.mult))
            for given, between, done, at in ((vss, vms, vrstd, 2), (yss, yms, yrstd, 4)):
                for t in range(T):
                    given.wait(pool, t + 1)
                    between.inc(nc.gpsimd.tensor_tensor(ms[:, at + t:at + t + 1], ss[:, at + t:at + t + 1], small[:, 1:2], ALU.add))
                    between.wait(pool, t + 1)
                    done.inc(nc.gpsimd.tensor_tensor(rstd[:, at + t:at + t + 1], ms[:, at + t:at + t + 1], small[:, 0:1], ALU.pow))

        def mix_dve(dve, place):
            def step(ins):
                vstep.inc(ins)
                vstep.wait(dve, vstep.k)

            def conv(out_, pad, w, b, done):
                step(nc.vector.tensor_scalar(out_, pad[:, 0:S], w[:, 0:1], b, ALU.mult, ALU.add))
                for j in range(1, 4):
                    ins = nc.vector.scalar_tensor_tensor(out=out_, in0=pad[:, j:j + S], scalar=w[:, j:j + 1], in1=out_, op0=ALU.mult, op1=ALU.add)
                    if j < 3:
                        step(ins)
                    else:
                        done.inc(ins)

            def emptied(name, ins):
                vec.inc(ins)
                assert BY_DVE[vec.k - 1] == name, name

            dve.wait_ge(par_loaded, mixround(1) * 16)
            split_lo(dve, place, [3, 4, 5])
            for b in range(AB):
                evac.wait(dve, BY_ACT.index(f"rec{b}") + 1)
                conv(recc[:, b, :], recpad[:, b, :], par[:, PM["rec_w"]][:, 4 * b:4 * b + 4], par[:, PM["rec_b"]][:, b:b + 1], rec_conv)
                split_lo(dve, place, [C_REC + b + 6])
            for b in range(XB):
                evac.wait(dve, BY_ACT.index(f"xbc{b}") + 1)
                conv(xbcc[:, b, :], xbcpad[:, b, :], par[:, PM["xbc_w"]][:, 4 * b:4 * b + 4], par[:, PM["xbc_b"]][:, b:b + 1], xbc_conv)
                split_lo(dve, place, [C_XBC + b + 6])
            evac.wait(dve, BY_ACT.index("dt") + 1)
            nt = T * HEADS
            for t in range(T):
                step(nc.vector.tensor_tensor(spin[:, t * HEADS:(t + 1) * HEADS], dtraw[:, t, :], par[:, PM["dt_bias"]], ALU.add))
            spin_ready.inc(nc.vector.tensor_scalar(spin[:, nt:], par[:, PM["lam"]], -1.0, None, ALU.mult))
            split_lo(dve, place, [C_DT + 6])
            soft.wait(dve, 3)
            spin_ready.wait(dve, 1)
            step(nc.vector.scalar_tensor_tensor(out=sp_[:, :], in0=spin[:, :], scalar=0.0, in1=spe[:, :], op0=ALU.max, op1=ALU.add))
            step(nc.vector.tensor_scalar(psp[:, 0, :], sp_[:, nt:], 8.0, None, ALU.mult))
            psp_ready.inc(nc.vector.tensor_scalar(psp[:, 1, :], sp_[:, nt:], -8.0, None, ALU.mult))
            ea_ready.wait(dve, 1)
            for t in range(T):
                ins = nc.vector.scalar_tensor_tensor(out=ad[:, t, :], in0=sp_[:, t * HEADS:(t + 1) * HEADS], scalar=-1.0, in1=ea[:, :], op0=ALU.mult, op1=ALU.mult)
                if t == 0:
                    step(ins)
                else:
                    ad_ready.inc(ins)
            split_lo(dve, place, [C_GATE0 + 6])
            for t in range(T):
                evac.wait(dve, BY_ACT.index(f"uv{t}") + 1)
                step(nc.vector.tensor_reduce(lnm[:, 0, t:t + 1], uv[:, t, CW:], AX.X, ALU.add))
                step(nc.vector.tensor_scalar(lnm[:, 1, t:t + 1], lnm[:, 0, t:t + 1], -1.0 / CW, None, ALU.mult))
                vcen.inc(nc.vector.tensor_scalar(vx[:, t, :], uv[:, t, CW:], lnm[:, 1, t:t + 1], None, ALU.add))
            split_lo(dve, place, range(C_UV + 6, C_UV + 10))
            split_lo(dve, place, [C_GATE1 + 6, C_GATE1 + 7])
            split_lo(dve, place, range(C_Z + 6, C_Z + 9))
            a_ready.wait(dve, AB)
            th_ready.wait(dve, AB)
            step(nc.vector.tensor_tensor(ig[:, :, :], ig[:, :, :], recc[:, :, :], ALU.mult))
            step(nc.vector.tensor_tensor(rg[:, :, :], aa[:, :, :], aa[:, :, :], ALU.mult))
            mult2.inc(nc.vector.scalar_tensor_tensor(out=th[:, :, :], in0=rg[:, :, :], scalar=1.0, in1=th[:, :, :], op0=ALU.add, op1=ALU.mult))
            for t in range(T):
                vrstd.wait(dve, t + 1)
                step(nc.vector.scalar_tensor_tensor(out=vx[:, t, :], in0=vx[:, t, :], scalar=rstd[:, 2 + t:3 + t], in1=par[:, PM["ln_g"]], op0=ALU.mult, op1=ALU.mult))
                vln.inc(nc.vector.tensor_tensor(vx[:, t, :], vx[:, t, :], par[:, PM["ln_b"]], ALU.add))
            for t in range(T):
                job.wait(dve, JOB[f"xtok{t}"])
                emptied(f"xtok{t}", nc.vector.tensor_copy(xtok[:, t, :], bank(f"xtok{t}", slice(0, BW))))
            job.wait(dve, JOB["cs"])
            emptied("cs", nc.vector.tensor_scalar(ncs[:, :, :], bank("cs", slice(0, 16)).rearrange("p (t h) -> p t h", t=T)[:, :, 0:HEADS], -1.0, None, ALU.mult))
            mult_ready.wait(dve, 1)
            step(nc.vector.tensor_tensor(th[:, :, :], th[:, :, :], ig[:, :, :], ALU.mult))
            for b in range(AB):
                step(nc.vector.tensor_tensor_scan(rg[:, b, :], aa[:, b, :], th[:, b, :], 0.0, ALU.mult, ALU.add))
            ya32.inc(nc.vector.tensor_tensor(rg[:, :, :], rg[:, :, :], gateT[:, :, :], ALU.mult))
            for t in range(T):
                job.wait(dve, JOB[f"sgu{t}"])
                emptied(f"sgu{t}", nc.vector.tensor_tensor(yc[:, t, :].rearrange("p (g n) -> p g n", g=4), bank(f"sgu{t}", slice(0, CW)).rearrange("p (g n) -> p g n", g=4),
                                                           bc(par[:, PM["b_s"]], HD), ALU.add))
                vec.wait(dve, vec.k)
                yc_ready.inc(nc.vector.tensor_tensor(yc[:, t, :], yc[:, t, :], uv[:, t, 0:CW], ALU.mult))
            for i in range(2):
                y_hi.wait(dve, 1 + i)
                y_lo.inc(nc.vector.tensor_tensor(ylo[:, 6 + i, :], bank(f"yct{i}", slice(0, S)), yhi[:, 6 + i, :].bitcast(F32), ALU.subtract))
            y_hi.wait(dve, 3)
            ya32.wait(dve, 1)
            y_lo.inc(nc.vector.tensor_tensor(ylo[:, 0:AB, :], rg[:, :, :], yhi[:, 0:AB, :].bitcast(F32), ALU.subtract))
            for t in range(T):
                step(nc.vector.tensor_tensor(yb[:, t, :].rearrange("p (h n) -> p h n", h=HEADS), xtok[:, t, :].rearrange("p (h n) -> p h n", h=HEADS),
                                             bc(par[:, PM["d_skip"]], HD), ALU.mult))

            def exponent(h):
                job.wait(dve, JOB[f"csb{h}"])
                if h >= 2:
                    m_ready.wait(dve, h - 1)
                o = dm[:, h % 2]
                vec.wait(dve, BY_DVE.index("cs") + 1)
                step(nc.vector.scalar_tensor_tensor(out=o[:, 0:S], in0=bank(f"csb{h}", slice(0, S)), scalar=ncs[:, 0, h:h + 1], in1=maskadd[:, :], op0=ALU.add, op1=ALU.add))
                emptied(f"csb{h}", nc.vector.scalar_tensor_tensor(out=o[:, S:384], in0=bank(f"csb{h}", slice(P, S)), scalar=ncs[:, 1, h:h + 1], in1=maskadd[:, 0:P], op0=ALU.add, op1=ALU.add))

            exponent(0)
            for h in range(HEADS):
                if h + 1 < HEADS:
                    exponent(h + 1)
                dexp.wait(dve, h + 1)
                if h >= 2:
                    job.wait(dve, JOB[f"y{h - 2}"])
                cb = acc[:, 1, (h // 3) * 512:(h // 3) * 512 + 384]
                step(nc.vector.scalar_tensor_tensor(out=mm[:, h % 2, 0:S], in0=dm[:, h % 2, 0:S], scalar=sp_[:, h:h + 1], in1=cb[:, 0:S], op0=ALU.mult, op1=ALU.mult))
                m_ready.inc(nc.vector.scalar_tensor_tensor(out=mm[:, h % 2, S:384], in0=dm[:, h % 2, S:384], scalar=sp_[:, HEADS + h:HEADS + h + 1], in1=cb[:, S:384], op0=ALU.mult, op1=ALU.mult))
            job.wait(dve, JOB[f"y{HEADS - 1}"])
            for t in range(T):
                step(nc.vector.tensor_tensor(yb[:, t, :], yb[:, t, :], acc[:, 0, t * 512:t * 512 + BW], ALU.add))
                ysum.inc(nc.vector.tensor_tensor(yb[:, t, :], yb[:, t, :], zs[:, t, :], ALU.mult))
            for t in range(T):
                yrstd.wait(dve, t + 1)
                ybn.inc(nc.vector.scalar_tensor_tensor(out=yb[:, t, :], in0=yb[:, t, :], scalar=rstd[:, 4 + t:5 + t], in1=par[:, PM["norm_g"]], op0=ALU.mult, op1=ALU.mult))
            for b in range(AB):
                y_hi.wait(dve, 4 + b)
                y_lo.inc(nc.vector.tensor_tensor(ylo[:, 3 + b, :], bank(f"ybt{b}", slice(0, S)), yhi[:, 3 + b, :].bitcast(F32), ALU.subtract))
            split_lo(dve, place, range(C_OUT + 6, MIX_CHUNKS - 1 + 4))

        def bank2(name, cols=slice(0, 512)):
            return W[BANK2[name]][:, cols]

        def begin2(pe, name):
            i = BANKED2.index(name)
            if i >= 4:
                before = BANKED2[i - 4]
                if before in BY_ACT2:
                    evac2.wait(pe, BY_ACT2.index(before) + 1)
                else:
                    vec2.wait(pe, BY_DVE2.index(before) + 1)

        def nkeys(t):
            return (t + 1) * P

        def mix2_pe(pe, q, place):
            def done(name, ins):
                job2.inc(ins)
                assert JOBS2[job2.k - 1] == name, (name, JOBS2[job2.k - 1])

            def channels(name, c, order=None):
                begin2(pe, name)
                pe.wait_ge(lo_ready, place.count(c))
                hi, lo = chunk(whi, place, c), chunk(wlo, place, c)
                for k in range(KD):
                    m = product(bank2(name, slice(0, S)), hi[:, k * P:(k + 1) * P], lo[:, k * P:(k + 1) * P],
                                xhi[:, k, :], xlo[:, k, :], k == 0, k == KD - 1)
                m[-1].then_inc(consumed, 1)

            def tokens(name, t, c, n, at=0):
                chunks = -(-KD * n // CH)
                pe.wait_ge(lo_ready, place.count(c + chunks - 1))
                hi, lo = chunk(whi, place, c, chunks), chunk(wlo, place, c, chunks)
                recent = []
                for k in range(KD):
                    recent += product(bank2(name, slice(at, at + n)), xhi[:, k, t * P:(t + 1) * P], xlo[:, k, t * P:(t + 1) * P],
                                      hi[:, k * n:(k + 1) * n], lo[:, k * n:(k + 1) * n], k == 0, k == KD - 1)
                return recent[-4:]

            def release(matmuls, n):
                for m in matmuls[-n:]:
                    m.then_inc(consumed, 1)

            pe.wait_ge(xlo_ready, q * 2 * T + 2 * T)
            begin2(pe, "q0")
            done("q0", tokens("q0", 0, D_Q, 512)[-1])
            begin2(pe, "q1")
            release(tokens("q1", 1, D_Q, 512), 4)
            for i in range(4):
                channels(f"kvc{i}", D_KVC + i)
            begin2(pe, "ng")
            tokens("ng", 0, D_NG, 24)
            release(tokens("ng", 1, D_NG, 24, at=24), 1)
            for b in range(3):
                channels(f"u{b}", D_U + b)
            begin2(pe, "kv0")
            done("kv0", tokens("kv0", 0, D_KV, 512)[-1])
            begin2(pe, "kv1")
            release(tokens("kv1", 1, D_KV, 512), 4)
            channels("u3", D_U3)
            for w in range(2):
                begin2(pe, f"hid{w}")
                xc_ready.wait(pe, w + 1)
                for j in range(16):
                    c = D_W1 + 4 * w + j // 4
                    pe.wait_ge(lo_ready, place.count(c))
                    at = slice(j % 4 * S, (j % 4 + 1) * S)
                    m = product(bank2(f"hid{w}", slice(0, S))[0:16], xchi[:, w, j, :], xclo[:, w, j, :], chunk(whi, place, c)[:, at], chunk(wlo, place, c)[:, at], j == 0, j == 15)[-1]
                    if j % 4 == 3:
                        m.then_inc(consumed, 1)
            for w in range(2):
                begin2(pe, f"hidt{w}")
                evac2.wait(pe, BY_ACT2.index(f"hid{w}") + 1)
                for b in range(2):
                    m = nc.tensor.transpose(bank2(f"hidt{w}", slice(b * 16, b * 16 + 16)), hid[0:16, w, b * P:(b + 1) * P], ident[0:16, 0:16])
                done(f"hidt{w}", m)
            for w in range(2):
                begin2(pe, f"cmp{w}")
                evac2.wait(pe, BY_ACT2.index(f"hidt{w}") + 1)
                for b in range(2):
                    m = nc.tensor.matmul(bank2(f"cmp{w}", slice(0, HD))[0:16], hidT[:, w, b, :], par[:, PN["w2"]][:, (2 * w + b) * HD:(2 * w + b + 1) * HD],
                                         start=b == 0, stop=b == 1)
                done(f"cmp{w}", m)
            qn_ready.wait(pe, T)
            for t in range(T):
                for b in range(2):
                    name = f"qt{t}{b}"
                    begin2(pe, name)
                    for a in range(4):
                        h = 4 * b + a
                        m = nc.tensor.transpose(bank2(name, slice(a * P, (a + 1) * P))[0:HD], xn[:, t, h * HD:(h + 1) * HD], ident[:, :])
                    done(name, m)
            for t in range(T):
                name = f"kt{t}"
                begin2(pe, name)
                for a in range(4):
                    m = nc.tensor.transpose(bank2(name, slice(a * P, (a + 1) * P))[0:HD], xn[:, t, 512 + a * HD:512 + (a + 1) * HD], ident[:, :])
                done(name, m)
            begin2(pe, "kct")
            kcn_ready.wait(pe, 1)
            done("kct", nc.tensor.transpose(bank2("kct", slice(0, 16))[0:HD], kcn[0:16, :], ident[0:16, 0:16]))
            evac2.wait(pe, BY_ACT2.index("kct") + 1)
            for t in range(T):
                begin2(pe, f"cs{t}")
                for h in range(8):
                    m = nc.tensor.matmul(bank2(f"cs{t}", slice(h * 8, h * 8 + 8)), qT[:, h, t * P:(t + 1) * P], kcT[:, (h // 4) * 8:(h // 4) * 8 + 8], start=True, stop=True)
                done(f"cs{t}", m)
            uhl_ready.wait(pe, 4)
            wc_ready.wait(pe, 1)
            pc_ready.wait(pe, T)

            def scores(r):
                h, t = r // 2, r % 2
                begin2(pe, f"sc{r}")
                for b in range(2):
                    m = nc.tensor.matmul(bank2(f"sc{r}", slice(b * S, b * S + nkeys(t))), qT[:, h, t * P:(t + 1) * P], kT[:, 2 * b + h // 4, 0:nkeys(t)], start=True, stop=True)
                done(f"sc{r}", m)

            def states_in(r):
                c = D_B[r // 4]
                begin2(pe, f"bu{r}")
                pe.wait_ge(lo_ready, place.count(c))
                for i in range(2):
                    at = slice((r % 4 * 2 + i) * P, (r % 4 * 2 + i + 1) * P)
                    m = product(bank2(f"bu{r}", slice(i * S, (i + 1) * S)), chunk(whi, place, c)[:, at], chunk(wlo, place, c)[:, at],
                                y5hi[:, r // 4, :], y5lo[:, r // 4, :], True, True)
                if r % 4 == 3:
                    m[-1].then_inc(consumed, 1)
                else:
                    done(f"bu{r}", m[-1])

            def states_out(r):
                rot_ready.wait(pe, r + 1)
                k, at = r // 4, 32 * (r % 4)
                o = acc[at:at + 32, 1, (k % 2) * S:(k % 2 + 1) * S]
                w = [par[:, PN["c"]][:, (2 * r + i) * 32:(2 * r + i + 1) * 32] for i in range(2)]
                terms = [(w[0], q1[:, 0, :]), (w[1], q1[:, 1, :]), (w[1], q2[:, 0, :]), (w[0], q2[:, 1, :])]
                for i, (lh, rh) in enumerate(terms):
                    m = nc.tensor.matmul(o, lh, rh, start=i == 0, stop=i == 3)
                done(f"y5{r}", m)

            def turn(r):
                t = r % 2
                begin2(pe, f"pt{r}")
                pscaled.wait(pe, r + 1)
                for b in range(2):
                    for k in range(t + 1):
                        nc.tensor.transpose(bank2(f"pt{r}", slice((b * 2 + k) * P, (b * 2 + k + 1) * P)), sm[:, r % 2, b, k * P:(k + 1) * P], ident[:, :])
                done(f"pt{r}", nc.tensor.transpose(acc[0:16, 1, 512 + (r % 4) * P:512 + (r % 4 + 1) * P], pc[:, t, r // 2, :], ident[:, :]))

            def values(r):
                h, t = r // 2, r % 2
                o = acc[:, 0, t * 512 + h * HD:t * 512 + (h + 1) * HD]
                evac2.wait(pe, BY_ACT2.index(f"pt{r}") + 1)
                nc.tensor.matmul(o, pcT[:, r % 2, :], vcs[:, :], start=True, stop=False)
                for b in range(2):
                    for k in range(t + 1):
                        m = nc.tensor.matmul(o, pT[:, r % 2, (b * 2 + k) * P:(b * 2 + k + 1) * P], xn[:, k, 768 + b * P + (h // 4) * HD:768 + b * P + (h // 4 + 1) * HD],
                                             start=False, stop=b == 1 and k == t)
                done(f"pv{r}", m)

            for r in range(17):
                if r >= 1:
                    turn(r - 1)
                if r < 16:
                    scores(r)
                    states_in(r)
                if r < 12:
                    channels(f"cv{r}", D_CONV[r])
                if r >= 1:
                    states_out(r - 1)
                    values(r - 1)
            otok_ready.wait(pe, T)
            for b in range(4):
                begin2(pe, f"ot{b}")
                for t in range(T):
                    m = nc.tensor.transpose(bank2(f"ot{b}", slice(t * P, (t + 1) * P)), otok[:, t, b * P:(b + 1) * P], ident[:, :])
                done(f"ot{b}", m)
            for i in range(KD):
                for b in range(3):
                    channels(f"g{i}{b}", D_MIX + 5 * i + b)
                for name, c, left, right in ((f"lin{i}", D_MIX + 5 * i + 3, (y5hi, y5lo), (y5hi, y5lo)), (f"br{i}", D_MIX + 5 * i + 4, (cvhi, cvlo), (ohi, olo))):
                    begin2(pe, name)
                    pe.wait_ge(lo_ready, place.count(c))
                    if i == 0:
                        y5_split.wait(pe, 4)
                        cv_split.wait(pe, 4)
                        vec2.wait(pe, BY_DVE2.index("ot3") + 1)
                    for half, (rh, rl) in enumerate((left, right)):
                        for k in range(4):
                            at = slice((half * 4 + k) * P, (half * 4 + k + 1) * P)
                            m = product(bank2(name, slice(half * S, (half + 1) * S)), chunk(whi, place, c)[:, at], chunk(wlo, place, c)[:, at],
                                        rh[:, k, :], rl[:, k, :], k == 0, k == 3)[-1]
                    m.then_inc(consumed, 1)
            for k in range(KD):
                c = D_OUT + k
                pe.wait_ge(lo_ready, place.count(c))
                mix_lo.wait(pe, k + 1)
                hi, lo = chunk(whi, place, c), chunk(wlo, place, c)
                for t in range(T):
                    for h in range(2):
                        cols = slice(h * 512, (h + 1) * 512)
                        m = product(acc[:, t, cols], mxhi[:, k, t * P:(t + 1) * P], mxlo[:, k, t * P:(t + 1) * P],
                                    hi[:, cols], lo[:, cols], k == 0, k == KD - 1)[-1]
                    if t == 0 and k == KD - 1:
                        m.then_inc(acc_ready, 1)
                m.then_inc(consumed, 1)

        def mix2_act(act, place):
            def emptied(name, ins):
                evac2.inc(ins)
                assert BY_ACT2[evac2.k - 1] == name, (name, BY_ACT2[evac2.k - 1])

            def projected(c):
                act.wait_ge(consumed, place.count(c) + RING)

            def copy(name, o, i):
                emptied(name, nc.scalar.activation(o, i, ACT.Copy))

            split_hi(act, place, [4, 5])
            act.wait_ge(par_loaded, 3 * 16)
            s5a.inc(nc.scalar.activation(s5p[:, 0, :], par[:, PN["ldt"]], ACT.Exp))
            s5v.wait(act, 2)
            s5a.inc(nc.scalar.activation(s5p[:, 3, :], s5p[:, 1, :], ACT.Exp))
            job2.wait(act, JOB2["q0"])
            copy("q0", xn[:, 0, 0:512], bank2("q0"))
            projected(D_Q + 3)
            copy("q1", xn[:, 1, 0:512], bank2("q1"))
            split_hi(act, place, range(6, 10))
            for i in range(4):
                w, h = i // 2, i % 2
                projected(D_KVC + i)
                for p in range(2):
                    rows = slice(p * HD, (p + 1) * HD)
                    src = bank2(f"kvc{i}", slice(0, S))[rows].rearrange("d (b j p) -> d j b p", b=8, p=2)[:, :, :, p]
                    ins = nc.scalar.activation(xc[rows, w, :, h * 8:h * 8 + 8], src, ACT.Copy)
                emptied(f"kvc{i}", ins)
                split_hi(act, place, [10 + i])
            projected(D_NG)
            emptied("ng", nc.scalar.activation(ngate[:, :], bank2("ng", slice(0, 48)), ACT.Sigmoid))
            split_hi(act, place, [14])
            for b in range(3):
                projected(D_U + b)
                copy(f"u{b}", uT[:, b, :], bank2(f"u{b}", slice(0, S)))
                split_hi(act, place, [15 + b])
            job2.wait(act, JOB2["kv0"])
            copy("kv0", xn[:, 0, 512:], bank2("kv0"))
            projected(D_KV + 3)
            copy("kv1", xn[:, 1, 512:], bank2("kv1"))
            split_hi(act, place, range(18, 22))
            projected(D_U3)
            copy("u3", uT[:, 3, :], bank2("u3", slice(0, S)))
            split_hi(act, place, [22])
            evac2.wait(act, evac2.k)
            for b in range(4):
                ucopy.inc(nc.scalar.activation(y5hi[:, b, :], uT[:, b, :], ACT.Copy))
            for w in range(2):
                xc32.wait(act, w + 1)
                xcs.inc(nc.scalar.activation(xchi[:, w], xc[:, w], ACT.Copy))
            s5v.wait(act, 3)
            s5a.inc(nc.scalar.activation(s5p[:, 4, :], s5p[:, 2, :], ACT.Sin, scale=TWO_PI))
            s5a.inc(nc.scalar.activation(s5p[:, 5, :], s5p[:, 2, :], ACT.Sin, scale=TWO_PI / 2))
            for w in range(2):
                projected(D_W1 + 4 * w + 3)
                emptied(f"hid{w}", nc.scalar.activation(hid[0:16, w, :], bank2(f"hid{w}", slice(0, S))[0:16], ACT.Gelu_apprx_tanh))
                split_hi(act, place, range(23 + 4 * w, 27 + 4 * w))
            for w in range(2):
                job2.wait(act, JOB2[f"hidt{w}"])
                copy(f"hidt{w}", hidT[:, w], bank2(f"hidt{w}", slice(0, 32)).rearrange("p (b n) -> p b n", b=2))
            for w in range(2):
                job2.wait(act, JOB2[f"cmp{w}"])
                copy(f"cmp{w}", kcn[0:16, :] if w == 0 else vcs[0:16, :], bank2(f"cmp{w}", slice(0, HD))[0:16])
            for t in range(T):
                for b in range(2):
                    job2.wait(act, JOB2[f"qt{t}{b}"])
                    copy(f"qt{t}{b}", qT[:, 4 * b:4 * b + 4, t * P:(t + 1) * P], bank2(f"qt{t}{b}")[0:HD].rearrange("p (a n) -> p a n", a=4))
            for t in range(T):
                job2.wait(act, JOB2[f"kt{t}"])
                copy(f"kt{t}", kT[:, :, t * P:(t + 1) * P], bank2(f"kt{t}")[0:HD].rearrange("p (a n) -> p a n", a=4))
            job2.wait(act, JOB2["kct"])
            copy("kct", kcT[:, :], bank2("kct", slice(0, 16))[0:HD])
            for t in range(T):
                csm.wait(act, t + 1)
                cexp.inc(nc.scalar.activation(ce[:, t], ce[:, t], ACT.Exp))

            def tables(g):
                for i in range(2):
                    tab_k.inc(nc.scalar.activation(frac[:, i, :], tokens_f[:, :], ACT.Identity, scale=s5p[:, 2, 2 * g + i:2 * g + i + 1], bias=magic[:, 0:1]))
                tab_k.wait(act, 4 * g + 2)
                for i in range(2):
                    tab_k.inc(nc.scalar.activation(frac[:, i, :], frac[:, i, :], ACT.Identity, bias=magic[:, 1:2]))
                frac_ready.wait(act, g + 1)
                if g:
                    rot_ready.wait(act, 2 * g)
                tab.inc(nc.scalar.activation(table[:, :, 1, :], frac[:, :, :], ACT.Sin, scale=TWO_PI))
                tab.inc(nc.scalar.activation(table[:, :, 2, :], frac[:, :, :], ACT.Sin, scale=-TWO_PI))
                tab.inc(nc.scalar.activation(table[:, :, 0, :], frac[:, :, :], ACT.Sin, scale=TWO_PI / 2))
                tab.wait(act, 4 * g + 3)
                tab.inc(nc.scalar.activation(table[:, :, 0, :], table[:, :, 0, :], ACT.Square))

            for r in range(17):
                if r >= 1:
                    p = r - 1
                    job2.wait(act, JOB2[f"pt{p}"])
                    if p >= 2:
                        job2.wait(act, JOB2[f"pv{p - 2}"])
                    nb = p % 2 + 1
                    src = bank2(f"pt{p}").rearrange("p (b n) -> p b n", b=2)[:, :, 0:nb * P]
                    dst = pT[:, p % 2, :].rearrange("p (b n) -> p b n", b=2)[:, :, 0:nb * P]
                    nc.scalar.activation(pcT[:, p % 2, :], acc[0:16, 1, 512 + (p % 4) * P:512 + (p % 4 + 1) * P], ACT.Copy)
                    copy(f"pt{p}", dst, src)
                if r < 16:
                    if r % 2 == 0:
                        tables(r // 2)
                    smax.wait(act, r + 1)
                    for b in range(2):
                        sexp.inc(nc.scalar.activation(sm[:, r % 2, b, 0:nkeys(r % 2)], sm[:, r % 2, b, 0:nkeys(r % 2)], ACT.Exp,
                                                      bias=nm[:, r % 2, b:b + 1], accum_out=rs[:, r % 2, b:b + 1]))
                if r < 12:
                    projected(D_CONV[r])
                    if r % 3 == 0:
                        if r:
                            cz.wait(act, r // 3)
                        copy(f"cv{r}", cc[:, :], bank2(f"cv{r}", slice(0, S)))
                    elif r % 3 == 2:
                        if r > 2:
                            cv32.wait(act, r // 3)
                        copy(f"cv{r}", cb[:, :], bank2(f"cv{r}", slice(0, S)))
                if r in SPLIT_AFTER:
                    split_hi(act, place, SPLIT_AFTER[r])
                if r < 12 and r % 3 == 2:
                    cv32.wait(act, r // 3 + 1)
                    cv_hi.inc(nc.scalar.activation(cvhi[:, r // 3, :], cvt[:, :], ACT.Copy))
                if r >= 4 and r % 4 == 0:
                    y5sum.wait(act, r // 4)
                    y5g.inc(nc.scalar.activation(y5t[:, :], y5t[:, :], ACT.Gelu_apprx_tanh))
                    y5g.wait(act, r // 4)
                    y5_hi.inc(nc.scalar.activation(y5hi[:, r // 4 - 1, :], y5t[:, :], ACT.Copy))
            for b in range(4):
                job2.wait(act, JOB2[f"ot{b}"])
                o_hi.inc(nc.scalar.activation(ohi[:, b, :], bank2(f"ot{b}", slice(0, S)), ACT.Copy))
            def mixed_high(i):
                mix32.wait(act, i + 1)
                mix_hi.inc(nc.scalar.activation(mxhi[:, i, :], mt[:, 0, :], ACT.Copy))

            for i in range(KD):
                for b in range(3):
                    c = D_MIX + 5 * i + b
                    projected(c)
                    if i >= 2 and b == 0:
                        mix_lo.wait(act, i - 1)
                    emptied(f"g{i}{b}", nc.scalar.activation(gsg[:, i % 2, b, :], bank2(f"g{i}{b}", slice(0, S)), ACT.Sigmoid))
                    split_hi(act, place, [c + 6])
                if i:
                    mixed_high(i - 1)
                c = D_MIX + 5 * i + 3
                projected(c)
                sgl_ready.inc(nc.scalar.activation(sgl[:, i % 2, :], bank2(f"lin{i}", slice(S, 2 * S)), ACT.Sigmoid))
                split_hi(act, place, [c + 6])
                projected(c + 1)
                split_hi(act, place, [c + 7])
            mixed_high(KD - 1)
            split_hi(act, place, range(D_OUT + 6, MIX2_CHUNKS + 4))

        def mix2_pool(pool):
            s5m.wait(pool, 1)
            nrm.inc(nc.gpsimd.tensor_tensor(qk_rstd[:, :], qk_ms[:, :], halves[:, 0:24], ALU.pow))
            s5m.wait(pool, 2)
            nrm.inc(nc.gpsimd.tensor_tensor(kc_st[0:16, 1:2], kc_st[0:16, 0:1], halves[0:16, 0:1], ALU.pow))

        def mix2_dve(dve, place):
            def step(ins):
                vstep2.inc(ins)
                vstep2.wait(dve, vstep2.k)

            def emptied(name, ins):
                vec2.inc(ins)
                assert BY_DVE2[vec2.k - 1] == name, (name, BY_DVE2[vec2.k - 1])

            tt, ts, stt = nc.vector.tensor_tensor, nc.vector.tensor_scalar, nc.vector.scalar_tensor_tensor
            sp = lambda i: s5p[:, i, :]
            split_lo(dve, place, [4, 5])
            s5a.wait(dve, 1)
            s5v.inc(tt(sp(6), par[:, PN["lim"]], sp(0), ALU.mult))
            s5v.inc(tt(sp(1), par[:, PN["lre"]], sp(0), ALU.mult))
            s5v.wait(dve, 2)
            step(ts(sp(7), sp(6), 1.0 / TWO_PI_EXACT, MAGIC, ALU.mult, ALU.add))
            step(ts(sp(7), sp(7), MAGIC, None, ALU.subtract))
            for part in TWO_PI_PARTS:
                step(stt(out=sp(6), in0=sp(7), scalar=-part, in1=sp(6), op0=ALU.mult, op1=ALU.add))
            step(ts(sp(2), sp(6), 1.0 / TWO_PI_EXACT, 0.5, ALU.mult, ALU.min))
            s5v.inc(ts(sp(2), sp(2), -0.5, None, ALU.max))
            split_lo(dve, place, range(6, 10))
            sq = otok
            for t in range(T):
                evac2.wait(dve, BY_ACT2.index(f"q{t}") + 1)
                step(tt(sq[:, t, :], xn[:, t, 0:512], xn[:, t, 0:512], ALU.mult))
                step(nc.vector.tensor_reduce(qk_ms[:, t * 12:t * 12 + 8], sq[:, t, :].rearrange("p (h n) -> p h n", h=8), AX.X, ALU.add))
            split_lo(dve, place, range(10, 14))
            split_lo(dve, place, [14])
            split_lo(dve, place, range(15, 18))
            for w in range(2):
                evac2.wait(dve, BY_ACT2.index(f"kvc{2 * w + 1}") + 1)
                xc32.inc(tt(xc[:, w], xc[:, w], bc(par[:, PN["pe"]][:, w * 16:(w + 1) * 16], 16), ALU.add))
            for t in range(T):
                evac2.wait(dve, BY_ACT2.index(f"kv{t}") + 1)
                step(tt(sq[:, t, 0:S], xn[:, t, 512:768], xn[:, t, 512:768], ALU.mult))
                step(nc.vector.tensor_reduce(qk_ms[:, t * 12 + 8:t * 12 + 12], sq[:, t, 0:S].rearrange("p (h n) -> p h n", h=4), AX.X, ALU.add))
            s5m.inc(ts(qk_ms[:, :], qk_ms[:, :], 1.0 / HD, EPS, ALU.mult, ALU.add))
            split_lo(dve, place, range(18, 22))
            split_lo(dve, place, [22])
            for b in range(4):
                ucopy.wait(dve, b + 1)
                uhl_ready.inc(tt(y5lo[:, b, :], uT[:, b, :], y5hi[:, b, :].bitcast(F32), ALU.subtract))
            for w in range(2):
                xcs.wait(dve, w + 1)
                xc_ready.inc(tt(xclo[:, w], xc[:, w], xchi[:, w].bitcast(F32), ALU.subtract))
            nrm.wait(dve, 1)
            for t in range(T):
                q3 = xn[:, t, 0:512].rearrange("p (h n) -> p h n", h=8)
                k3 = xn[:, t, 512:768].rearrange("p (h n) -> p h n", h=4)
                step(tt(q3, q3, bc(qk_rstd[:, t * 12:t * 12 + 8], HD), ALU.mult))
                step(stt(out=q3, in0=q3, scalar=HD ** -0.5, in1=par[:, PN["q_g"]].unsqueeze(1).broadcast_to([P, 8, HD]), op0=ALU.mult, op1=ALU.mult))
                step(tt(k3, k3, bc(qk_rstd[:, t * 12 + 8:t * 12 + 12], HD), ALU.mult))
                for b in range(2):
                    kb = k3[:, 2 * b:2 * b + 2, :]
                    ins = tt(kb, kb, par[:, PN["k_g"]][:, (b + 1) * HD:(b + 2) * HD].unsqueeze(1).broadcast_to([P, 2, HD]), ALU.mult)
                    if b == 0:
                        step(ins)
                    else:
                        qn_ready.inc(ins)
            s5a.wait(dve, 4)
            step(tt(sp(5), sp(5), sp(5), ALU.mult))
            step(ts(sp(5), sp(5), -2.0, 1.0, ALU.mult, ALU.add))
            step(tt(sp(5), sp(5), sp(3), ALU.mult))
            step(ts(sp(5), sp(5), 1.0, None, ALU.subtract))
            step(tt(sp(4), sp(4), sp(3), ALU.mult))
            step(tt(sp(6), par[:, PN["lre"]], par[:, PN["lre"]], ALU.mult))
            step(tt(sp(7), par[:, PN["lim"]], par[:, PN["lim"]], ALU.mult))
            step(tt(sp(6), sp(6), sp(7), ALU.add))
            step(nc.vector.reciprocal(sp(6), sp(6)))
            step(tt(sp(7), sp(5), par[:, PN["lre"]], ALU.mult))
            step(tt(sp(0), sp(4), par[:, PN["lim"]], ALU.mult))
            step(tt(sp(7), sp(7), sp(0), ALU.add))
            step(tt(sp(7), sp(7), sp(6), ALU.mult))
            step(tt(sp(0), sp(4), par[:, PN["lre"]], ALU.mult))
            step(tt(sp(1), sp(5), par[:, PN["lim"]], ALU.mult))
            step(tt(sp(0), sp(0), sp(1), ALU.subtract))
            step(tt(sp(0), sp(0), sp(6), ALU.mult))
            c4 = par[:, PN["c"]].rearrange("p (r i n) -> p r i n", r=16, i=2)
            cre, cim = c4[:, :, 0, :], c4[:, :, 1, :]
            a3, b3, d3 = [v.rearrange("p (r n) -> p r n", r=16) for v in (sg[:, :, :].rearrange("p a n -> p (a n)"), h32[:, :, :].rearrange("p a n -> p (a n)"), v2[:, :, :].rearrange("p a n -> p (a n)"))]
            step(tt(a3, cre, bc(sp(7), 32), ALU.mult))
            step(tt(b3, cim, bc(sp(0), 32), ALU.mult))
            step(tt(a3, a3, b3, ALU.subtract))
            step(tt(b3, cre, bc(sp(0), 32), ALU.mult))
            step(tt(d3, cim, bc(sp(7), 32), ALU.mult))
            step(stt(out=cim, in0=b3, scalar=-1.0, in1=d3, op0=ALU.mult, op1=ALU.subtract))
            wc_ready.inc(nc.vector.tensor_copy(cre, a3))
            split_lo(dve, place, range(23, 27))
            split_lo(dve, place, range(27, 31))
            evac2.wait(dve, BY_ACT2.index("cmp1") + 1)
            step(tt(sq[0:16, 0, 0:HD], kcn[0:16, :], kcn[0:16, :], ALU.mult))
            step(nc.vector.tensor_reduce(kc_st[0:16, 0:1], sq[0:16, 0, 0:HD], AX.X, ALU.add))
            s5m.inc(ts(kc_st[0:16, 0:1], kc_st[0:16, 0:1], 1.0 / HD, EPS, ALU.mult, ALU.add))
            nrm.wait(dve, 2)
            kcn_ready.inc(stt(out=kcn[0:16, :], in0=kcn[0:16, :], scalar=kc_st[0:16, 1:2], in1=par[0:16, PN["k_g"]][:, 0:HD], op0=ALU.mult, op1=ALU.mult))
            for t in range(T):
                job2.wait(dve, JOB2[f"cs{t}"])
                c3 = ce[:, t]
                m3 = cmask[:, t, 0, :].unsqueeze(1).broadcast_to([P, 8, 8])
                o3 = cmask[:, t, 1, :].unsqueeze(1).broadcast_to([P, 8, 8])
                emptied(f"cs{t}", tt(c3, bank2(f"cs{t}", slice(0, 64)).rearrange("p (h n) -> p h n", h=8), m3, ALU.add))
                vec2.wait(dve, vec2.k)
                step(nc.vector.tensor_reduce(cst[:, 0:8], c3, AX.X, ALU.max))
                csm.inc(tt(c3, c3, bc(cst[:, 0:8], 8), ALU.subtract))
                cexp.wait(dve, t + 1)
                step(tt(c3, c3, o3, ALU.mult))
                step(nc.vector.tensor_reduce(cst[:, 0:8], c3, AX.X, ALU.add))
                step(ts(cst[:, 0:8], cst[:, 0:8], 1e-30, None, ALU.max))
                step(nc.vector.reciprocal(cst[:, 0:8], cst[:, 0:8]))
                step(tt(cst[:, 0:8], cst[:, 0:8], ngate[:, t * 24:(t + 1) * 24].rearrange("p (h n) -> p h n", n=3)[:, :, 0], ALU.mult))
                step(tt(pc[:, t, 0:4, 0:8], c3[:, 0:4, :], bc(cst[:, 0:4], 8), ALU.mult))
                pc_ready.inc(tt(pc[:, t, 4:8, 8:16], c3[:, 4:8, :], bc(cst[:, 4:8], 8), ALU.mult))

            def fraction(g):
                for i in range(2):
                    tab_k.wait(dve, 4 * g + 4)
                    step(stt(out=frac[:, i, :], in0=tokens_f[:, :], scalar=s5p[:, 2, 2 * g + i:2 * g + i + 1], in1=frac[:, i, :], op0=ALU.mult, op1=ALU.subtract))
                frac_ready.inc(ts(frac[:, :, :], frac[:, :, :], 0.5, -0.5, ALU.min, ALU.max))

            def s5_sum(k):
                job2.wait(dve, JOB2[f"y5{4 * k + 3}"])
                y5sum.inc(stt(out=y5t[:, :], in0=uT[:, k, :], scalar=par[:, PN["ssm_d"]][:, k:k + 1], in1=acc[:, 1, (k % 2) * S:(k % 2 + 1) * S], op0=ALU.mult, op1=ALU.add))

            def s5_low(k):
                y5_hi.wait(dve, k + 1)
                y5_split.inc(tt(y5lo[:, k, :], y5t[:, :], y5hi[:, k, :].bitcast(F32), ALU.subtract))

            for r in range(16):
                h, t = r // 2, r % 2
                nk = nkeys(t)
                if r % 2 == 0:
                    fraction(r // 2)
                job2.wait(dve, JOB2[f"sc{r}"])
                if r >= 2:
                    job2.wait(dve, JOB2[f"pt{r - 2}"])
                s3 = sm[:, t, :, 0:nk]
                emptied(f"sc{r}", tt(s3, bank2(f"sc{r}").rearrange("p (b n) -> p b n", b=2)[:, :, 0:nk],
                                     qmask[:, S - nk:S].unsqueeze(1).broadcast_to([P, 2, nk]), ALU.add))
                vec2.wait(dve, vec2.k)
                smax.inc(nc.vector.tensor_reduce(nm[:, t, :], s3, AX.X, ALU.max, negate=True))
                if r % 2 == 0:
                    tab.wait(dve, 4 * (r // 2) + 4)
                    step(ts(table[:, :, 0, :], table[:, :, 0, :], -2.0, 1.0, ALU.mult, ALU.add))
                cosr = table[:, t, 0, :].unsqueeze(1).broadcast_to([P, 2, S])
                sins = table[:, t, 1:3, :]
                if r % 4 == 3:
                    dve.wait_ge(consumed, place.count(D_B[r // 4]) + RING)
                else:
                    job2.wait(dve, JOB2[f"bu{r}"])
                b3 = bank2(f"bu{r}").rearrange("p (b n) -> p b n", b=2)
                step(tt(sg[:, :, :], b3, cosr, ALU.mult))
                emptied(f"bu{r}", tt(h32[:, :, :], b3, sins, ALU.mult))
                vec2.wait(dve, vec2.k)
                step(tt(v2[:, 0, :], sg[:, 0, :], h32[:, 1, :], ALU.subtract))
                step(tt(v2[:, 1, :], sg[:, 1, :], h32[:, 0, :], ALU.subtract))
                for i in range(2):
                    step(nc.vector.tensor_tensor_scan(g2[:, i, :], s5p[:, 3, r:r + 1].broadcast_to([P, S]), v2[:, i, :], 0.0, ALU.mult, ALU.add))
                if r >= 1:
                    job2.wait(dve, JOB2[f"y5{r - 1}"])
                if r % 4 == 0 and r:
                    s5_sum(r // 4 - 1)
                step(tt(q1[:, :, :], g2[:, :, :], cosr, ALU.mult))
                rot_ready.inc(tt(q2[:, :, :], g2[:, :, :], sins, ALU.mult))
                sexp.wait(dve, 2 * r + 2)
                step(ts(rs[:, t, :], rs[:, t, :], 1e-30, None, ALU.max))
                step(nc.vector.reciprocal(rs[:, t, :], rs[:, t, :]))
                step(tt(rs[:, t, :], rs[:, t, :], ngate[:, t * 24 + 3 * h + 1:t * 24 + 3 * h + 3], ALU.mult))
                step(ts(sm[:, t, 0, 0:nk], sm[:, t, 0, 0:nk], rs[:, t, 0:1], None, ALU.mult))
                pscaled.inc(ts(sm[:, t, 1, 0:nk], sm[:, t, 1, 0:nk], rs[:, t, 1:2], None, ALU.mult))
                if r < 12:
                    j = r // 3
                    if r % 3 == 1:
                        dve.wait_ge(consumed, place.count(D_CONV[r]) + RING)
                        evac2.wait(dve, BY_ACT2.index(f"cv{r - 1}") + 1)
                        emptied(f"cv{r}", tt(zpad[:, 2:], bank2(f"cv{r}", slice(0, S)), cc[:, :], ALU.mult))
                        vec2.wait(dve, vec2.k)
                        cz.inc(ts(cvt[:, :], zpad[:, 0:S], par[:, PN["cw"]][:, 3 * j:3 * j + 1], None, ALU.mult))
                        cz.wait(dve, j + 1)
                    if r % 3 == 2:
                        for k in range(1, 3):
                            step(stt(out=cvt[:, :], in0=zpad[:, k:k + S], scalar=par[:, PN["cw"]][:, 3 * j + k:3 * j + k + 1], in1=cvt[:, :], op0=ALU.mult, op1=ALU.add))
                        evac2.wait(dve, BY_ACT2.index(f"cv{r}") + 1)
                        cv32.inc(tt(cvt[:, :], cvt[:, :], cb[:, :], ALU.mult))
                if r in SPLIT_AFTER:
                    split_lo(dve, place, SPLIT_AFTER[r])
                if r < 12 and r % 3 == 2:
                    cv_hi.wait(dve, j + 1)
                    cv_split.inc(tt(cvlo[:, j, :], cvt[:, :], cvhi[:, j, :].bitcast(F32), ALU.subtract))
                if r % 4 == 1 and r > 1:
                    s5_low(r // 4 - 1)
            s5_sum(3)
            s5_low(3)
            for t in range(T):
                job2.wait(dve, JOB2["pv15"])
                otok_ready.inc(nc.vector.tensor_copy(otok[:, t, :], acc[:, 0, t * 512:(t + 1) * 512]))
            for b in range(4):
                o_hi.wait(dve, b + 1)
                ins = tt(olo[:, b, :], bank2(f"ot{b}", slice(0, S)), ohi[:, b, :].bitcast(F32), ALU.subtract)
                emptied(f"ot{b}", ins)
            def mixed_low(i):
                mix_hi.wait(dve, i + 1)
                mix_lo.inc(tt(mxlo[:, i, :], mt[:, 0, :], mxhi[:, i, :].bitcast(F32), ALU.subtract))
                mix_lo.wait(dve, i + 1)

            for i in range(KD):
                c = D_MIX + 5 * i
                split_lo(dve, place, [c + 6, c + 7, c + 8])
                if i:
                    mixed_low(i - 1)
                sgl_ready.wait(dve, i + 1)
                evac2.wait(dve, BY_ACT2.index(f"g{i}2") + 1)
                emptied(f"lin{i}", tt(mt[:, 0, :], bank2(f"lin{i}", slice(0, S)), sgl[:, i % 2, :], ALU.mult))
                vec2.wait(dve, vec2.k)
                step(tt(mt[:, 0, :], mt[:, 0, :], gsg[:, i % 2, 0, :], ALU.mult))
                split_lo(dve, place, [c + 9])
                dve.wait_ge(consumed, place.count(c + 4) + RING)
                emptied(f"br{i}", tt(mt[:, 1:3, :], bank2(f"br{i}").rearrange("p (b n) -> p b n", b=2), gsg[:, i % 2, 1:3, :], ALU.mult))
                vec2.wait(dve, vec2.k)
                step(tt(mt[:, 0, :], mt[:, 0, :], mt[:, 1, :], ALU.add))
                mix32.inc(tt(mt[:, 0, :], mt[:, 0, :], mt[:, 2, :], ALU.add))
                split_lo(dve, place, [c + 10])
            mixed_low(KD - 1)
            split_lo(dve, place, range(D_OUT + 6, MIX2_CHUNKS + 4))
            for t in range(T):
                acc_wait(dve, 6, t, place.count(D_OUT + KD - 1))
                tt(x[:, t, :], x[:, t, :], acc[:, t, :], ALU.add).then_inc(x_ready, 1)

        def mixround(n):
            return mixsigs["job"].round + n

        def layer_places(l):
            r = l * (LAYER_CHUNKS // RING)
            return [Place(r, b) for b in (FFN_BASES[0], MIX_BASE, FFN_BASES[1])]

        def begin_mix(signals, l):
            for s in signals:
                s.begin(l)

        @block.sync
        def _(sp):
            sp.dma_start(xn[:, :, :], x_in.rearrange("(t p) d -> p t d", p=P)).then_inc(x_loaded, 16)
            for c in range(RING):
                sp.dma_start(chunk(raw, Place(0, 0), c), stream[c]).then_inc(arrived[c], 16)
            with sp.Fori(1, TOTAL // RING) as i:
                for c in range(RING):
                    sp.wait_ge(lo_ready, i * RING + (c - RING + 1))
                    sp.dma_start(chunk(raw, Place(0, 0), c), stream[i * RING + c]).then_inc(arrived[c], 16)
            for c in range(TOTAL // RING * RING, TOTAL):
                sp.wait_ge(lo_ready, c - RING + 1)
                sp.dma_start(chunk(raw, Place(0, 0), c % RING), stream[c]).then_inc(arrived[c % RING], 16)
            sp.wait_ge(x_ready, T * 9)
            sp.dma_start(out.rearrange("(t p) d -> p t d", p=P), x[:, :, :]).then_inc(out_stored, 16)
            sp.wait_ge(out_stored, 16)

        @block.gpsimd
        def _(pool):
            nc.gpsimd.memset(ident[:, :], 0.0).then_inc(pads, 1)
            nc.gpsimd.memset(upper[:, :], 1.0).then_inc(pads, 1)
            nc.gpsimd.memset(maskadd[:, :], 0.0).then_inc(pads, 1)
            nc.gpsimd.memset(recpad[:, :, 0:3], 0.0).then_inc(pads, 1)
            nc.gpsimd.memset(xbcpad[:, :, 0:3], 0.0).then_inc(pads, 1)
            nc.gpsimd.memset(lnm[:, :, :], 0.0).then_inc(pads, 1)
            pool.wait_ge(pads, 6)
            nc.gpsimd.affine_select(out=ident[:, :], in_=ident[:, :], compare_op=ALU.not_equal, fill=1.0, base=0, pattern=[[-1, P]], channel_multiplier=1).then_inc(consts, 1)
            nc.gpsimd.affine_select(out=upper[:, :], in_=upper[:, :], compare_op=ALU.is_ge, fill=0.0, base=0, pattern=[[1, S]], channel_multiplier=-1).then_inc(consts, 1)
            nc.gpsimd.affine_select(out=maskadd[:, :], in_=maskadd[:, :], compare_op=ALU.is_ge, fill=NEG, base=0, pattern=[[1, S]], channel_multiplier=-1).then_inc(consts, 1)
            nc.gpsimd.memset(small[:, 0:1], -0.5).then_inc(consts, 1)
            nc.gpsimd.memset(small[:, 1:2], EPS).then_inc(consts, 1)
            nc.gpsimd.memset(small[:, 2:3], 4 * EPS).then_inc(consts, 1)
            pool.wait_ge(consts, 6)
            with pool.Fori(0, LAYERS) as l:
                for s in (wst, vms, vrstd, yms, yrstd):
                    s.begin(l)
                begin_mix([vss, yss], l)
                prenorm_pool(pool, l * 3)
                postnorm_pool(pool, l * 3, 0.5)
                prenorm_pool(pool, l * 3 + 1)
                mixsigs["job"].round = l
                mix_pool(pool)
                postnorm_pool(pool, l * 3 + 1, 1)
                prenorm_pool(pool, l * 3 + 2)
                postnorm_pool(pool, l * 3 + 2, 0.5)
            pool.wait_ge(x_ready, T * 7)
            ints = frac[:, 0, :].bitcast(mybir.dt.int32)
            nc.gpsimd.iota(ints, pattern=[[1, S]], base=0, channel_multiplier=0).then_inc(pads, 1)
            nc.gpsimd.memset(qmask[:, :], 0.0).then_inc(pads, 1)
            nc.gpsimd.memset(cmask[:, :, 0, :], 0.0).then_inc(pads, 1)
            nc.gpsimd.memset(cmask[:, :, 1, :], 1.0).then_inc(pads, 1)
            nc.gpsimd.memset(halves[:, :], -0.5).then_inc(pads, 1)
            nc.gpsimd.memset(magic[:, 0:1], MAGIC).then_inc(pads, 1)
            nc.gpsimd.memset(magic[:, 1:2], -MAGIC).then_inc(pads, 1)
            nc.gpsimd.memset(zpad[:, 0:2], 0.0).then_inc(consts2, 1)
            nc.gpsimd.memset(pc[:, :, :, :], 0.0).then_inc(consts2, 1)
            pool.wait_ge(pads, 13)
            nc.gpsimd.tensor_copy(tokens_f[:, :], ints).then_inc(consts2, 1)
            nc.gpsimd.affine_select(out=qmask[:, :], in_=qmask[:, :], compare_op=ALU.is_ge, fill=NEG, base=P, pattern=[[-1, S]], channel_multiplier=1).then_inc(consts2, 1)
            for i, fill in enumerate((NEG, 0.0)):
                nc.gpsimd.affine_select(out=cmask[:, :, i, :], in_=cmask[:, :, i, :], compare_op=ALU.is_ge, fill=fill, base=-31, pattern=[[P, T], [-32, 8]], channel_multiplier=1).then_inc(consts2, 1)
            nc.gpsimd.memset(cst[:, :], 0.0).then_inc(consts2, 1)
            prenorm_pool(pool, 6)
            mix2_pool(pool)
            prenorm_pool(pool, 7)

        @block.scalar
        def _(act):
            act.dma_start(pfa[:, :], pf_a[0]).then_inc(pfa_loaded, 16)
            act.wait_ge(credits, 1)
            split_hi(act, Place(0, 0), range(4))
            with act.Fori(0, LAYERS) as l:
                begin_mix(mixsigs.values(), l)
                mixsigs["job"].round = l
                f1, mx, f2 = layer_places(l)
                prenorm_act(act, l * 3)
                act.dma_start(par[:, :], pm[l]).then_inc(par_loaded, 16)
                act.dma_start(pfb[:, :], pf_b[l]).then_inc(pfb_loaded, 16)
                ffn_act(act, l * 2, f1)
                postnorm_act(act, l * 3, f1.count(FFN_CHUNKS - 1), 0.5)
                prenorm_act(act, l * 3 + 1)
                act.dma_start(pfa[:, :], pf_a[l + 1]).then_inc(pfa_loaded, 16)
                mix_act(act, mx)
                postnorm_act(act, l * 3 + 1, mx.count(C_OUT + KD - 1), 1)
                prenorm_act(act, l * 3 + 2)
                ffn_act(act, l * 2 + 1, f2)
                postnorm_act(act, l * 3 + 2, f2.count(FFN_CHUNKS - 1), 0.5)
            act.dma_start(par[:, 0:NPN], pm2).then_inc(par_loaded, 16)
            prenorm_act(act, 6)
            act.wait_ge(consts2, 7)
            mix2_act(act, Place(0, MIX2_BASE))
            prenorm_act(act, 7)
            ffn_act(act, 4, Place(0, FFN3_BASE), last=True)

        @block.vector
        def _(dve):
            dve.wait_ge(x_loaded, 16)
            for t in range(T):
                nc.vector.tensor_copy(x[:, t, :], xn[:, t, :]).then_inc(x_ready, 1)
            split_lo(dve, Place(0, 0), range(4))
            dve.wait_ge(consts, 6)
            with dve.Fori(0, LAYERS) as l:
                begin_mix(mixsigs.values(), l)
                mixsigs["job"].round = l
                f1, mx, f2 = layer_places(l)
                dve.wait_ge(pfa_loaded, (l + 1) * 16)
                prenorm_dve(dve, l * 3, pfa[:, PF["pre_g"]])
                ffn_dve(dve, l * 2, f1)
                postnorm_dve(dve, l * 3, pfa[:, PF["post_g"]])
                dve.wait_ge(par_loaded, (l + 1) * 16)
                prenorm_dve(dve, l * 3 + 1, par[:, PM["pre_g"]])
                mix_dve(dve, mx)
                postnorm_dve(dve, l * 3 + 1, par[:, PM["post_g"]])
                dve.wait_ge(pfb_loaded, (l + 1) * 16)
                prenorm_dve(dve, l * 3 + 2, pfb[:, PF["pre_g"]])
                ffn_dve(dve, l * 2 + 1, f2)
                postnorm_dve(dve, l * 3 + 2, pfb[:, PF["post_g"]])
            dve.wait_ge(par_loaded, (LAYERS + 1) * 16)
            dve.wait_ge(consts2, 7)
            prenorm_dve(dve, 6, par[:, PN["mix_g"]])
            mix2_dve(dve, Place(0, MIX2_BASE))
            dve.wait_ge(pfa_loaded, 3 * 16)
            prenorm_dve(dve, 7, pfa[:, PF["pre_g"]])
            ffn_dve(dve, 4, Place(0, FFN3_BASE), last=True)
            for t in range(T):
                acc_wait(dve, 7, t, TOTAL)
                nc.vector.tensor_tensor(x[:, t, :], x[:, t, :], acc[:, t, :], ALU.add).then_inc(x_ready, 1)

        @block.tensor
        def _(pe):
            pe.sem_inc(consumed, RING)
            pe.sem_inc(credits, 1)
            pe.wait_ge(consts, 6)
            with pe.Fori(0, LAYERS) as l:
                begin_mix(mixsigs.values(), l)
                f1, mx, f2 = layer_places(l)
                prenorm_pe(pe, l * 3)
                ffn_pe(pe, l * 2, l * 3, f1)
                prenorm_pe(pe, l * 3 + 1, padding=True)
                mix_pe(pe, l * 3 + 1, mx)
                prenorm_pe(pe, l * 3 + 2)
                ffn_pe(pe, l * 2 + 1, l * 3 + 2, f2)
            prenorm_pe(pe, 6)
            mix2_pe(pe, 6, Place(0, MIX2_BASE))
            prenorm_pe(pe, 7)
            ffn_pe(pe, 4, 7, Place(0, FFN3_BASE))




def channel_chunks(w):
    k, n = w.shape
    return w.reshape(k // P, P, n // P, P).transpose(2, 1, 0, 3).reshape(n // P, P, -1)


def region(w):
    import numpy as np
    k, n = w.shape
    flat = w.reshape(k // P, P, n).transpose(1, 0, 2).reshape(P, -1)
    chunks = -(-flat.shape[1] // CH)
    flat = np.concatenate([flat, np.zeros((P, chunks * CH - flat.shape[1]), w.dtype)], axis=1)
    return flat.reshape(P, chunks, CH).transpose(1, 0, 2)


def ffn_chunks(w_gu, w_down):
    gate, up, down = channel_chunks(w_gu[:, :FF]), channel_chunks(w_gu[:, FF:]), w_down.reshape(FT, P, D)
    order = [gate[0], up[0]]
    for j in range(1, FT):
        order += [gate[j], up[j], down[j - 1]]
    return order + [down[FT - 1]]


def mix_chunks(w_in, w_out):
    import numpy as np
    cut = np.cumsum([AW, AW, BW, XB * P, HEADS, 2 * CW])[:-1]
    gate, rec, z, xbc, dt, uv = np.split(w_in, cut, axis=1)
    gate = channel_chunks(gate)
    rows = w_out.reshape(KD, P, D)
    return ([np.zeros((P, CH), w_in.dtype)] + list(channel_chunks(rec)) + list(channel_chunks(xbc)) + list(region(dt)) + [gate[0]]
            + list(region(uv)) + [gate[1], gate[2]] + list(region(z)) + [rows[k] for k in OUT_ORDER])


def per_partition(v):
    return v.reshape(-1, P).T


def across(v):
    import numpy as np
    return np.broadcast_to(v.reshape(1, -1), (P, v.size))


def taps(w):
    return w.reshape(w.shape[0], -1, P).transpose(2, 1, 0).reshape(P, -1)


def diagonal(w):
    import numpy as np
    out = np.zeros((P, AB, P), w.dtype)
    for h in range(w.shape[0]):
        r = HD * (h % 2)
        out[r:r + HD, h // 2, r:r + HD] = w[h]
    return out.reshape(P, -1)


def mix_params(a, l):
    import numpy as np
    parts = [per_partition(a["mix_pre_g"][l]), taps(a["lru_conv_w"][l]), per_partition(a["lru_conv_b"][l]),
             taps(a["ssd_conv_w"][l]), per_partition(a["ssd_conv_b"][l]), per_partition(a["lru_b_r"][l]),
             per_partition(a["lru_b_i"][l]), per_partition(a["lru_lambda"][l]), diagonal(a["lru_w_r"][l]), diagonal(a["lru_w_i"][l]),
             across(a["mix_post_g"][l]), across(a["ssd_norm_g"][l]), across(a["sgu_ln_g"][l]), across(a["sgu_ln_b"][l]),
             across(a["ssd_dt_bias"][l]), across(a["ssd_a_log"][l]), across(a["ssd_d"][l]), a["sgu_b_s"][l].T,
             a["sgu_w_s"][l].transpose(2, 0, 1).reshape(P, -1)]
    return np.concatenate(parts, axis=1)


def mix2_chunks(a):
    import numpy as np
    w = a["w_in_2"][0]
    cut = np.cumsum([512, 512, 512, 512, 512] + [P] * 6 + [24])
    u, c_b, c_c, c_x, q, kc, vc, ks, vs, kw, vw, ng, mg = np.split(w, cut, axis=1)
    twice = [channel_chunks(np.concatenate([v[:, h * HD:(h + 1) * HD]] * 2, axis=1))[0] for v in (kc, vc) for h in range(2)]
    u, c_b, c_c, c_x, mg = [channel_chunks(v) for v in (u, c_b, c_c, c_x, mg)]
    b = np.zeros((4, P, 4, 2, P), w.dtype)
    for g in range(32):
        k, r, j = g // 8, g // 2 % 4, g % 2
        for i, name in enumerate(("ssm_b_re_2", "ssm_b_im_2")):
            b[k, 16 * (g % 8):16 * (g % 8) + 16, r, i, HD * j:HD * (j + 1)] = a[name][0, g].T
    b = b.reshape(4, P, CH)
    chunks = {}
    conv = [v for k in range(4) for v in (c_c[k], c_x[k], c_b[k])]
    chunks.update(zip(D_CONV, conv))
    chunks.update(zip(D_B, b))
    parts = list(region(q)) + twice + list(region(ng)) + [u[0], u[1], u[2]] + list(region(np.concatenate([ks, kw, vs, vw], axis=1))) + [u[3]]
    parts += [c for i in range(2) for c in region(a["cmp_w1_2"][0, i])]
    parts += [chunks[c] for c in range(D_CONV[0], D_MIX)]

    def half(v, i):
        return v[:, i * P:(i + 1) * P].reshape(4, P, P).transpose(1, 0, 2).reshape(P, -1)

    glu, conv_out, w_o = a["ssm_w_glu_2"][0], a["conv_w_out_2"][0], a["nsa_w_o_2"][0]
    for i in range(KD):
        parts += [mg[i], mg[KD + i], mg[2 * KD + i],
                  np.concatenate([half(glu, i), half(glu, KD + i)], axis=1), np.concatenate([half(conv_out, i), half(w_o, i)], axis=1)]
    parts += list(a["w_out_2"][0].reshape(KD, P, D))
    assert len(parts) == MIX2_CHUNKS
    return parts


def mix2_params(a):
    import numpy as np
    c = np.zeros((P, 16, 2, 32), a["ssm_c_re_2"].dtype)
    for g in range(32):
        j = g % 2
        for i, name in enumerate(("ssm_c_re_2", "ssm_c_im_2")):
            c[HD * j:HD * (j + 1), g // 2, i, 16 * j:16 * (j + 1)] = a[name][0, g].T
    states = lambda v: v.reshape(16, P).T
    pe = a["cmp_pe_2"][0].reshape(2, 16, 2 * HD).transpose(2, 0, 1).reshape(P, -1)
    w2 = a["cmp_w2_2"][0].reshape(2, 2, P, HD).transpose(2, 0, 1, 3).reshape(P, -1)
    parts = [per_partition(a["mix_norm_g_2"][0]), taps(a["conv_w_2"][0]), per_partition(a["ssm_d_2"][0]), states(a["ssm_lam_re_2"][0]),
             states(a["ssm_lam_im_2"][0]), states(np.repeat(a["ssm_log_dt_2"][0], HD)), c.reshape(P, -1), across(a["q_norm_g_2"][0]),
             across(a["k_norm_g_2"][0].reshape(-1)), pe, w2]
    return np.concatenate(parts, axis=1)


def kernel(**inputs):
    import numpy as np
    import concourse.bacc as bacc
    from concourse.bass_utils import run_bass_kernel_spmd as run

    a = {k: np.asarray(v) for k, v in inputs.items()}
    parts = []
    for l in range(LAYERS):
        parts += ffn_chunks(a["ffn1_w_gu"][l], a["ffn1_w_down"][l])
        parts += mix_chunks(a["mix_w_in"][l], a["mix_w_out"][l])
        parts += ffn_chunks(a["ffn2_w_gu"][l], a["ffn2_w_down"][l])
    parts += mix2_chunks(a)
    parts += ffn_chunks(a["ffn_w_gate_up_2"][0], a["ffn_w_down_2"][0])
    ffn_par = lambda pre, post: np.concatenate([per_partition(pre), across(post)], axis=1)
    g3 = a["ffn_norm_g_2"][0]
    arrays = {
        "stream": np.stack(parts),
        "x_in": a["x"].reshape(S, D),
        "pf_a": np.stack([ffn_par(a["ffn1_pre_g"][l], a["ffn1_post_g"][l]) for l in range(LAYERS)] + [ffn_par(g3, np.zeros_like(g3))]),
        "pf_b": np.stack([ffn_par(a["ffn2_pre_g"][l], a["ffn2_post_g"][l]) for l in range(LAYERS)]),
        "pm": np.stack([mix_params(a, l) for l in range(LAYERS)]),
        "pm2": mix2_params(a),
    }
    arrays = {k: np.ascontiguousarray(v) for k, v in arrays.items()}
    nc = bacc.Bacc("TRN2", target_bir_lowering=False, num_devices=1)
    args = [nc.dram_tensor(k, v.shape, F32, kind="ExternalInput").ap() for k, v in arrays.items()]
    out = nc.dram_tensor("out", (S, D), F32, kind="ExternalOutput").ap()
    block_program(nc, *args, out)
    r = run(nc, [arrays], core_ids=[0])
    return r.results[0]["out"].reshape(1, S, D)
```

```python
import concourse.bass as bass
from concourse import mybir
from concourse.alu_op_type import AluOpType as ALU
from contextlib import ExitStack

F32 = mybir.dt.float32
F32R = mybir.dt.float32r
ACT = mybir.ActivationFunctionType
AX = mybir.AxisListType

P = 128
S = 256
T = S // P
D = 1024
KD = D // P
FF = 2816
FT = FF // P
CH = 1024
RING = 6
EPS = 1e-6
NEG = -1e30
LAYERS = 2

AW, BW, CW = 384, 384, 256
AB = AW // P
XB = 7
HEADS = 6
HD = 64
VSTEPS = 63
AHEAD = 3

FFN_CHUNKS = 3 * FT
MIX_CHUNKS = 30
LAYER_CHUNKS = 2 * FFN_CHUNKS + MIX_CHUNKS
MIX2_CHUNKS = 89
MIX2_BASE = LAYERS * LAYER_CHUNKS
FFN3_BASE = MIX2_BASE + MIX2_CHUNKS
TOTAL = FFN3_BASE + FFN_CHUNKS
FFN_BASES = [0, FFN_CHUNKS + MIX_CHUNKS]
MIX_BASE = FFN_CHUNKS + 1

C_REC, C_XBC, C_DT, C_GATE0, C_UV, C_GATE1, C_Z, C_OUT = 0, 3, 10, 11, 12, 16, 18, 21
OUT_ORDER = [6, 7, 0, 1, 2, 3, 4, 5]


D_Q, D_KVC, D_NG, D_U, D_KV, D_U3, D_W1, D_EARLY = 0, 4, 8, 9, 12, 16, 17, 25
EARLY = [(i, b) for i in range(KD) for b in range(3)][:8]
D_ROUNDS = D_EARLY + len(EARLY)
D_CONV = [D_ROUNDS + c for c in (0, 1, 2, 4, 5, 6, 7, 9, 10, 11, 12, 14)]
D_B = [D_ROUNDS + c for c in (3, 8, 13, 15)]
SPLIT_AFTER = {0: [6], 1: [7], 2: [8], 3: [9, 10], 4: [11], 5: [12], 6: [13], 7: [14, 15], 8: [16], 9: [17],
               10: [18], 11: [19, 20], 15: [21]}
SPLIT_AFTER = {r: [D_ROUNDS + c for c in cs] for r, cs in SPLIT_AFTER.items()}
LATE = {}
for _i in range(KD):
    for _name in [f"g{_i}{_b}" for _b in range(3) if (_i, _b) not in EARLY] + [f"lin{_i}", f"br{_i}"]:
        LATE[_name] = D_ROUNDS + 16 + len(LATE)
D_OUT = D_ROUNDS + 16 + len(LATE)
TWO_PI_EXACT = 6.283185307179586
TWO_PI = 6.283185
TWO_PI_PARTS = [6.28125, 2.0 ** -9 * 0.990234375, TWO_PI_EXACT - 6.28125 - 2.0 ** -9 * 0.990234375]
MAGIC = 1.5 * 2.0 ** 23


def columns(*widths):
    at, out = 0, {}
    for name, w in widths:
        out[name] = slice(at, at + w)
        at += w
    return out, at


PM, NPM = columns(("pre_g", KD), ("rec_w", AB * 4), ("rec_b", AB), ("xbc_w", XB * 4), ("xbc_b", XB),
                  ("b_r", AB), ("b_i", AB), ("lam", AB), ("w_r", AB * P), ("w_i", AB * P),
                  ("post_g", D), ("norm_g", BW), ("ln_g", CW), ("ln_b", CW), ("dt_bias", HEADS),
                  ("a_log", HEADS), ("d_skip", HEADS), ("b_s", 4), ("w_s", 4 * P))
PF, NPF = columns(("pre_g", KD), ("post_g", D))


PN, NPN = columns(("cw", 12), ("ssm_d", 4), ("lre", 16), ("lim", 16), ("ldt", 16), ("c", 1024), ("q_g", HD),
                  ("k_g", 3 * HD), ("pe", 32), ("w2", 4 * HD), ("ffn_g", KD))


class Signal:

    def __init__(self, sem, per):
        self.sem, self.per, self.k = sem, per, 0

    def begin(self, round_):
        self.base, self.k = round_ * self.per, 0

    def inc(self, ins):
        ins.then_inc(self.sem, 1)
        self.k += 1

    def wait(self, eng, k):
        eng.wait_ge(self.sem, self.base + k)

    def end(self, name=""):
        assert self.k == self.per, (name, self.k, self.per)


class Place:

    def __init__(self, rounds, base):
        self.rounds, self.base = rounds, base

    def slot(self, c):
        return (self.base + c) % RING

    def count(self, c):
        return self.rounds * RING + (self.base + c + 1)

    def loaded(self, c):
        return (self.rounds + ((self.base + c) // RING + 1)) * 16

    def later(self, rounds):
        return Place(self.rounds + rounds, self.base)


BANKED = ([f"rec{b}" for b in range(AB)] + [f"xbc{b}" for b in range(XB)] + ["dt"] + [f"lru{b}" for b in range(AB)]
          + ["gate0", "uv0", "uv1", "gate1", "gate2", "xtok0", "xtok1", "cs", "z0", "z1", "sgu0", "sgu1", "yct0", "yct1"]
          + [f"csb{h}" for h in range(HEADS)] + ["ybt0", "ybt1", "ybt2"])
JOBS = [f"lru{b}" for b in range(AB)] + ["uv0", "xtok0", "xtok1", "cs", "cbt", "z0", "sgu0", "sgu1", "yct0", "yct1"]
JOBS += [f"csb{_h}" for _h in range(AHEAD)]
for _h in range(HEADS):
    JOBS += [f"y{_h}"] + ([f"csb{_h + AHEAD}"] if _h + AHEAD < HEADS else [])
JOBS += ["ybt0", "ybt1", "ybt2"]
JOB = {name: k + 1 for k, name in enumerate(JOBS)}
BANK = {name: k % 4 for k, name in enumerate(BANKED)}
BY_DVE = ["xtok0", "xtok1", "cs", "sgu0", "sgu1"] + [f"csb{h}" for h in range(HEADS)]
BY_ACT = [name for name in BANKED[:BANKED.index("sgu0")] if name not in BY_DVE]
Y_ORDER = ["yct0", "yct1", "ya", "ybt0", "ybt1", "ybt2"]


ROUNDS = 16
BANKED2 = (["q0", "q1"] + [f"kvc{i}" for i in range(4)] + ["ng", "u0", "u1", "u2", "kv0", "kv1", "u3", "hid0", "hid1", "e0", "e1",
           "hidt0", "hidt1", "e2", "cmp0", "cmp1", "e3", "qt00", "qt01", "qt10", "qt11", "kt0", "kt1", "e4", "kct", "e5", "e6", "cs0", "cs1", "e7"])
BY_DVE2 = ["cs0", "cs1"]
BY_ACT2 = [name for name in BANKED2 if name not in BY_DVE2]
JOBS2 = ["q0", "kv0"] + [name for name in BANKED2[BANKED2.index("hidt0"):] if name[0] != "e"]
for _r in range(ROUNDS + 1):
    _turn = [f"pt{_r - 1}"] if _r else []
    _new = [f"sc{_r}", f"bu{_r}"] if _r < ROUNDS else []
    _conv = [f"cv{_r}"] if _r < 12 else []
    BANKED2 += _new + _turn + _conv
    BY_ACT2 += _turn + (_conv if _r % 3 != 1 else [])
    BY_DVE2 += _new + (_conv if _r % 3 == 1 else [])
    JOBS2 += (_new if _r % 4 != 3 else _new[:1]) + ([f"y5{_r - 1}", f"pt{_r - 1}", f"pv{_r - 1}"] if _r else [])
_ots = [f"ot{b}" for b in range(4)]
BANKED2 += _ots
BY_DVE2 += _ots
JOBS2 += _ots
for _i in range(KD):
    _gates = [f"g{_i}{_b}" for _b in range(3) if (_i, _b) not in EARLY]
    BANKED2 += _gates + [f"lin{_i}", f"br{_i}"]
    BY_ACT2 += _gates
    BY_DVE2 += [f"lin{_i}", f"br{_i}"]
JOB2 = {name: k + 1 for k, name in enumerate(JOBS2)}
BANK2 = {name: k % 4 for k, name in enumerate(BANKED2)}


def block_program(nc, stream, x_in, pf_a, pf_b, pm, pm2, out):
    ctx = ExitStack()
    with ctx:
        def sb(name, shape, dt=F32):
            return ctx.enter_context(nc.sbuf_tensor(name, shape, dt))

        def sem(name):
            return ctx.enter_context(nc.semaphore(name))

        raw = sb("raw", [P, RING * CH])
        whi = sb("whi", [P, RING * CH], F32R)
        wlo = sb("wlo", [P, RING * CH], F32R)
        x = sb("x", [P, T, D])
        xn = sb("xn", [P, T, D])
        u32 = sb("u32", [P, 4, S])
        xhi = sb("xhi", [P, KD, S], F32R)
        xlo = sb("xlo", [P, KD, S], F32R)
        yhi, ylo = xhi, xlo
        sg = sb("sg", [P, 2, S])
        h32 = sb("h32", [P, 2, S])
        hhi = sb("hhi", [P, 2, S], F32R)
        hlo = sb("hlo", [P, 2, S], F32R)
        pfa = sb("pfa", [P, NPF])
        pfb = sb("pfb", [P, NPF])
        par = sb("par", [P, NPM])
        ident = sb("ident", [P, P])
        upper = sb("upper", [P, S])
        maskadd = sb("maskadd", [P, S])
        ss = sb("ss", [P, 4 * T])
        ms = sb("ms", [P, 4 * T])
        rstd = sb("rstd", [P, 4 * T])
        pss, prstd = sb("pss", [P, 2 * T]), sb("prstd", [P, T])
        xss, xrstd = sb("xss", [P, 2 * T]), sb("xrstd", [P, T])
        small = sb("small", [P, 2])

        scope = ExitStack()

        def m1(name, shape, dt=F32):
            return scope.enter_context(nc.sbuf_tensor(name, shape, dt))

        recpad = m1("recpad", [P, AB, S + 3])
        xbcpad = m1("xbcpad", [P, XB, S + 3])
        recc = m1("recc", [P, AB, S])
        xbcc = m1("xbcc", [P, XB, S])
        gateT = m1("gateT", [P, AB, S])
        rg = m1("rg", [P, AB, S])
        ig = m1("ig", [P, AB, S])
        aa = m1("aa", [P, AB, S])
        th = m1("th", [P, AB, S])
        uv = m1("uv", [P, T, 2 * CW])
        zs = m1("zs", [P, T, BW])
        xtok = m1("xtok", [P, T, BW])
        spin = m1("spin", [P, T * HEADS + AB])
        spe = m1("spe", [P, T * HEADS + AB])
        sp_ = m1("sp_", [P, T * HEADS + AB])
        dtraw = m1("dtraw", [P, T, HEADS])
        ea = m1("ea", [P, HEADS])
        ad = m1("ad", [P, T, HEADS])
        ncs = m1("ncs", [P, T, HEADS])
        psp = m1("psp", [P, 2, AB])
        dm = m1("dm", [P, 2, 384])
        mm = m1("mm", [P, 2, 384])
        yb = m1("yb", [P, T, BW])
        yc = m1("yc", [P, T, CW])
        vx = m1("vx", [P, T, CW])
        lnm = m1("lnm", [P, 2, T])

        scope.close()
        y5hi, y5lo = sb("y5hi", [P, 4, S], F32R), sb("y5lo", [P, 4, S], F32R)
        cvhi, cvlo = sb("cvhi", [P, 4, S], F32R), sb("cvlo", [P, 4, S], F32R)
        scope = ExitStack()
        qT = m1("qT", [HD, 8, S])
        kT = m1("kT", [HD, 4, S])
        xchi, xclo = m1("xchi", [P, 2, 16, 16], F32R), m1("xclo", [P, 2, 16, 16], F32R)
        hidT = m1("hidT", [P, 2, 2, 16])
        kcn, vcs = m1("kcn", [16, HD]), m1("vcs", [16, HD])
        kcT = m1("kcT", [HD, 16])
        zpad = m1("zpad", [P, S + 2])
        cc, cb, cvt = m1("cc", [P, S]), m1("cb", [P, S]), m1("cvt", [P, S])
        sm = m1("sm", [P, 2, 2, S])
        pT = m1("pT", [P, 2, 512])
        pcT = m1("pcT", [16, 2, P])
        pc = m1("pc", [P, T, 8, 16])
        ce = m1("ce", [P, T, 8, 8])
        cst = m1("cst", [P, 8])
        table = [m1("table", [P, 2, 3, S]), par[:, NPN:NPN + 6 * S].rearrange("p (a b n) -> p a b n", a=2, b=3)]
        frac = m1("frac", [P, 2, S])
        v2, g2 = m1("v2", [P, 2, S]), m1("g2", [P, 2, S])
        q1, q2 = m1("q1", [P, 2, S]), m1("q2", [P, 2, S])
        y5t = m1("y5t", [P, S])
        tokens_f = m1("tokens_f", [P, S])
        qmask = m1("qmask", [P, S])
        cmask = m1("cmask", [P, T, 2, 8])
        ngate = m1("ngate", [P, T * 24])
        s5p = m1("s5p", [P, 8, 16])
        qk_ms, qk_rstd = m1("qk_ms", [P, 24]), m1("qk_rstd", [P, 24])
        kc_st = m1("kc_st", [P, 2])
        halves = m1("halves", [P, 24])
        magic = m1("magic", [P, 2])
        nm, rs = m1("nm", [P, 2, 2]), m1("rs", [P, 2, 2])
        uT = u32
        gates32 = [pfb[:, j * S:(j + 1) * S] for j in range(4)] + [xn[:, t, j * S:(j + 1) * S] for t in range(T) for j in range(2)]
        xc = v2[:, :, :].rearrange("p w (j n) -> p w j n", j=16)
        hid = g2
        otok = sm[:, :, :, :].rearrange("p t b n -> p t (b n)")
        scope.close()
        ohi, olo = sb("ohi", [P, 4, S], F32R), sb("olo", [P, 4, S], F32R)
        mxhi, mxlo = sb("mxhi", [P, KD, S], F32R), sb("mxlo", [P, KD, S], F32R)
        gsg, sgl = sb("gsg", [P, 2, 3, S]), sb("sgl", [P, 2, S])
        mt = sb("mt", [P, 3, S])

        acc = ctx.enter_context(nc.psum_tensor("acc", [P, T, D], F32))
        W = [ctx.enter_context(nc.psum_tensor(f"work{i}", [P, 512], F32)) for i in range(4)]

        arrived = [sem(f"arrived{i}") for i in range(RING)]
        hi_ready = sem("hi_ready")
        lo_ready = sem("lo_ready")
        consumed = sem("consumed")
        credits = sem("credits")
        consts = sem("consts")
        x_loaded = sem("x_loaded")
        pfa_loaded, pfb_loaded, par_loaded = sem("pfa_loaded"), sem("pfb_loaded"), sem("par_loaded")
        x_ready = sem("x_ready")
        ss_ready = sem("ss_ready")
        ms_ready = sem("ms_ready")
        rstd_ready = sem("rstd_ready")
        xn_ready = sem("xn_ready")
        xt_ready = sem("xt_ready")
        xhi_ready = sem("xhi_ready")
        xlo_ready = sem("xlo_ready")
        acc_ready = sem("acc_ready")
        pss_ready = sem("pss_ready")
        pms_ready = sem("pms_ready")
        prstd_ready = sem("prstd_ready")
        upd_ready = sem("upd_ready")
        sg_ready = sem("sg_ready")
        h32_ready = sem("h32_ready")
        hhi_ready = sem("hhi_ready")
        hlo_ready = sem("hlo_ready")
        out_stored = sem("out_stored")
        pads = sem("pads")

        mixsigs = {}

        def mixsig(name, per):
            mixsigs[name] = Signal(sem("m_" + name), per)
            return mixsigs[name]

        job = mixsig("job", len(JOBS))
        evac = mixsig("evac", len(BY_ACT))
        vec = mixsig("vec", len(BY_DVE))
        y_hi = mixsig("y_hi", len(Y_ORDER))
        y_lo = mixsig("y_lo", len(Y_ORDER))
        rec_conv = mixsig("rec_conv", AB)
        xbc_conv = mixsig("xbc_conv", XB)
        xbc_act = mixsig("xbc_act", XB)
        spin_ready = mixsig("spin", 1)
        soft = mixsig("soft", 3)
        ea_ready = mixsig("ea", 1)
        psp_ready = mixsig("psp", 1)
        ad_ready = mixsig("ad", 1)
        a_ready = mixsig("a", AB)
        th_ready = mixsig("th", AB)
        mult2 = mixsig("mult2", 1)
        mult_ready = mixsig("mult", 1)
        ya32 = mixsig("ya32", 1)
        dexp = mixsig("dexp", HEADS)
        m_ready = mixsig("m", HEADS)
        ysum = mixsig("ysum", T)
        yss = mixsig("yss", T)
        yms = mixsig("yms", T)
        yrstd = mixsig("yrstd", T)
        ybn = mixsig("ybn", T)
        vcen = mixsig("vcen", T)
        vss = mixsig("vss", T)
        vms = mixsig("vms", T)
        vrstd = mixsig("vrstd", T)
        vln = mixsig("vln", T)
        yc_ready = mixsig("yc", T)
        wst = mixsig("wst", 1)
        vstep = mixsig("vstep", VSTEPS)

        def one(name):
            s = Signal(sem("n_" + name), 0)
            s.begin(0)
            return s

        job2, evac2, vec2 = one("job"), one("evac"), one("vec")
        (s5a, s5v, s5m, nrm, ucopy, uhl_ready, xc32, xcs, xc_ready, qn_ready, kcn_ready, wc_ready, csm, cexp, pc_ready, tab_k, tab,
         frac_ready, smax, sexp, pscaled, rot_ready, y5sum, y5g, y5_hi, y5_split, scanned, coef_ready, pool_step, early_gate, cz, cv32, cv_hi, cv_split, otok_ready, o_hi, sgl_ready,
         mix32, mix_hi, mix_lo, vstep2) = [one(n) for n in (
             "s5a s5v s5m nrm ucopy uhl xc32 xcs xc qn kcn wc csm cexp pc tabk tab frac smax sexp pscaled rot y5sum y5g y5hi y5split "
             "scanned coef poolstep egate cz cv32 cvhi cvsplit otok ohi sgl mix32 mixhi mixlo vstep2").split()]
        consts2 = sem("consts2")

        block = ctx.enter_context(nc.Block())

        def chunk(tensor, place, c, n=1):
            at = place.slot(c)
            assert at + n <= RING
            return tensor[:, at * CH:(at + n) * CH]

        def split_hi(act, place, cs):
            for c in cs:
                act.wait_ge(arrived[place.slot(c)], place.loaded(c))
                act.wait_ge(consumed, place.count(c))
                nc.scalar.activation(chunk(whi, place, c), chunk(raw, place, c), ACT.Copy).then_inc(hi_ready, 1)

        def split_lo(dve, place, cs):
            for c in cs:
                dve.wait_ge(hi_ready, place.count(c))
                nc.vector.tensor_tensor(chunk(wlo, place, c), chunk(raw, place, c), chunk(whi, place, c).bitcast(F32),
                                        ALU.subtract).then_inc(lo_ready, 1)

        def product(o, lhi, llo, rhi, rlo, start, stop):
            return [nc.tensor.matmul(o, lhi, rhi, start=start, stop=False),
                    nc.tensor.matmul(o, lhi, rlo, start=False, stop=False),
                    nc.tensor.matmul(o, llo, rhi, start=False, stop=stop)]

        def bc(ap, n):
            return ap.unsqueeze(2).broadcast_to([P, ap.shape[1], n])

        def granule(i, a):
            bank = W[i % 4][:, 0:512] if i < 4 else acc[:, i % 4 // 2, (i % 2) * 512:(i % 2 + 1) * 512]
            return bank[:, a * P:(a + 1) * P], i // 4, i % 4 * 2 + a

        def acc_wait(eng, p, t, h, end):
            if (t, h) == (T - 1, 1):
                eng.wait_ge(consumed, end + RING)
            else:
                eng.wait_ge(acc_ready, p * (2 * T - 1) + (2 * t + h + 1))

        def halves_of(h):
            return slice(h * D // 2, (h + 1) * D // 2)

        def post_squares(act, p, end, c):
            for t in range(T):
                for h in range(2):
                    acc_wait(act, p, t, h, end)
                    nc.scalar.activation(xn[:, t, halves_of(h)], acc[:, t, halves_of(h)], ACT.Square, scale=D ** -0.5 / c,
                                         accum_out=pss[:, 2 * t + h:2 * t + h + 1]).then_inc(pss_ready, 1)

        def prenorm_act(act, q, g, place=None, early=()):
            for t in range(T):
                for h in range(2):
                    act.wait_ge(x_ready, q * 2 * T + (2 * t + h + 1))
                    nc.scalar.activation(xn[:, t, halves_of(h)], x[:, t, halves_of(h)], ACT.Square, scale=D ** -0.5,
                                         accum_out=xss[:, 2 * t + h:2 * t + h + 1]).then_inc(ss_ready, 1)
            split_hi(act, place, early)
            for i in range(8):
                act.wait_ge(xt_ready, q * 8 + (i + 1))
                for a in range(2):
                    bank, t, k = granule(i, a)
                    ins = nc.scalar.activation(xhi[:, k, t * P:(t + 1) * P], bank, ACT.Identity, scale=g[:, k:k + 1])
                ins.then_inc(xhi_ready, 1)

        def mean_square(parts, t, out, done, eps):
            nc.vector.scalar_tensor_tensor(out=out[:, t:t + 1], in0=parts[:, 2 * t:2 * t + 1], scalar=eps, in1=parts[:, 2 * t + 1:2 * t + 2],
                                           op0=ALU.add, op1=ALU.add).then_inc(done, 1)

        ffn_late = [FFN_CHUNKS + 2, FFN_CHUNKS + 3]

        def norm_pool(pool, q, p=None):
            if p is not None:
                for t in range(T):
                    pool.wait_ge(pms_ready, p * T + (t + 1))
                    nc.gpsimd.tensor_tensor(prstd[:, t:t + 1], prstd[:, t:t + 1], small[:, 0:1], ALU.pow).then_inc(prstd_ready, 1)
            for t in range(T):
                pool.wait_ge(ms_ready, q * T + (t + 1))
                nc.gpsimd.tensor_tensor(xrstd[:, t:t + 1], xrstd[:, t:t + 1], small[:, 0:1], ALU.pow).then_inc(rstd_ready, 1)

        def post_mean(dve, p, t, c):
            dve.wait_ge(pss_ready, p * 2 * T + (2 * t + 2))
            mean_square(pss, t, prstd, pms_ready, EPS / c ** 2)

        def post_update(dve, p, t, g):
            dve.wait_ge(prstd_ready, p * T + (t + 1))
            for h in range(2):
                o = xn[:, t, halves_of(h)]
                nc.vector.scalar_tensor_tensor(out=o, in0=acc[:, t, halves_of(h)], scalar=prstd[:, t:t + 1],
                                               in1=g[:, halves_of(h)], op0=ALU.mult, op1=ALU.mult).then_inc(upd_ready, 1)
                dve.wait_ge(upd_ready, p * 2 * T + (2 * t + h + 1))
                nc.vector.tensor_tensor(x[:, t, halves_of(h)], x[:, t, halves_of(h)], o, ALU.add).then_inc(x_ready, 1)

        def plain_update(dve, p, t, end):
            for h in range(2):
                acc_wait(dve, p, t, h, end)
                nc.vector.tensor_tensor(x[:, t, halves_of(h)], x[:, t, halves_of(h)], acc[:, t, halves_of(h)], ALU.add).then_inc(x_ready, 1)

        def norm_dve(dve, q, g, updates=((lambda: None,) * 3), place=None, late=()):
            def mean(t):
                dve.wait_ge(ss_ready, q * 2 * T + (2 * t + 2))
                mean_square(xss, t, xrstd, ms_ready, EPS)

            def scaled(t):
                dve.wait_ge(rstd_ready, q * T + (t + 1))
                for h in range(2):
                    nc.vector.tensor_scalar(xn[:, t, halves_of(h)], x[:, t, halves_of(h)], xrstd[:, t:t + 1], None, ALU.mult).then_inc(xn_ready, 1)

            def low(i):
                dve.wait_ge(xhi_ready, q * 8 + (i + 1))
                for a in range(2):
                    bank, t, k = granule(i, a)
                    ins = nc.vector.scalar_tensor_tensor(out=xlo[:, k, t * P:(t + 1) * P], in0=bank, scalar=g[:, k:k + 1],
                                                         in1=xhi[:, k, t * P:(t + 1) * P].bitcast(F32), op0=ALU.mult, op1=ALU.subtract)
                ins.then_inc(xlo_ready, 1)

            updates[0]()
            updates[1]()
            split_lo(dve, place, late[:1])
            mean(0)
            updates[2]()
            scaled(0)
            mean(1)
            split_lo(dve, place, late[1:])
            scaled(1)
            for i in range(8):
                low(i)

        def post_updates(dve, p, g, c):
            def first():
                post_mean(dve, p, 0, c)
                post_update(dve, p, 0, g)
            return first, lambda: post_mean(dve, p, 1, c), lambda: post_update(dve, p, 1, g)

        def norm_pe(pe, q, padding=False):
            for i in range(8):
                pe.wait_ge(xn_ready, q * 2 * T + (i // 2 + 1))
                for a in range(2):
                    bank, t, k = granule(i, a)
                    m = nc.tensor.transpose(bank, xn[:, t, k * P:(k + 1) * P], ident[:, :])
                    if padding and i == 0 and a == 0:
                        m.then_inc(consumed, 1)
                m.then_inc(xt_ready, 1)

        def xn_wait(pe, q, k):
            if k % 2 == 0:
                pe.wait_ge(xlo_ready, q * 8 + (5 + k // 2))

        def last_two(pe, at, cs, left, ready):
            for t in range(T):
                for n, c in enumerate(cs):
                    if t == 0:
                        pe.wait_ge(lo_ready, at.count(c))
                        ready(n)
                    hi, lo = chunk(whi, at, c), chunk(wlo, at, c)
                    for h in range(2):
                        m = product(acc[:, t, halves_of(h)], *left(n, t), hi[:, halves_of(h)], lo[:, halves_of(h)], False, n == 1)[-1]
                        if (t, h) == (T - 1, 1):
                            m.then_inc(consumed, 1)
                        elif n == 1:
                            m.then_inc(acc_ready, 1)

        def ffn_pe(pe, n, q, place):
            def gate_up(at, c, j, drained=None, first=False):
                for i in range(2):
                    pe.wait_ge(lo_ready, at.count(c + i))
                    if i == 0 and drained is not None:
                        pe.wait_ge(h32_ready, drained)
                    hi, lo = chunk(whi, at, c + i), chunk(wlo, at, c + i)
                    for k in range(KD):
                        if first and i == 0:
                            xn_wait(pe, q, k)
                        m = product(W[j][:, i * S:(i + 1) * S], hi[:, k * P:(k + 1) * P], lo[:, k * P:(k + 1) * P],
                                    xhi[:, k, :], xlo[:, k, :], k == 0, k == KD - 1)[-1]
                    m.then_inc(consumed, 1)

            def down(at, c, j, hidden, first=False):
                pe.wait_ge(lo_ready, at.count(c))
                pe.wait_ge(hlo_ready, hidden)
                hi, lo = chunk(whi, at, c), chunk(wlo, at, c)
                for t in range(T):
                    for h in range(2):
                        cols = slice(h * 512, (h + 1) * 512)
                        m = product(acc[:, t, cols], hhi[:, j, t * P:(t + 1) * P], hlo[:, j, t * P:(t + 1) * P],
                                    hi[:, cols], lo[:, cols], first, False)[-1]
                m.then_inc(consumed, 1)

            gate_up(place, 0, 0, first=True)
            gate_up(place, 2, 1)
            down(place, 4, 0, n * FT + 1, first=True)

            def pair(i, last=False):
                for u in range(2):
                    gate_up(place.later(i), 5 + 3 * u, u, drained=n * FT + i * 2 + (u + 1))
                    if not (last and u):
                        down(place.later(i), 7 + 3 * u, 1 - u, n * FT + i * 2 + (u + 2))

            pairs = (FT - 2) // 2
            with pe.Fori(0, pairs - 1) as i:
                pair(i)
            pair(pairs - 1, last=True)
            last_two(pe, place, [FFN_CHUNKS - 2, FFN_CHUNKS - 1],
                     lambda j, t: (hhi[:, j, t * P:(t + 1) * P], hlo[:, j, t * P:(t + 1) * P]),
                     lambda j: pe.wait_ge(hlo_ready, n * FT + (FT - 1 + j)))

        def ffn_act(act, n, place, last=False):
            def tile(at, j, c, split):
                act.wait_ge(consumed, at.count(c) + RING)
                nc.scalar.activation(sg[:, j, :], W[j][:, 0:S], ACT.Silu).then_inc(sg_ready, 1)
                split_hi(act, at, split)

            tile(place, 0, 1, range(4, 7))
            tile(place, 1, 3, range(7, 10))
            with act.Fori(1, FT // 2 - last) as i:
                for u in range(2):
                    tile(place.later(i), u, 3 * u, range(4 + 3 * u, 7 + 3 * u))
            if last:
                tile(place, 0, 3 * (FT - 2), range(FFN_CHUNKS - 2, FFN_CHUNKS))
                tile(place, 1, 3 * (FT - 1), [])

        def ffn_dve(dve, n, place, last=False):
            def tile(at, m, j, c, split, free=None):
                dve.wait_ge(consumed, at.count(c) + RING)
                dve.wait_ge(sg_ready, m + 1)
                nc.vector.tensor_tensor(h32[:, j, :], sg[:, j, :], W[j][:, S:2 * S], ALU.mult).then_inc(h32_ready, 1)
                if free is not None:
                    dve.wait_ge(consumed, at.count(free) + RING)
                dve.wait_ge(h32_ready, m + 1)
                nc.vector.tensor_copy(hhi[:, j, :], h32[:, j, :]).then_inc(hhi_ready, 1)
                dve.wait_ge(hhi_ready, m + 1)
                nc.vector.tensor_tensor(hlo[:, j, :], h32[:, j, :], hhi[:, j, :].bitcast(F32), ALU.subtract).then_inc(hlo_ready, 1)
                split_lo(dve, at, split)

            tile(place, n * FT, 0, 1, range(4, 7))
            tile(place, n * FT + 1, 1, 3, range(7, 10))
            with dve.Fori(1, FT // 2 - 1) as i:
                for u in range(2):
                    tile(place.later(i), n * FT + i * 2 + u, u, 3 * u, range(4 + 3 * u, 7 + 3 * u), free=3 * u - 2)
            end = range(3 * (FT - 2) + 4, FFN_CHUNKS) if last else range(3 * (FT - 2) + 4, 3 * (FT - 2) + 7)
            tile(place, n * FT + FT - 2, 0, 3 * (FT - 2), end, free=3 * (FT - 2) - 2)
            tile(place, n * FT + FT - 1, 1, 3 * (FT - 1), [] if last else [FFN_CHUNKS + 1], free=3 * (FT - 1) - 2)

        def bank(name, cols=slice(0, 512)):
            return W[BANK[name]][:, cols]

        def begin(pe, banked, name):
            i = banked.index(name)
            if i < 4:
                return
            before = banked[i - 4]
            if before in BY_ACT:
                evac.wait(pe, BY_ACT.index(before) + 1)
            elif before in BY_DVE:
                vec.wait(pe, BY_DVE.index(before) + 1)
            else:
                y_lo.wait(pe, Y_ORDER.index(before) + 1)

        def mix_pe(pe, q, place):
            def done(name, ins):
                job.inc(ins)
                assert job.k == JOB[name], name

            def channels(name, c):
                begin(pe, BANKED, name)
                pe.wait_ge(lo_ready, place.count(c))
                hi, lo = chunk(whi, place, c), chunk(wlo, place, c)
                for k in range(KD):
                    m = product(bank(name, slice(0, S)), hi[:, k * P:(k + 1) * P], lo[:, k * P:(k + 1) * P],
                                xhi[:, k, :], xlo[:, k, :], k == 0, k == KD - 1)
                m[-1].then_inc(consumed, 1)

            def tokens(name, t, c, n, at=0):
                chunks = -(-KD * n // CH)
                pe.wait_ge(lo_ready, place.count(c + chunks - 1))
                hi, lo = chunk(whi, place, c, chunks), chunk(wlo, place, c, chunks)
                recent = []
                for k in range(KD):
                    recent += product(bank(name, slice(at, at + n)), xhi[:, k, t * P:(t + 1) * P], xlo[:, k, t * P:(t + 1) * P],
                                      hi[:, k * n:(k + 1) * n], lo[:, k * n:(k + 1) * n], k == 0, k == KD - 1)
                return recent[-4:]

            def release(matmuls, n):
                for m in matmuls[-n:]:
                    m.then_inc(consumed, 1)

            pe.wait_ge(xlo_ready, q * 8 + 8)
            for b in range(AB):
                channels(f"rec{b}", C_REC + b)
            for b in range(XB):
                channels(f"xbc{b}", C_XBC + b)
            begin(pe, BANKED, "dt")
            tokens("dt", 0, C_DT, HEADS)
            release(tokens("dt", 1, C_DT, HEADS, at=8), 1)
            for b in range(AB):
                begin(pe, BANKED, f"lru{b}")
                rec_conv.wait(pe, b + 1)
                for i, w in enumerate(("w_r", "w_i")):
                    m = nc.tensor.matmul(bank(f"lru{b}", slice(i * S, (i + 1) * S)), par[:, PM[w]][:, b * P:(b + 1) * P],
                                         recc[:, b, :], start=True, stop=True)
                done(f"lru{b}", m)
            channels("gate0", C_GATE0)
            begin(pe, BANKED, "uv0")
            done("uv0", tokens("uv0", 0, C_UV, 2 * CW)[-1])
            begin(pe, BANKED, "uv1")
            release(tokens("uv1", 1, C_UV, 2 * CW), 4)
            channels("gate1", C_GATE1)
            channels("gate2", C_GATE1 + 1)
            xbc_act.wait(pe, AB)
            for t in range(T):
                begin(pe, BANKED, f"xtok{t}")
                for b in range(AB):
                    m = nc.tensor.transpose(bank(f"xtok{t}", slice(b * P, (b + 1) * P)), xbcc[:, b, t * P:(t + 1) * P], ident[:, :])
                done(f"xtok{t}", m)
            begin(pe, BANKED, "cs")
            ad_ready.wait(pe, 1)
            tri, ones = upper[:, 0:P], upper[:, P:S]
            nc.tensor.matmul(bank("cs", slice(0, HEADS)), tri, ad[:, 0, :], start=True, stop=True)
            nc.tensor.matmul(bank("cs", slice(8, 8 + HEADS)), ones, ad[:, 0, :], start=True, stop=False)
            done("cs", nc.tensor.matmul(bank("cs", slice(8, 8 + HEADS)), tri, ad[:, 1, :], start=False, stop=True))
            xbc_act.wait(pe, XB)
            for g in range(2):
                bT, cT, o = xbcc[:, AB + g, :], xbcc[:, AB + 2 + g, :], acc[:, 1, g * 512:g * 512 + 384]
                nc.tensor.matmul(o[:, 0:S], bT[:, 0:P], cT, start=True, stop=True)
                m = nc.tensor.matmul(o[:, S:384], bT[:, P:S], cT[:, P:S], start=True, stop=True)
            done("cbt", m)
            begin(pe, BANKED, "z0")
            done("z0", tokens("z0", 0, C_Z, BW)[-1])
            begin(pe, BANKED, "z1")
            release(tokens("z1", 1, C_Z, BW), 3)
            wst.wait(pe, 1)
            for t in range(T):
                begin(pe, BANKED, f"sgu{t}")
                vln.wait(pe, t + 1)
                for g in range(4):
                    m = nc.tensor.matmul(bank(f"sgu{t}", slice(g * HD, (g + 1) * HD)), par[:, PM["w_s"]][:, g * P:(g + 1) * P],
                                         vx[:, t, g * HD:(g + 1) * HD], start=True, stop=True)
                done(f"sgu{t}", m)
            yc_ready.wait(pe, T)
            for b in range(2):
                begin(pe, BANKED, f"yct{b}")
                for t in range(T):
                    m = nc.tensor.transpose(bank(f"yct{b}", slice(t * P, (t + 1) * P)), yc[:, t, b * P:(b + 1) * P], ident[:, :])
                done(f"yct{b}", m)

            def sums(h):
                begin(pe, BANKED, f"csb{h}")
                o = bank(f"csb{h}", slice(0, S))
                nc.tensor.matmul(o, ad[:, 0, h:h + 1].broadcast_to([P, P]), upper[:, :], start=True, stop=False)
                done(f"csb{h}", nc.tensor.matmul(o[:, P:S], ad[:, 1, h:h + 1].broadcast_to([P, P]), tri, start=False, stop=True))

            for h in range(AHEAD):
                sums(h)
            vec.wait(pe, BY_DVE.index("xtok1") + 1)
            for h in range(HEADS):
                m_ready.wait(pe, h + 1)
                w, cols = mm[:, h % 2], slice(h * HD, (h + 1) * HD)
                o1 = acc[:, 0, 512 + h * HD:512 + (h + 1) * HD]
                nc.tensor.matmul(acc[:, 0, cols], w[:, 0:P], xtok[:, 0, cols], start=True, stop=True)
                nc.tensor.matmul(o1, w[:, P:S], xtok[:, 0, cols], start=True, stop=False)
                done(f"y{h}", nc.tensor.matmul(o1, w[:, S:384], xtok[:, 1, cols], start=False, stop=True))
                if h + AHEAD < HEADS:
                    sums(h + AHEAD)
            ysum.wait(pe, T)
            need = [1, 2, 3, 3, 3, 4, 5, 6]
            for i, k in enumerate(OUT_ORDER[:-2]):
                if i == 2:
                    ybn.wait(pe, T)
                    for b in range(AB):
                        begin(pe, BANKED, f"ybt{b}")
                        for t in range(T):
                            m = nc.tensor.transpose(bank(f"ybt{b}", slice(t * P, (t + 1) * P)), yb[:, t, b * P:(b + 1) * P], ident[:, :])
                        done(f"ybt{b}", m)
                pe.wait_ge(lo_ready, place.count(C_OUT + i))
                y_lo.wait(pe, need[i])
                hi, lo = chunk(whi, place, C_OUT + i), chunk(wlo, place, C_OUT + i)
                for t in range(T):
                    for h in range(2):
                        cols = slice(h * 512, (h + 1) * 512)
                        m = product(acc[:, t, cols], yhi[:, k, t * P:(t + 1) * P], ylo[:, k, t * P:(t + 1) * P],
                                    hi[:, cols], lo[:, cols], i == 0, False)[-1]
                m.then_inc(consumed, 1)
            last_two(pe, place, [C_OUT + KD - 2, C_OUT + KD - 1],
                     lambda n, t: (yhi[:, OUT_ORDER[KD - 2 + n], t * P:(t + 1) * P], ylo[:, OUT_ORDER[KD - 2 + n], t * P:(t + 1) * P]),
                     lambda n: y_lo.wait(pe, need[KD - 2 + n]))

        def mix_act(act, place):
            def emptied(name, ins):
                evac.inc(ins)
                assert BY_ACT[evac.k - 1] == name, name

            def projected(c):
                act.wait_ge(consumed, place.count(c) + RING)

            split_hi(act, place, [3, 4, 5])
            for b in range(AB):
                projected(C_REC + b)
                emptied(f"rec{b}", nc.scalar.activation(recpad[:, b, 3:], bank(f"rec{b}", slice(0, S)), ACT.Copy))
                split_hi(act, place, [C_REC + b + 6])
            for b in range(XB):
                projected(C_XBC + b)
                emptied(f"xbc{b}", nc.scalar.activation(xbcpad[:, b, 3:], bank(f"xbc{b}", slice(0, S)), ACT.Copy))
                split_hi(act, place, [C_XBC + b + 6])
            projected(C_DT)
            emptied("dt", nc.scalar.activation(dtraw[:, :, :], bank("dt", slice(0, 16)).rearrange("p (t h) -> p t h", t=T)[:, :, 0:HEADS], ACT.Copy))
            split_hi(act, place, [C_DT + 6])
            act.wait_ge(par_loaded, mixround(1) * 16)
            spin_ready.wait(act, 1)
            soft.inc(nc.scalar.activation(spe[:, :], spin[:, :], ACT.Abs))
            soft.wait(act, 1)
            soft.inc(nc.scalar.activation(sp_[:, :], spe[:, :], ACT.Exp, scale=-1.0))
            soft.wait(act, 2)
            soft.inc(nc.scalar.activation(spe[:, :], sp_[:, :], ACT.Ln, bias=1.0))
            ea_ready.inc(nc.scalar.activation(ea[:, :], par[:, PM["a_log"]], ACT.Exp))
            for b in range(AB):
                job.wait(act, JOB[f"lru{b}"])
                nc.scalar.activation(rg[:, b, :], bank(f"lru{b}", slice(0, S)), ACT.Sigmoid, bias=par[:, PM["b_r"]][:, b:b + 1])
                emptied(f"lru{b}", nc.scalar.activation(ig[:, b, :], bank(f"lru{b}", slice(S, 2 * S)), ACT.Sigmoid, bias=par[:, PM["b_i"]][:, b:b + 1]))
            projected(C_GATE0)
            emptied("gate0", nc.scalar.activation(gateT[:, 0, :], bank("gate0", slice(0, S)), ACT.Gelu_apprx_tanh))
            split_hi(act, place, [C_GATE0 + 6])
            job.wait(act, JOB["uv0"])
            emptied("uv0", nc.scalar.activation(uv[:, 0, :], bank("uv0"), ACT.Gelu_apprx_tanh))
            projected(C_UV + 3)
            emptied("uv1", nc.scalar.activation(uv[:, 1, :], bank("uv1"), ACT.Gelu_apprx_tanh))
            split_hi(act, place, range(C_UV + 6, C_UV + 10))
            for b in range(XB):
                xbc_conv.wait(act, b + 1)
                xbc_act.inc(nc.scalar.activation(xbcc[:, b, :], xbcc[:, b, :], ACT.Silu))
            for b in range(2):
                projected(C_GATE1 + b)
                emptied(f"gate{b + 1}", nc.scalar.activation(gateT[:, b + 1, :], bank(f"gate{b + 1}", slice(0, S)), ACT.Gelu_apprx_tanh))
                split_hi(act, place, [C_GATE1 + b + 6])
            psp_ready.wait(act, 1)
            evac.wait(act, BY_ACT.index(f"lru{AB - 1}") + 1)
            for b in range(AB):
                a_ready.inc(nc.scalar.activation(aa[:, b, :], rg[:, b, :], ACT.Exp, scale=psp[:, 1, b:b + 1]))
                th_ready.inc(nc.scalar.activation(th[:, b, :], rg[:, b, :], ACT.Tanh, scale=psp[:, 0, b:b + 1]))
            for t in range(T):
                vcen.wait(act, t + 1)
                vss.inc(nc.scalar.activation(yc[:, t, :], vx[:, t, :], ACT.Square, scale=CW ** -0.5, accum_out=ss[:, 2 + t:3 + t]))
            mult2.wait(act, 1)
            mult_ready.inc(nc.scalar.activation(th[:, :, :], th[:, :, :], ACT.Sqrt))
            job.wait(act, JOB["z0"])
            emptied("z0", nc.scalar.activation(zs[:, 0, :], bank("z0", slice(0, BW)), ACT.Silu))
            projected(C_Z + 2)
            emptied("z1", nc.scalar.activation(zs[:, 1, :], bank("z1", slice(0, BW)), ACT.Silu))
            split_hi(act, place, range(C_Z + 6, C_Z + 9))
            for i in range(2):
                job.wait(act, JOB[f"yct{i}"])
                y_hi.inc(nc.scalar.activation(yhi[:, 6 + i, :], bank(f"yct{i}", slice(0, S)), ACT.Copy))
            ya32.wait(act, 1)
            y_hi.inc(nc.scalar.activation(yhi[:, 0:AB, :], rg[:, :, :], ACT.Copy))
            for h in range(HEADS):
                vec.wait(act, BY_DVE.index(f"csb{h}") + 1)
                dexp.inc(nc.scalar.activation(dm[:, h % 2, :], dm[:, h % 2, :], ACT.Exp))
            for t in range(T):
                ysum.wait(act, t + 1)
                yss.inc(nc.scalar.activation(dm[:, t, :], yb[:, t, :], ACT.Square, scale=BW ** -0.5, accum_out=ss[:, 4 + t:5 + t]))
            for b in range(AB):
                job.wait(act, JOB[f"ybt{b}"])
                y_hi.inc(nc.scalar.activation(yhi[:, 3 + b, :], bank(f"ybt{b}", slice(0, S)), ACT.Copy))
            split_hi(act, place, range(C_OUT + 6, MIX_CHUNKS - 1 + 4))

        def mix_pool(pool):
            pool.wait_ge(par_loaded, mixround(1) * 16)
            w_s = par[:, PM["w_s"]].rearrange("p (g n) -> p g n", g=4)
            wst.inc(nc.gpsimd.tensor_tensor(w_s, w_s, upper[:, 0:P].unsqueeze(1).broadcast_to([P, 4, P]), ALU.mult))
            for given, between, done, at in ((vss, vms, vrstd, 2), (yss, yms, yrstd, 4)):
                for t in range(T):
                    given.wait(pool, t + 1)
                    between.inc(nc.gpsimd.tensor_tensor(ms[:, at + t:at + t + 1], ss[:, at + t:at + t + 1], small[:, 1:2], ALU.add))
                    between.wait(pool, t + 1)
                    done.inc(nc.gpsimd.tensor_tensor(rstd[:, at + t:at + t + 1], ms[:, at + t:at + t + 1], small[:, 0:1], ALU.pow))

        def mix_dve(dve, place):
            def step(ins):
                vstep.inc(ins)
                vstep.wait(dve, vstep.k)

            def conv(out_, pad, w, b, done):
                step(nc.vector.tensor_scalar(out_, pad[:, 0:S], w[:, 0:1], b, ALU.mult, ALU.add))
                for j in range(1, 4):
                    ins = nc.vector.scalar_tensor_tensor(out=out_, in0=pad[:, j:j + S], scalar=w[:, j:j + 1], in1=out_, op0=ALU.mult, op1=ALU.add)
                    if j < 3:
                        step(ins)
                    else:
                        done.inc(ins)

            def emptied(name, ins):
                vec.inc(ins)
                assert BY_DVE[vec.k - 1] == name, name

            dve.wait_ge(par_loaded, mixround(1) * 16)
            split_lo(dve, place, [3, 4, 5])
            for b in range(AB):
                evac.wait(dve, BY_ACT.index(f"rec{b}") + 1)
                conv(recc[:, b, :], recpad[:, b, :], par[:, PM["rec_w"]][:, 4 * b:4 * b + 4], par[:, PM["rec_b"]][:, b:b + 1], rec_conv)
                split_lo(dve, place, [C_REC + b + 6])
            for b in range(XB):
                evac.wait(dve, BY_ACT.index(f"xbc{b}") + 1)
                conv(xbcc[:, b, :], xbcpad[:, b, :], par[:, PM["xbc_w"]][:, 4 * b:4 * b + 4], par[:, PM["xbc_b"]][:, b:b + 1], xbc_conv)
                split_lo(dve, place, [C_XBC + b + 6])
            evac.wait(dve, BY_ACT.index("dt") + 1)
            nt = T * HEADS
            for t in range(T):
                step(nc.vector.tensor_tensor(spin[:, t * HEADS:(t + 1) * HEADS], dtraw[:, t, :], par[:, PM["dt_bias"]], ALU.add))
            spin_ready.inc(nc.vector.tensor_scalar(spin[:, nt:], par[:, PM["lam"]], -1.0, None, ALU.mult))
            split_lo(dve, place, [C_DT + 6])
            soft.wait(dve, 3)
            spin_ready.wait(dve, 1)
            step(nc.vector.scalar_tensor_tensor(out=sp_[:, :], in0=spin[:, :], scalar=0.0, in1=spe[:, :], op0=ALU.max, op1=ALU.add))
            step(nc.vector.tensor_scalar(psp[:, 0, :], sp_[:, nt:], 8.0, None, ALU.mult))
            psp_ready.inc(nc.vector.tensor_scalar(psp[:, 1, :], sp_[:, nt:], -8.0, None, ALU.mult))
            ea_ready.wait(dve, 1)
            for t in range(T):
                ins = nc.vector.scalar_tensor_tensor(out=ad[:, t, :], in0=sp_[:, t * HEADS:(t + 1) * HEADS], scalar=-1.0, in1=ea[:, :], op0=ALU.mult, op1=ALU.mult)
                if t == 0:
                    step(ins)
                else:
                    ad_ready.inc(ins)
            split_lo(dve, place, [C_GATE0 + 6])
            for t in range(T):
                evac.wait(dve, BY_ACT.index(f"uv{t}") + 1)
                step(nc.vector.tensor_reduce(lnm[:, 0, t:t + 1], uv[:, t, CW:], AX.X, ALU.add))
                step(nc.vector.tensor_scalar(lnm[:, 1, t:t + 1], lnm[:, 0, t:t + 1], -1.0 / CW, None, ALU.mult))
                vcen.inc(nc.vector.tensor_scalar(vx[:, t, :], uv[:, t, CW:], lnm[:, 1, t:t + 1], None, ALU.add))
            split_lo(dve, place, range(C_UV + 6, C_UV + 10))
            split_lo(dve, place, [C_GATE1 + 6, C_GATE1 + 7])
            a_ready.wait(dve, AB)
            th_ready.wait(dve, AB)
            step(nc.vector.tensor_tensor(ig[:, :, :], ig[:, :, :], recc[:, :, :], ALU.mult))
            step(nc.vector.tensor_tensor(rg[:, :, :], aa[:, :, :], aa[:, :, :], ALU.mult))
            mult2.inc(nc.vector.scalar_tensor_tensor(out=th[:, :, :], in0=rg[:, :, :], scalar=1.0, in1=th[:, :, :], op0=ALU.add, op1=ALU.mult))
            for t in range(T):
                vrstd.wait(dve, t + 1)
                step(nc.vector.scalar_tensor_tensor(out=vx[:, t, :], in0=vx[:, t, :], scalar=rstd[:, 2 + t:3 + t], in1=par[:, PM["ln_g"]], op0=ALU.mult, op1=ALU.mult))
                vln.inc(nc.vector.tensor_tensor(vx[:, t, :], vx[:, t, :], par[:, PM["ln_b"]], ALU.add))
            for t in range(T):
                job.wait(dve, JOB[f"xtok{t}"])
                emptied(f"xtok{t}", nc.vector.tensor_copy(xtok[:, t, :], bank(f"xtok{t}", slice(0, BW))))
            job.wait(dve, JOB["cs"])
            emptied("cs", nc.vector.tensor_scalar(ncs[:, :, :], bank("cs", slice(0, 16)).rearrange("p (t h) -> p t h", t=T)[:, :, 0:HEADS], -1.0, None, ALU.mult))
            mult_ready.wait(dve, 1)
            step(nc.vector.tensor_tensor(th[:, :, :], th[:, :, :], ig[:, :, :], ALU.mult))
            for b in range(AB):
                step(nc.vector.tensor_tensor_scan(rg[:, b, :], aa[:, b, :], th[:, b, :], 0.0, ALU.mult, ALU.add))
            evac.wait(dve, BY_ACT.index("gate2") + 1)
            ya32.inc(nc.vector.tensor_tensor(rg[:, :, :], rg[:, :, :], gateT[:, :, :], ALU.mult))
            for t in range(T):
                job.wait(dve, JOB[f"sgu{t}"])
                emptied(f"sgu{t}", nc.vector.tensor_tensor(yc[:, t, :].rearrange("p (g n) -> p g n", g=4), bank(f"sgu{t}", slice(0, CW)).rearrange("p (g n) -> p g n", g=4),
                                                           bc(par[:, PM["b_s"]], HD), ALU.add))
                vec.wait(dve, vec.k)
                yc_ready.inc(nc.vector.tensor_tensor(yc[:, t, :], yc[:, t, :], uv[:, t, 0:CW], ALU.mult))
            for i in range(2):
                y_hi.wait(dve, 1 + i)
                y_lo.inc(nc.vector.tensor_tensor(ylo[:, 6 + i, :], bank(f"yct{i}", slice(0, S)), yhi[:, 6 + i, :].bitcast(F32), ALU.subtract))
            y_hi.wait(dve, 3)
            ya32.wait(dve, 1)
            y_lo.inc(nc.vector.tensor_tensor(ylo[:, 0:AB, :], rg[:, :, :], yhi[:, 0:AB, :].bitcast(F32), ALU.subtract))
            for t in range(T):
                step(nc.vector.tensor_tensor(yb[:, t, :].rearrange("p (h n) -> p h n", h=HEADS), xtok[:, t, :].rearrange("p (h n) -> p h n", h=HEADS),
                                             bc(par[:, PM["d_skip"]], HD), ALU.mult))

            def exponent(h):
                job.wait(dve, JOB[f"csb{h}"])
                if h >= 2:
                    m_ready.wait(dve, h - 1)
                o = dm[:, h % 2]
                vec.wait(dve, BY_DVE.index("cs") + 1)
                step(nc.vector.scalar_tensor_tensor(out=o[:, 0:S], in0=bank(f"csb{h}", slice(0, S)), scalar=ncs[:, 0, h:h + 1], in1=maskadd[:, :], op0=ALU.add, op1=ALU.add))
                emptied(f"csb{h}", nc.vector.scalar_tensor_tensor(out=o[:, S:384], in0=bank(f"csb{h}", slice(P, S)), scalar=ncs[:, 1, h:h + 1], in1=maskadd[:, 0:P], op0=ALU.add, op1=ALU.add))

            exponent(0)
            for h in range(HEADS):
                if h + 1 < HEADS:
                    exponent(h + 1)
                dexp.wait(dve, h + 1)
                if h >= 2:
                    job.wait(dve, JOB[f"y{h - 2}"])
                cb = acc[:, 1, (h // 3) * 512:(h // 3) * 512 + 384]
                step(nc.vector.scalar_tensor_tensor(out=mm[:, h % 2, 0:S], in0=dm[:, h % 2, 0:S], scalar=sp_[:, h:h + 1], in1=cb[:, 0:S], op0=ALU.mult, op1=ALU.mult))
                m_ready.inc(nc.vector.scalar_tensor_tensor(out=mm[:, h % 2, S:384], in0=dm[:, h % 2, S:384], scalar=sp_[:, HEADS + h:HEADS + h + 1], in1=cb[:, S:384], op0=ALU.mult, op1=ALU.mult))
            job.wait(dve, JOB[f"y{HEADS - 1}"])
            evac.wait(dve, BY_ACT.index("z1") + 1)
            for t in range(T):
                step(nc.vector.tensor_tensor(yb[:, t, :], yb[:, t, :], acc[:, 0, t * 512:t * 512 + BW], ALU.add))
                ysum.inc(nc.vector.tensor_tensor(yb[:, t, :], yb[:, t, :], zs[:, t, :], ALU.mult))
            for t in range(T):
                yrstd.wait(dve, t + 1)
                ybn.inc(nc.vector.scalar_tensor_tensor(out=yb[:, t, :], in0=yb[:, t, :], scalar=rstd[:, 4 + t:5 + t], in1=par[:, PM["norm_g"]], op0=ALU.mult, op1=ALU.mult))
            split_lo(dve, place, range(C_Z + 6, C_Z + 9))
            for b in range(AB):
                y_hi.wait(dve, 4 + b)
                y_lo.inc(nc.vector.tensor_tensor(ylo[:, 3 + b, :], bank(f"ybt{b}", slice(0, S)), yhi[:, 3 + b, :].bitcast(F32), ALU.subtract))
            split_lo(dve, place, range(C_OUT + 6, MIX_CHUNKS - 1 + 2))

        def bank2(name, cols=slice(0, 512)):
            return W[BANK2[name]][:, cols]

        def begin2(pe, name):
            i = BANKED2.index(name)
            if i >= 4:
                before = BANKED2[i - 4]
                if before in BY_ACT2:
                    evac2.wait(pe, BY_ACT2.index(before) + 1)
                else:
                    vec2.wait(pe, BY_DVE2.index(before) + 1)

        def nkeys(t):
            return (t + 1) * P

        def mix2_pe(pe, q, place):
            def done(name, ins):
                job2.inc(ins)
                assert JOBS2[job2.k - 1] == name, (name, JOBS2[job2.k - 1])

            def channels(name, c):
                begin2(pe, name)
                pe.wait_ge(lo_ready, place.count(c))
                hi, lo = chunk(whi, place, c), chunk(wlo, place, c)
                for k in range(KD):
                    m = product(bank2(name, slice(0, S)), hi[:, k * P:(k + 1) * P], lo[:, k * P:(k + 1) * P],
                                xhi[:, k, :], xlo[:, k, :], k == 0, k == KD - 1)
                m[-1].then_inc(consumed, 1)

            def tokens(name, t, c, n, at=0):
                chunks = -(-KD * n // CH)
                pe.wait_ge(lo_ready, place.count(c + chunks - 1))
                hi, lo = chunk(whi, place, c, chunks), chunk(wlo, place, c, chunks)
                recent = []
                for k in range(KD):
                    recent += product(bank2(name, slice(at, at + n)), xhi[:, k, t * P:(t + 1) * P], xlo[:, k, t * P:(t + 1) * P],
                                      hi[:, k * n:(k + 1) * n], lo[:, k * n:(k + 1) * n], k == 0, k == KD - 1)
                return recent[-4:]

            def release(matmuls, n):
                for m in matmuls[-n:]:
                    m.then_inc(consumed, 1)

            pe.wait_ge(xlo_ready, q * 8 + 8)
            begin2(pe, "q0")
            done("q0", tokens("q0", 0, D_Q, 512)[-1])
            begin2(pe, "q1")
            release(tokens("q1", 1, D_Q, 512), 4)
            for i in range(4):
                channels(f"kvc{i}", D_KVC + i)
            begin2(pe, "ng")
            tokens("ng", 0, D_NG, 24)
            release(tokens("ng", 1, D_NG, 24, at=24), 1)
            for b in range(3):
                channels(f"u{b}", D_U + b)
            begin2(pe, "kv0")
            done("kv0", tokens("kv0", 0, D_KV, 512)[-1])
            begin2(pe, "kv1")
            release(tokens("kv1", 1, D_KV, 512), 4)
            channels("u3", D_U3)
            for w in range(2):
                begin2(pe, f"hid{w}")
                xc_ready.wait(pe, w + 1)
                for j in range(16):
                    c = D_W1 + 4 * w + j // 4
                    pe.wait_ge(lo_ready, place.count(c))
                    at = slice(j % 4 * S, (j % 4 + 1) * S)
                    m = product(bank2(f"hid{w}", slice(0, S))[0:16], xchi[:, w, j, :], xclo[:, w, j, :], chunk(whi, place, c)[:, at], chunk(wlo, place, c)[:, at], j == 0, j == 15)[-1]
                    if j % 4 == 3:
                        m.then_inc(consumed, 1)
            def early(*js):
                for j in js:
                    channels(f"e{j}", D_EARLY + j)

            early(0, 1)
            for w in range(2):
                begin2(pe, f"hidt{w}")
                evac2.wait(pe, BY_ACT2.index(f"hid{w}") + 1)
                for b in range(2):
                    m = nc.tensor.transpose(bank2(f"hidt{w}", slice(b * 16, b * 16 + 16)), hid[0:16, w, b * P:(b + 1) * P], ident[0:16, 0:16])
                done(f"hidt{w}", m)
            early(2)
            for w in range(2):
                begin2(pe, f"cmp{w}")
                evac2.wait(pe, BY_ACT2.index(f"hidt{w}") + 1)
                for b in range(2):
                    m = nc.tensor.matmul(bank2(f"cmp{w}", slice(0, HD))[0:16], hidT[:, w, b, :], par[:, PN["w2"]][:, (2 * w + b) * HD:(2 * w + b + 1) * HD],
                                         start=b == 0, stop=b == 1)
                done(f"cmp{w}", m)
            early(3)
            qn_ready.wait(pe, T)
            for t in range(T):
                for b in range(2):
                    name = f"qt{t}{b}"
                    begin2(pe, name)
                    for a in range(4):
                        h = 4 * b + a
                        m = nc.tensor.transpose(bank2(name, slice(a * P, (a + 1) * P))[0:HD], xn[:, t, h * HD:(h + 1) * HD], ident[:, :])
                    done(name, m)
            for t in range(T):
                name = f"kt{t}"
                begin2(pe, name)
                for a in range(4):
                    m = nc.tensor.transpose(bank2(name, slice(a * P, (a + 1) * P))[0:HD], xn[:, t, 512 + a * HD:512 + (a + 1) * HD], ident[:, :])
                done(name, m)
            early(4)
            begin2(pe, "kct")
            kcn_ready.wait(pe, 1)
            done("kct", nc.tensor.transpose(bank2("kct", slice(0, 16))[0:HD], kcn[0:16, :], ident[0:16, 0:16]))
            early(5, 6)
            evac2.wait(pe, BY_ACT2.index("kct") + 1)
            for t in range(T):
                begin2(pe, f"cs{t}")
                for h in range(8):
                    m = nc.tensor.matmul(bank2(f"cs{t}", slice(h * 8, h * 8 + 8)), qT[:, h, t * P:(t + 1) * P], kcT[:, (h // 4) * 8:(h // 4) * 8 + 8], start=True, stop=True)
                done(f"cs{t}", m)
            early(7)
            uhl_ready.wait(pe, 4)
            wc_ready.wait(pe, 1)

            def scores(r):
                h, t = r // 2, r % 2
                begin2(pe, f"sc{r}")
                for b in range(2):
                    m = nc.tensor.matmul(bank2(f"sc{r}", slice(b * S, b * S + nkeys(t))), qT[:, h, t * P:(t + 1) * P], kT[:, 2 * b + h // 4, 0:nkeys(t)], start=True, stop=True)
                done(f"sc{r}", m)

            def states_in(r):
                c = D_B[r // 4]
                begin2(pe, f"bu{r}")
                pe.wait_ge(lo_ready, place.count(c))
                for i in range(2):
                    at = slice((r % 4 * 2 + i) * P, (r % 4 * 2 + i + 1) * P)
                    m = product(bank2(f"bu{r}", slice(i * S, (i + 1) * S)), chunk(whi, place, c)[:, at], chunk(wlo, place, c)[:, at],
                                y5hi[:, r // 4, :], y5lo[:, r // 4, :], True, True)
                if r % 4 == 3:
                    m[-1].then_inc(consumed, 1)
                else:
                    done(f"bu{r}", m[-1])

            def states_out(r):
                rot_ready.wait(pe, r + 1)
                k, at = r // 4, 32 * (r % 4)
                o = acc[at:at + 32, 1, (k % 2) * S:(k % 2 + 1) * S]
                if r % 4 == 0 and r:
                    y5sum.wait(pe, k)
                w = [par[:, PN["c"]][:, (2 * r + i) * 32:(2 * r + i + 1) * 32] for i in range(2)]
                terms = [(w[0], q1[:, 0, :]), (w[1], q1[:, 1, :]), (w[1], q2[:, 0, :]), (w[0], q2[:, 1, :])]
                for i, (lh, rh) in enumerate(terms):
                    m = nc.tensor.matmul(o, lh, rh, start=i == 0, stop=i == 3)
                done(f"y5{r}", m)

            def turn(r):
                t = r % 2
                begin2(pe, f"pt{r}")
                if r:
                    evac2.wait(pe, BY_ACT2.index(f"pt{r - 1}") + 1)
                pscaled.wait(pe, r + 1)
                for b in range(2):
                    for k in range(t + 1):
                        nc.tensor.transpose(bank2(f"pt{r}", slice((b * 2 + k) * P, (b * 2 + k + 1) * P)), sm[:, r % 2, b, k * P:(k + 1) * P], ident[:, :])
                if r < T:
                    pc_ready.wait(pe, r + 1)
                done(f"pt{r}", nc.tensor.transpose(acc[0:16, 1, 512 + (r % 4) * P:512 + (r % 4 + 1) * P], pc[:, t, r // 2, :], ident[:, :]))

            def values(r):
                h, t = r // 2, r % 2
                o = acc[:, 0, t * 512 + h * HD:t * 512 + (h + 1) * HD]
                evac2.wait(pe, BY_ACT2.index(f"pt{r}") + 1)
                nc.tensor.matmul(o, pcT[:, r % 2, :], vcs[:, :], start=True, stop=False)
                for b in range(2):
                    for k in range(t + 1):
                        m = nc.tensor.matmul(o, pT[:, r % 2, (b * 2 + k) * P:(b * 2 + k + 1) * P], xn[:, k, 768 + b * P + (h // 4) * HD:768 + b * P + (h // 4 + 1) * HD],
                                             start=False, stop=b == 1 and k == t)
                done(f"pv{r}", m)

            for r in range(17):
                if r < 16:
                    scores(r)
                    states_in(r)
                if r >= 1:
                    states_out(r - 1)
                    turn(r - 1)
                if r < 12:
                    channels(f"cv{r}", D_CONV[r])
                if r >= 1:
                    values(r - 1)
            otok_ready.wait(pe, T)
            for b in range(4):
                begin2(pe, f"ot{b}")
                for t in range(T):
                    m = nc.tensor.transpose(bank2(f"ot{b}", slice(t * P, (t + 1) * P)), otok[:, t, b * P:(b + 1) * P], ident[:, :])
                done(f"ot{b}", m)
            for i in range(KD):
                for b in range(3):
                    if (i, b) not in EARLY:
                        channels(f"g{i}{b}", LATE[f"g{i}{b}"])
                for name, c, left, right in ((f"lin{i}", LATE[f"lin{i}"], (y5hi, y5lo), (y5hi, y5lo)), (f"br{i}", LATE[f"br{i}"], (cvhi, cvlo), (ohi, olo))):
                    begin2(pe, name)
                    pe.wait_ge(lo_ready, place.count(c))
                    if i == 0:
                        y5_split.wait(pe, 4)
                        cv_split.wait(pe, 4)
                        vec2.wait(pe, BY_DVE2.index("ot3") + 1)
                    for half, (rh, rl) in enumerate((left, right)):
                        for k in range(4):
                            at = slice((half * 4 + k) * P, (half * 4 + k + 1) * P)
                            m = product(bank2(name, slice(half * S, (half + 1) * S)), chunk(whi, place, c)[:, at], chunk(wlo, place, c)[:, at],
                                        rh[:, k, :], rl[:, k, :], k == 0, k == 3)[-1]
                    m.then_inc(consumed, 1)
            for k in range(KD - 2):
                c = D_OUT + k
                pe.wait_ge(lo_ready, place.count(c))
                mix_lo.wait(pe, k + 1)
                hi, lo = chunk(whi, place, c), chunk(wlo, place, c)
                for t in range(T):
                    for h in range(2):
                        cols = slice(h * 512, (h + 1) * 512)
                        m = product(acc[:, t, cols], mxhi[:, k, t * P:(t + 1) * P], mxlo[:, k, t * P:(t + 1) * P],
                                    hi[:, cols], lo[:, cols], k == 0, False)[-1]
                m.then_inc(consumed, 1)
            last_two(pe, place, [D_OUT + KD - 2, D_OUT + KD - 1],
                     lambda n, t: (mxhi[:, KD - 2 + n, t * P:(t + 1) * P], mxlo[:, KD - 2 + n, t * P:(t + 1) * P]),
                     lambda n: mix_lo.wait(pe, KD - 1 + n))

        def mix2_act(act, place):
            def emptied(name, ins):
                evac2.inc(ins)
                assert BY_ACT2[evac2.k - 1] == name, (name, BY_ACT2[evac2.k - 1])

            def projected(c):
                act.wait_ge(consumed, place.count(c) + RING)

            def copy(name, o, i):
                emptied(name, nc.scalar.activation(o, i, ACT.Copy))

            split_hi(act, place, [4, 5])
            act.wait_ge(par_loaded, 3 * 16)
            s5a.inc(nc.scalar.activation(s5p[:, 0, :], par[:, PN["ldt"]], ACT.Exp))
            s5v.wait(act, 2)
            s5a.inc(nc.scalar.activation(s5p[:, 3, :], s5p[:, 1, :], ACT.Exp))
            s5v.wait(act, 3)
            s5a.inc(nc.scalar.activation(s5p[:, 4, :], s5p[:, 2, :], ACT.Sin, scale=TWO_PI))
            s5a.inc(nc.scalar.activation(s5p[:, 5, :], s5p[:, 2, :], ACT.Sin, scale=TWO_PI / 2))

            def turns(g):
                if g:
                    tab.wait(act, 4 * g - 1)
                for i in range(2):
                    tab_k.inc(nc.scalar.activation(frac[:, i, :], tokens_f[:, :], ACT.Identity, scale=s5p[:, 2, 2 * g + i:2 * g + i + 1], bias=magic[:, 0:1]))
                tab_k.wait(act, 4 * g + 2)
                for i in range(2):
                    tab_k.inc(nc.scalar.activation(frac[:, i, :], frac[:, i, :], ACT.Identity, bias=magic[:, 1:2]))

            def tables(g):
                o = table[g % 2]
                if g == 1:
                    wc_ready.wait(act, 1)
                frac_ready.wait(act, g + 1)
                if g >= 2:
                    rot_ready.wait(act, 2 * g - 2)
                tab.inc(nc.scalar.activation(o[:, :, 1, :], frac[:, :, :], ACT.Sin, scale=TWO_PI))
                tab.inc(nc.scalar.activation(o[:, :, 2, :], frac[:, :, :], ACT.Sin, scale=-TWO_PI))
                tab.inc(nc.scalar.activation(o[:, :, 0, :], frac[:, :, :], ACT.Sin, scale=TWO_PI / 2))
                tab.wait(act, 4 * g + 3)
                tab.inc(nc.scalar.activation(o[:, :, 0, :], o[:, :, 0, :], ACT.Square))

            turns(0)
            tables(0)
            job2.wait(act, JOB2["q0"])
            copy("q0", xn[:, 0, 0:512], bank2("q0"))
            projected(D_Q + 3)
            copy("q1", xn[:, 1, 0:512], bank2("q1"))
            split_hi(act, place, range(6, 10))
            for i in range(4):
                w, h = i // 2, i % 2
                projected(D_KVC + i)
                for p in range(2):
                    rows = slice(p * HD, (p + 1) * HD)
                    src = bank2(f"kvc{i}", slice(0, S))[rows].rearrange("d (b j p) -> d j b p", b=8, p=2)[:, :, :, p]
                    ins = nc.scalar.activation(xc[rows, w, :, h * 8:h * 8 + 8], src, ACT.Copy)
                emptied(f"kvc{i}", ins)
                split_hi(act, place, [10 + i])
            projected(D_NG)
            emptied("ng", nc.scalar.activation(ngate[:, :], bank2("ng", slice(0, 48)), ACT.Sigmoid))
            split_hi(act, place, [14])
            for b in range(3):
                projected(D_U + b)
                copy(f"u{b}", uT[:, b, :], bank2(f"u{b}", slice(0, S)))
                split_hi(act, place, [15 + b])
            for w in range(2):
                xc32.wait(act, w + 1)
                xcs.inc(nc.scalar.activation(xchi[:, w], xc[:, w], ACT.Copy))
            job2.wait(act, JOB2["kv0"])
            copy("kv0", xn[:, 0, 512:], bank2("kv0"))
            projected(D_KV + 3)
            copy("kv1", xn[:, 1, 512:], bank2("kv1"))
            split_hi(act, place, range(18, 22))
            projected(D_U3)
            copy("u3", uT[:, 3, :], bank2("u3", slice(0, S)))
            split_hi(act, place, [22])
            evac2.wait(act, evac2.k)
            for b in range(4):
                ucopy.inc(nc.scalar.activation(y5hi[:, b, :], uT[:, b, :], ACT.Copy))
            for w in range(2):
                projected(D_W1 + 4 * w + 3)
                emptied(f"hid{w}", nc.scalar.activation(hid[0:16, w, :], bank2(f"hid{w}", slice(0, S))[0:16], ACT.Gelu_apprx_tanh))
                split_hi(act, place, range(D_W1 + 6 + 4 * w, D_W1 + 10 + 4 * w))
            def early(*js):
                for j in js:
                    projected(D_EARLY + j)
                    copy(f"e{j}", gates32[j], bank2(f"e{j}", slice(0, S)))
                    split_hi(act, place, [D_EARLY + j + 6])

            early(0, 1)
            for w in range(2):
                job2.wait(act, JOB2[f"hidt{w}"])
                copy(f"hidt{w}", hidT[:, w], bank2(f"hidt{w}", slice(0, 32)).rearrange("p (b n) -> p b n", b=2))
            early(2)
            for w in range(2):
                job2.wait(act, JOB2[f"cmp{w}"])
                copy(f"cmp{w}", kcn[0:16, :] if w == 0 else vcs[0:16, :], bank2(f"cmp{w}", slice(0, HD))[0:16])
            early(3)
            for t in range(T):
                for b in range(2):
                    job2.wait(act, JOB2[f"qt{t}{b}"])
                    copy(f"qt{t}{b}", qT[:, 4 * b:4 * b + 4, t * P:(t + 1) * P], bank2(f"qt{t}{b}")[0:HD].rearrange("p (a n) -> p a n", a=4))
            for t in range(T):
                job2.wait(act, JOB2[f"kt{t}"])
                copy(f"kt{t}", kT[:, :, t * P:(t + 1) * P], bank2(f"kt{t}")[0:HD].rearrange("p (a n) -> p a n", a=4))
            early(4)
            job2.wait(act, JOB2["kct"])
            copy("kct", kcT[:, :], bank2("kct", slice(0, 16))[0:HD])
            early(5, 6)
            for t in range(T):
                csm.wait(act, t + 1)
                cexp.inc(nc.scalar.activation(ce[:, t], ce[:, t], ACT.Exp))

            early(7)
            for r in range(17):
                if r >= 1:
                    p = r - 1
                    job2.wait(act, JOB2[f"pt{p}"])
                    if p >= 2:
                        job2.wait(act, JOB2[f"pv{p - 2}"])
                    nb = p % 2 + 1
                    src = bank2(f"pt{p}").rearrange("p (b n) -> p b n", b=2)[:, :, 0:nb * P]
                    dst = pT[:, p % 2, :].rearrange("p (b n) -> p b n", b=2)[:, :, 0:nb * P]
                    nc.scalar.activation(pcT[:, p % 2, :], acc[0:16, 1, 512 + (p % 4) * P:512 + (p % 4 + 1) * P], ACT.Copy)
                    copy(f"pt{p}", dst, src)
                if r < 16:
                    smax.wait(act, r + 1)
                    for b in range(2):
                        sexp.inc(nc.scalar.activation(sm[:, r % 2, b, 0:nkeys(r % 2)], sm[:, r % 2, b, 0:nkeys(r % 2)], ACT.Exp,
                                                      bias=nm[:, r % 2, b:b + 1], accum_out=rs[:, r % 2, b:b + 1]))
                if r < 14:
                    if r % 2 == 0:
                        turns(r // 2 + 1)
                    else:
                        tables(r // 2 + 1)
                if r < 12:
                    projected(D_CONV[r])
                    if r % 3 == 0:
                        if r:
                            cz.wait(act, r // 3)
                        copy(f"cv{r}", cc[:, :], bank2(f"cv{r}", slice(0, S)))
                    elif r % 3 == 2:
                        if r > 2:
                            cv32.wait(act, r // 3)
                        copy(f"cv{r}", cb[:, :], bank2(f"cv{r}", slice(0, S)))
                if r in SPLIT_AFTER:
                    split_hi(act, place, SPLIT_AFTER[r])
                if r < 12 and r % 3 == 2:
                    cv32.wait(act, r // 3 + 1)
                    cv_hi.inc(nc.scalar.activation(cvhi[:, r // 3, :], cvt[:, :], ACT.Copy))
                if r >= 4 and r % 4 == 0:
                    y5sum.wait(act, r // 4)
                    y5g.inc(nc.scalar.activation(y5t[:, :], y5t[:, :], ACT.Gelu_apprx_tanh))
                    y5g.wait(act, r // 4)
                    y5_hi.inc(nc.scalar.activation(y5hi[:, r // 4 - 1, :], y5t[:, :], ACT.Copy))
            for b in range(4):
                job2.wait(act, JOB2[f"ot{b}"])
                o_hi.inc(nc.scalar.activation(ohi[:, b, :], bank2(f"ot{b}", slice(0, S)), ACT.Copy))

            def mixed_high(i):
                mix32.wait(act, i + 1)
                mix_hi.inc(nc.scalar.activation(mxhi[:, i, :], mt[:, 0, :], ACT.Copy))

            for i in range(KD):
                for b in range(3):
                    if i >= 2 and b == 0:
                        mix_lo.wait(act, i - 1)
                    if (i, b) in EARLY:
                        early_gate.inc(nc.scalar.activation(gsg[:, i % 2, b, :], gates32[EARLY.index((i, b))], ACT.Sigmoid))
                    else:
                        c = LATE[f"g{i}{b}"]
                        projected(c)
                        emptied(f"g{i}{b}", nc.scalar.activation(gsg[:, i % 2, b, :], bank2(f"g{i}{b}", slice(0, S)), ACT.Sigmoid))
                        split_hi(act, place, [c + 6])
                if i:
                    mixed_high(i - 1)
                c = LATE[f"lin{i}"]
                projected(c)
                sgl_ready.inc(nc.scalar.activation(sgl[:, i % 2, :], bank2(f"lin{i}", slice(S, 2 * S)), ACT.Sigmoid))
                split_hi(act, place, [c + 6])
                projected(c + 1)
                split_hi(act, place, [c + 7])
            mixed_high(KD - 1)
            split_hi(act, place, range(D_OUT + 6, MIX2_CHUNKS + 4))

        def mix2_pool(pool):
            s5m.wait(pool, 1)
            nrm.inc(nc.gpsimd.tensor_tensor(qk_rstd[:, :], qk_ms[:, :], halves[:, 0:24], ALU.pow))
            s5m.wait(pool, 2)
            nrm.inc(nc.gpsimd.tensor_tensor(kc_st[0:16, 1:2], kc_st[0:16, 0:1], halves[0:16, 0:1], ALU.pow))

            coef_ready.wait(pool, 1)

            def step(ins):
                pool_step.inc(ins)
                pool_step.wait(pool, pool_step.k)

            c4 = par[:, PN["c"]].rearrange("p (r i n) -> p r i n", r=16, i=2)
            cre, cim = c4[:, :, 0, :], c4[:, :, 1, :]
            flat = table[1].rearrange("p a b n -> p (a b n)")
            a3, b3, d3 = [flat[:, i * 512:(i + 1) * 512].rearrange("p (r n) -> p r n", r=16) for i in range(3)]
            tt = nc.gpsimd.tensor_tensor
            step(tt(a3, cre, bc(s5p[:, 7, :], 32), ALU.mult))
            step(tt(b3, cim, bc(s5p[:, 5, :], 32), ALU.mult))
            step(tt(a3, a3, b3, ALU.add))
            step(tt(b3, cre, bc(s5p[:, 5, :], 32), ALU.mult))
            step(tt(d3, cim, bc(s5p[:, 1, :], 32), ALU.mult))
            step(tt(cim, b3, d3, ALU.add))
            wc_ready.inc(nc.gpsimd.tensor_copy(cre, a3))
            for r in range(ROUNDS):
                cosr = table[r // 2 % 2][:, r % 2, 0, :].unsqueeze(1).broadcast_to([P, 2, S])
                sins = table[r // 2 % 2][:, r % 2, 1:3, :]
                scanned.wait(pool, 2 * r + 2)
                if r >= 1:
                    job2.wait(pool, JOB2[f"y5{r - 1}"])
                nc.gpsimd.tensor_tensor(q1[:, :, :], g2[:, :, :], cosr, ALU.mult)
                rot_ready.inc(nc.gpsimd.tensor_tensor(q2[:, :, :], g2[:, :, :], sins, ALU.mult))

        def mix2_dve(dve, place):
            def step(ins):
                vstep2.inc(ins)
                vstep2.wait(dve, vstep2.k)

            def emptied(name, ins):
                vec2.inc(ins)
                assert BY_DVE2[vec2.k - 1] == name, (name, BY_DVE2[vec2.k - 1])

            tt, ts, stt = nc.vector.tensor_tensor, nc.vector.tensor_scalar, nc.vector.scalar_tensor_tensor
            sp = lambda i: s5p[:, i, :]
            split_lo(dve, place, [4, 5])
            s5a.wait(dve, 1)
            s5v.inc(tt(sp(6), par[:, PN["lim"]], sp(0), ALU.mult))
            s5v.inc(tt(sp(1), par[:, PN["lre"]], sp(0), ALU.mult))
            s5v.wait(dve, 2)
            step(ts(sp(7), sp(6), 1.0 / TWO_PI_EXACT, MAGIC, ALU.mult, ALU.add))
            step(ts(sp(7), sp(7), MAGIC, None, ALU.subtract))
            for part in TWO_PI_PARTS:
                step(stt(out=sp(6), in0=sp(7), scalar=-part, in1=sp(6), op0=ALU.mult, op1=ALU.add))
            step(ts(sp(2), sp(6), 1.0 / TWO_PI_EXACT, 0.5, ALU.mult, ALU.min))
            s5v.inc(ts(sp(2), sp(2), -0.5, None, ALU.max))

            def fraction(g):
                for i in range(2):
                    tab_k.wait(dve, 4 * g + 4)
                    step(stt(out=frac[:, i, :], in0=tokens_f[:, :], scalar=s5p[:, 2, 2 * g + i:2 * g + i + 1], in1=frac[:, i, :], op0=ALU.mult, op1=ALU.subtract))
                frac_ready.inc(ts(frac[:, :, :], frac[:, :, :], 0.5, -0.5, ALU.min, ALU.max))

            s5v.wait(dve, 3)
            fraction(0)
            split_lo(dve, place, range(6, 10))
            sq = otok
            for t in range(T):
                evac2.wait(dve, BY_ACT2.index(f"q{t}") + 1)
                step(tt(sq[:, t, :], xn[:, t, 0:512], xn[:, t, 0:512], ALU.mult))
                step(nc.vector.tensor_reduce(qk_ms[:, t * 12:t * 12 + 8], sq[:, t, :].rearrange("p (h n) -> p h n", h=8), AX.X, ALU.add))
            s5a.wait(dve, 4)
            step(tt(sp(5), sp(5), sp(5), ALU.mult))
            step(ts(sp(5), sp(5), -2.0, 1.0, ALU.mult, ALU.add))
            step(tt(sp(5), sp(5), sp(3), ALU.mult))
            step(ts(sp(5), sp(5), 1.0, None, ALU.subtract))
            step(tt(sp(4), sp(4), sp(3), ALU.mult))
            step(tt(sp(6), par[:, PN["lre"]], par[:, PN["lre"]], ALU.mult))
            step(tt(sp(7), par[:, PN["lim"]], par[:, PN["lim"]], ALU.mult))
            step(tt(sp(6), sp(6), sp(7), ALU.add))
            step(nc.vector.reciprocal(sp(6), sp(6)))
            step(tt(sp(7), sp(5), par[:, PN["lre"]], ALU.mult))
            step(tt(sp(0), sp(4), par[:, PN["lim"]], ALU.mult))
            step(tt(sp(7), sp(7), sp(0), ALU.add))
            step(tt(sp(7), sp(7), sp(6), ALU.mult))
            step(tt(sp(0), sp(4), par[:, PN["lre"]], ALU.mult))
            step(tt(sp(1), sp(5), par[:, PN["lim"]], ALU.mult))
            step(tt(sp(0), sp(0), sp(1), ALU.subtract))
            step(tt(sp(0), sp(0), sp(6), ALU.mult))
            step(ts(sp(5), sp(0), -1.0, None, ALU.mult))
            coef_ready.inc(ts(sp(1), sp(7), -1.0, None, ALU.mult))
            split_lo(dve, place, range(10, 14))
            split_lo(dve, place, [14])
            split_lo(dve, place, range(15, 18))
            for w in range(2):
                evac2.wait(dve, BY_ACT2.index(f"kvc{2 * w + 1}") + 1)
                xc32.inc(tt(xc[:, w], xc[:, w], bc(par[:, PN["pe"]][:, w * 16:(w + 1) * 16], 16), ALU.add))
            for w in range(2):
                xcs.wait(dve, w + 1)
                xc_ready.inc(tt(xclo[:, w], xc[:, w], xchi[:, w].bitcast(F32), ALU.subtract))
            for t in range(T):
                evac2.wait(dve, BY_ACT2.index(f"kv{t}") + 1)
                step(tt(sq[:, t, 0:S], xn[:, t, 512:768], xn[:, t, 512:768], ALU.mult))
                step(nc.vector.tensor_reduce(qk_ms[:, t * 12 + 8:t * 12 + 12], sq[:, t, 0:S].rearrange("p (h n) -> p h n", h=4), AX.X, ALU.add))
            s5m.inc(ts(qk_ms[:, :], qk_ms[:, :], 1.0 / HD, EPS, ALU.mult, ALU.add))
            split_lo(dve, place, range(18, 22))
            split_lo(dve, place, [22])
            for b in range(4):
                ucopy.wait(dve, b + 1)
                uhl_ready.inc(tt(y5lo[:, b, :], uT[:, b, :], y5hi[:, b, :].bitcast(F32), ALU.subtract))
            nrm.wait(dve, 1)
            for t in range(T):
                q3 = xn[:, t, 0:512].rearrange("p (h n) -> p h n", h=8)
                k3 = xn[:, t, 512:768].rearrange("p (h n) -> p h n", h=4)
                step(tt(q3, q3, bc(qk_rstd[:, t * 12:t * 12 + 8], HD), ALU.mult))
                step(stt(out=q3, in0=q3, scalar=HD ** -0.5, in1=par[:, PN["q_g"]].unsqueeze(1).broadcast_to([P, 8, HD]), op0=ALU.mult, op1=ALU.mult))
                step(tt(k3, k3, bc(qk_rstd[:, t * 12 + 8:t * 12 + 12], HD), ALU.mult))
                for b in range(2):
                    kb = k3[:, 2 * b:2 * b + 2, :]
                    ins = tt(kb, kb, par[:, PN["k_g"]][:, (b + 1) * HD:(b + 2) * HD].unsqueeze(1).broadcast_to([P, 2, HD]), ALU.mult)
                    if b == 0:
                        step(ins)
                    else:
                        qn_ready.inc(ins)
            split_lo(dve, place, range(D_W1 + 6, D_EARLY + 6))
            split_lo(dve, place, range(D_EARLY + 6, D_EARLY + 8))
            evac2.wait(dve, BY_ACT2.index("cmp1") + 1)
            step(tt(sq[0:16, 0, 0:HD], kcn[0:16, :], kcn[0:16, :], ALU.mult))
            step(nc.vector.tensor_reduce(kc_st[0:16, 0:1], sq[0:16, 0, 0:HD], AX.X, ALU.add))
            s5m.inc(ts(kc_st[0:16, 0:1], kc_st[0:16, 0:1], 1.0 / HD, EPS, ALU.mult, ALU.add))
            nrm.wait(dve, 2)
            kcn_ready.inc(stt(out=kcn[0:16, :], in0=kcn[0:16, :], scalar=kc_st[0:16, 1:2], in1=par[0:16, PN["k_g"]][:, 0:HD], op0=ALU.mult, op1=ALU.mult))
            split_lo(dve, place, range(D_EARLY + 8, D_EARLY + 13))
            for t in range(T):
                job2.wait(dve, JOB2[f"cs{t}"])
                c3 = ce[:, t]
                m3 = cmask[:, t, 0, :].unsqueeze(1).broadcast_to([P, 8, 8])
                o3 = cmask[:, t, 1, :].unsqueeze(1).broadcast_to([P, 8, 8])
                emptied(f"cs{t}", tt(c3, bank2(f"cs{t}", slice(0, 64)).rearrange("p (h n) -> p h n", h=8), m3, ALU.add))
                vec2.wait(dve, vec2.k)
                step(nc.vector.tensor_reduce(cst[:, 0:8], c3, AX.X, ALU.max))
                csm.inc(tt(c3, c3, bc(cst[:, 0:8], 8), ALU.subtract))
                cexp.wait(dve, t + 1)
                step(tt(c3, c3, o3, ALU.mult))
                step(nc.vector.tensor_reduce(cst[:, 0:8], c3, AX.X, ALU.add))
                step(ts(cst[:, 0:8], cst[:, 0:8], 1e-30, None, ALU.max))
                step(nc.vector.reciprocal(cst[:, 0:8], cst[:, 0:8]))
                step(tt(cst[:, 0:8], cst[:, 0:8], ngate[:, t * 24:(t + 1) * 24].rearrange("p (h n) -> p h n", n=3)[:, :, 0], ALU.mult))
                step(tt(pc[:, t, 0:4, 0:8], c3[:, 0:4, :], bc(cst[:, 0:4], 8), ALU.mult))
                pc_ready.inc(tt(pc[:, t, 4:8, 8:16], c3[:, 4:8, :], bc(cst[:, 4:8], 8), ALU.mult))

            def s5_sum(k):
                job2.wait(dve, JOB2[f"y5{4 * k + 3}"])
                y5sum.inc(stt(out=y5t[:, :], in0=uT[:, k, :], scalar=par[:, PN["ssm_d"]][:, k:k + 1], in1=acc[:, 1, (k % 2) * S:(k % 2 + 1) * S], op0=ALU.mult, op1=ALU.add))

            def s5_low(k):
                y5_hi.wait(dve, k + 1)
                y5_split.inc(tt(y5lo[:, k, :], y5t[:, :], y5hi[:, k, :].bitcast(F32), ALU.subtract))

            def cosines(g):
                tab.wait(dve, 4 * g + 4)
                step(ts(table[g % 2][:, :, 0, :], table[g % 2][:, :, 0, :], -2.0, 1.0, ALU.mult, ALU.add))

            split_lo(dve, place, [D_EARLY + 13])
            cosines(0)
            for r in range(16):
                h, t = r // 2, r % 2
                nk = nkeys(t)
                job2.wait(dve, JOB2[f"sc{r}"])
                if r >= 2:
                    job2.wait(dve, JOB2[f"pt{r - 2}"])
                s3 = sm[:, t, :, 0:nk]
                emptied(f"sc{r}", tt(s3, bank2(f"sc{r}").rearrange("p (b n) -> p b n", b=2)[:, :, 0:nk],
                                     qmask[:, S - nk:S].unsqueeze(1).broadcast_to([P, 2, nk]), ALU.add))
                vec2.wait(dve, vec2.k)
                smax.inc(nc.vector.tensor_reduce(nm[:, t, :], s3, AX.X, ALU.max, negate=True))
                cosr = table[r // 2 % 2][:, t, 0, :].unsqueeze(1).broadcast_to([P, 2, S])
                sins = table[r // 2 % 2][:, t, 1:3, :]
                if r % 4 == 3:
                    dve.wait_ge(consumed, place.count(D_B[r // 4]) + RING)
                else:
                    job2.wait(dve, JOB2[f"bu{r}"])
                b3 = bank2(f"bu{r}").rearrange("p (b n) -> p b n", b=2)
                step(tt(sg[:, :, :], b3, cosr, ALU.mult))
                emptied(f"bu{r}", tt(h32[:, :, :], b3, sins, ALU.mult))
                vec2.wait(dve, vec2.k)
                step(tt(v2[:, 0, :], sg[:, 0, :], h32[:, 1, :], ALU.subtract))
                step(tt(v2[:, 1, :], sg[:, 1, :], h32[:, 0, :], ALU.subtract))
                if r:
                    rot_ready.wait(dve, r)
                for i in range(2):
                    scanned.inc(nc.vector.tensor_tensor_scan(g2[:, i, :], s5p[:, 3, r:r + 1].broadcast_to([P, S]), v2[:, i, :], 0.0, ALU.mult, ALU.add))
                if r % 4 == 0 and r:
                    s5_sum(r // 4 - 1)
                sexp.wait(dve, 2 * r + 2)
                step(ts(rs[:, t, :], rs[:, t, :], 1e-30, None, ALU.max))
                step(nc.vector.reciprocal(rs[:, t, :], rs[:, t, :]))
                step(tt(rs[:, t, :], rs[:, t, :], ngate[:, t * 24 + 3 * h + 1:t * 24 + 3 * h + 3], ALU.mult))
                step(ts(sm[:, t, 0, 0:nk], sm[:, t, 0, 0:nk], rs[:, t, 0:1], None, ALU.mult))
                pscaled.inc(ts(sm[:, t, 1, 0:nk], sm[:, t, 1, 0:nk], rs[:, t, 1:2], None, ALU.mult))
                if r < 14:
                    if r % 2 == 0:
                        fraction(r // 2 + 1)
                    else:
                        cosines(r // 2 + 1)
                if r < 12:
                    j = r // 3
                    if r % 3 == 1:
                        dve.wait_ge(consumed, place.count(D_CONV[r]) + RING)
                        evac2.wait(dve, BY_ACT2.index(f"cv{r - 1}") + 1)
                        emptied(f"cv{r}", tt(zpad[:, 2:], bank2(f"cv{r}", slice(0, S)), cc[:, :], ALU.mult))
                        vec2.wait(dve, vec2.k)
                        cz.inc(ts(cvt[:, :], zpad[:, 0:S], par[:, PN["cw"]][:, 3 * j:3 * j + 1], None, ALU.mult))
                        cz.wait(dve, j + 1)
                    if r % 3 == 2:
                        for k in range(1, 3):
                            step(stt(out=cvt[:, :], in0=zpad[:, k:k + S], scalar=par[:, PN["cw"]][:, 3 * j + k:3 * j + k + 1], in1=cvt[:, :], op0=ALU.mult, op1=ALU.add))
                        evac2.wait(dve, BY_ACT2.index(f"cv{r}") + 1)
                        cv32.inc(tt(cvt[:, :], cvt[:, :], cb[:, :], ALU.mult))
                if r in SPLIT_AFTER:
                    split_lo(dve, place, SPLIT_AFTER[r])
                if r < 12 and r % 3 == 2:
                    cv_hi.wait(dve, j + 1)
                    cv_split.inc(tt(cvlo[:, j, :], cvt[:, :], cvhi[:, j, :].bitcast(F32), ALU.subtract))
                if r % 4 == 1 and r > 1:
                    s5_low(r // 4 - 1)
            s5_sum(3)
            s5_low(3)
            for t in range(T):
                job2.wait(dve, JOB2["pv15"])
                otok_ready.inc(nc.vector.tensor_copy(otok[:, t, :], acc[:, 0, t * 512:(t + 1) * 512]))
            for b in range(4):
                o_hi.wait(dve, b + 1)
                ins = tt(olo[:, b, :], bank2(f"ot{b}", slice(0, S)), ohi[:, b, :].bitcast(F32), ALU.subtract)
                emptied(f"ot{b}", ins)

            def mixed_low(i):
                mix_hi.wait(dve, i + 1)
                mix_lo.inc(tt(mxlo[:, i, :], mt[:, 0, :], mxhi[:, i, :].bitcast(F32), ALU.subtract))
                mix_lo.wait(dve, i + 1)

            for i in range(KD):
                c = LATE[f"lin{i}"]
                late = [LATE[f"g{i}{b}"] for b in range(3) if (i, b) not in EARLY]
                split_lo(dve, place, [g + 6 for g in late])
                if i:
                    mixed_low(i - 1)
                sgl_ready.wait(dve, i + 1)
                if late:
                    evac2.wait(dve, BY_ACT2.index(f"g{i}2") + 1)
                if len(late) < 3:
                    early_gate.wait(dve, min(3 * i + 3, len(EARLY)))
                emptied(f"lin{i}", tt(mt[:, 0, :], bank2(f"lin{i}", slice(0, S)), sgl[:, i % 2, :], ALU.mult))
                vec2.wait(dve, vec2.k)
                step(tt(mt[:, 0, :], mt[:, 0, :], gsg[:, i % 2, 0, :], ALU.mult))
                split_lo(dve, place, [c + 6])
                dve.wait_ge(consumed, place.count(c + 1) + RING)
                emptied(f"br{i}", tt(mt[:, 1:3, :], bank2(f"br{i}").rearrange("p (b n) -> p b n", b=2), gsg[:, i % 2, 1:3, :], ALU.mult))
                vec2.wait(dve, vec2.k)
                step(tt(mt[:, 0, :], mt[:, 0, :], mt[:, 1, :], ALU.add))
                mix32.inc(tt(mt[:, 0, :], mt[:, 0, :], mt[:, 2, :], ALU.add))
                split_lo(dve, place, [c + 7])
            mixed_low(KD - 1)
            split_lo(dve, place, range(D_OUT + 6, MIX2_CHUNKS + 2))

        def mixround(n):
            return mixsigs["job"].round + n

        def layer_places(l):
            r = l * (LAYER_CHUNKS // RING)
            return [Place(r, b) for b in (FFN_BASES[0], MIX_BASE, FFN_BASES[1])]

        def begin_mix(signals, l):
            for s in signals:
                s.begin(l)

        @block.sync
        def _(sp):
            sp.dma_start(xn[:, :, :], x_in.rearrange("(t p) d -> p t d", p=P)).then_inc(x_loaded, 16)
            for c in range(RING):
                sp.dma_start(chunk(raw, Place(0, 0), c), stream[c]).then_inc(arrived[c], 16)
            with sp.Fori(1, TOTAL // RING) as i:
                for c in range(RING):
                    sp.wait_ge(lo_ready, i * RING + (c - RING + 1))
                    sp.dma_start(chunk(raw, Place(0, 0), c), stream[i * RING + c]).then_inc(arrived[c], 16)
            for c in range(TOTAL // RING * RING, TOTAL):
                sp.wait_ge(lo_ready, c - RING + 1)
                sp.dma_start(chunk(raw, Place(0, 0), c % RING), stream[c]).then_inc(arrived[c % RING], 16)
            for t in range(T):
                sp.wait_ge(x_ready, 2 * T * 8 + 2 * t + 2)
                sp.dma_start(out[t * P:(t + 1) * P], x[:, t, :]).then_inc(out_stored, 16)
            sp.wait_ge(out_stored, T * 16)

        @block.gpsimd
        def _(pool):
            nc.gpsimd.memset(ident[:, :], 0.0).then_inc(pads, 1)
            nc.gpsimd.memset(upper[:, :], 1.0).then_inc(pads, 1)
            nc.gpsimd.memset(maskadd[:, :], 0.0).then_inc(pads, 1)
            nc.gpsimd.memset(recpad[:, :, 0:3], 0.0).then_inc(pads, 1)
            nc.gpsimd.memset(xbcpad[:, :, 0:3], 0.0).then_inc(pads, 1)
            nc.gpsimd.memset(lnm[:, :, :], 0.0).then_inc(pads, 1)
            pool.wait_ge(pads, 6)
            nc.gpsimd.affine_select(out=ident[:, :], in_=ident[:, :], compare_op=ALU.not_equal, fill=1.0, base=0, pattern=[[-1, P]], channel_multiplier=1).then_inc(consts, 1)
            nc.gpsimd.affine_select(out=upper[:, :], in_=upper[:, :], compare_op=ALU.is_ge, fill=0.0, base=0, pattern=[[1, S]], channel_multiplier=-1).then_inc(consts, 1)
            nc.gpsimd.affine_select(out=maskadd[:, :], in_=maskadd[:, :], compare_op=ALU.is_ge, fill=NEG, base=0, pattern=[[1, S]], channel_multiplier=-1).then_inc(consts, 1)
            nc.gpsimd.memset(small[:, 0:1], -0.5).then_inc(consts, 1)
            nc.gpsimd.memset(small[:, 1:2], EPS).then_inc(consts, 1)
            pool.wait_ge(consts, 5)
            norm_pool(pool, 0)
            with pool.Fori(0, LAYERS) as l:
                norm_pool(pool, l * 3 + 1, l * 3)
                for s in (wst, vms, vrstd, yms, yrstd):
                    s.begin(l)
                begin_mix([vss, yss], l)
                mixsigs["job"].round = l
                mix_pool(pool)
                norm_pool(pool, l * 3 + 2, l * 3 + 1)
                norm_pool(pool, l * 3 + 3, l * 3 + 2)
            pool.wait_ge(x_ready, 2 * T * 7)
            ints = frac[:, 0, :].bitcast(mybir.dt.int32)
            nc.gpsimd.iota(ints, pattern=[[1, S]], base=0, channel_multiplier=0).then_inc(pads, 1)
            nc.gpsimd.memset(qmask[:, :], 0.0).then_inc(pads, 1)
            nc.gpsimd.memset(cmask[:, :, 0, :], 0.0).then_inc(pads, 1)
            nc.gpsimd.memset(cmask[:, :, 1, :], 1.0).then_inc(pads, 1)
            nc.gpsimd.memset(halves[:, :], -0.5).then_inc(pads, 1)
            nc.gpsimd.memset(magic[:, 0:1], MAGIC).then_inc(pads, 1)
            nc.gpsimd.memset(magic[:, 1:2], -MAGIC).then_inc(pads, 1)
            nc.gpsimd.memset(zpad[:, 0:2], 0.0).then_inc(consts2, 1)
            nc.gpsimd.memset(pc[:, :, :, :], 0.0).then_inc(consts2, 1)
            pool.wait_ge(pads, 13)
            nc.gpsimd.tensor_copy(tokens_f[:, :], ints).then_inc(consts2, 1)
            nc.gpsimd.affine_select(out=qmask[:, :], in_=qmask[:, :], compare_op=ALU.is_ge, fill=NEG, base=P, pattern=[[-1, S]], channel_multiplier=1).then_inc(consts2, 1)
            for i, fill in enumerate((NEG, 0.0)):
                nc.gpsimd.affine_select(out=cmask[:, :, i, :], in_=cmask[:, :, i, :], compare_op=ALU.is_ge, fill=fill, base=-31, pattern=[[P, T], [-32, 8]], channel_multiplier=1).then_inc(consts2, 1)
            nc.gpsimd.memset(cst[:, :], 0.0).then_inc(consts2, 1)
            mix2_pool(pool)
            norm_pool(pool, 7)

        @block.scalar
        def _(act):
            act.dma_start(pfa[:, :], pf_a[0]).then_inc(pfa_loaded, 16)
            act.wait_ge(credits, 1)
            act.wait_ge(pfa_loaded, 16)
            prenorm_act(act, 0, pfa[:, PF["pre_g"]], Place(0, 0), range(2))
            split_hi(act, Place(0, 0), range(2, 4))
            with act.Fori(0, LAYERS) as l:
                begin_mix(mixsigs.values(), l)
                mixsigs["job"].round = l
                f1, mx, f2 = layer_places(l)
                act.dma_start(par[:, :], pm[l]).then_inc(par_loaded, 16)
                act.dma_start(pfb[:, :], pf_b[l]).then_inc(pfb_loaded, 16)
                ffn_act(act, l * 2, f1)
                act.wait_ge(par_loaded, (l + 1) * 16)
                post_squares(act, l * 3, f1.count(FFN_CHUNKS - 1), 0.5)
                prenorm_act(act, l * 3 + 1, par[:, PM["pre_g"]])
                act.dma_start(pfa[:, :], pf_a[l + 1]).then_inc(pfa_loaded, 16)
                mix_act(act, mx)
                act.wait_ge(pfb_loaded, (l + 1) * 16)
                post_squares(act, l * 3 + 1, mx.count(C_OUT + KD - 1), 1)
                prenorm_act(act, l * 3 + 2, pfb[:, PF["pre_g"]])
                ffn_act(act, l * 2 + 1, f2)
                act.wait_ge(pfa_loaded, (l + 2) * 16)
                post_squares(act, l * 3 + 2, f2.count(FFN_CHUNKS - 1), 0.5)
                prenorm_act(act, l * 3 + 3, pfa[:, PF["pre_g"]])
            act.dma_start(par[:, 0:NPN], pm2).then_inc(par_loaded, 16)
            act.wait_ge(consts2, 7)
            mix2_act(act, Place(0, MIX2_BASE))
            prenorm_act(act, 7, par[:, PN["ffn_g"]])
            ffn_act(act, 4, Place(0, FFN3_BASE), last=True)

        @block.vector
        def _(dve):
            dve.wait_ge(x_loaded, 16)
            for t in range(T):
                for h in range(2):
                    nc.vector.tensor_copy(x[:, t, halves_of(h)], xn[:, t, halves_of(h)]).then_inc(x_ready, 1)
            dve.wait_ge(consts, 5)
            dve.wait_ge(pfa_loaded, 16)
            norm_dve(dve, 0, pfa[:, PF["pre_g"]])
            split_lo(dve, Place(0, 0), range(4))
            with dve.Fori(0, LAYERS) as l:
                begin_mix(mixsigs.values(), l)
                mixsigs["job"].round = l
                f1, mx, f2 = layer_places(l)
                ffn_dve(dve, l * 2, f1)
                dve.wait_ge(par_loaded, (l + 1) * 16)
                norm_dve(dve, l * 3 + 1, par[:, PM["pre_g"]], post_updates(dve, l * 3, pfa[:, PF["post_g"]], 0.5), f1, ffn_late)
                mix_dve(dve, mx)
                dve.wait_ge(pfb_loaded, (l + 1) * 16)
                norm_dve(dve, l * 3 + 2, pfb[:, PF["pre_g"]], post_updates(dve, l * 3 + 1, par[:, PM["post_g"]], 1), mx, [MIX_CHUNKS + 1, MIX_CHUNKS + 2])
                ffn_dve(dve, l * 2 + 1, f2)
                dve.wait_ge(pfa_loaded, (l + 2) * 16)
                norm_dve(dve, l * 3 + 3, pfa[:, PF["pre_g"]], post_updates(dve, l * 3 + 2, pfb[:, PF["post_g"]], 0.5), f2, ffn_late)
            dve.wait_ge(par_loaded, (LAYERS + 1) * 16)
            dve.wait_ge(consts2, 7)
            mix2_dve(dve, Place(0, MIX2_BASE))
            norm_dve(dve, 7, par[:, PN["ffn_g"]], (lambda: plain_update(dve, 6, 0, FFN3_BASE), lambda: None, lambda: plain_update(dve, 6, 1, FFN3_BASE)), Place(0, FFN3_BASE), [2, 3])
            ffn_dve(dve, 4, Place(0, FFN3_BASE), last=True)
            for t in range(T):
                plain_update(dve, 7, t, TOTAL)

        @block.tensor
        def _(pe):
            pe.sem_inc(consumed, RING)
            pe.sem_inc(credits, 1)
            pe.wait_ge(consts, 5)
            norm_pe(pe, 0)
            with pe.Fori(0, LAYERS) as l:
                begin_mix(mixsigs.values(), l)
                f1, mx, f2 = layer_places(l)
                ffn_pe(pe, l * 2, l * 3, f1)
                norm_pe(pe, l * 3 + 1, padding=True)
                mix_pe(pe, l * 3 + 1, mx)
                norm_pe(pe, l * 3 + 2)
                ffn_pe(pe, l * 2 + 1, l * 3 + 2, f2)
                norm_pe(pe, l * 3 + 3)
            mix2_pe(pe, 6, Place(0, MIX2_BASE))
            norm_pe(pe, 7)
            ffn_pe(pe, 4, 7, Place(0, FFN3_BASE))


def channel_chunks(w):
    k, n = w.shape
    return w.reshape(k // P, P, n // P, P).transpose(2, 1, 0, 3).reshape(n // P, P, -1)


def region(w):
    import numpy as np
    k, n = w.shape
    flat = w.reshape(k // P, P, n).transpose(1, 0, 2).reshape(P, -1)
    chunks = -(-flat.shape[1] // CH)
    flat = np.concatenate([flat, np.zeros((P, chunks * CH - flat.shape[1]), w.dtype)], axis=1)
    return flat.reshape(P, chunks, CH).transpose(1, 0, 2)


def ffn_chunks(w_gu, w_down):
    gate, up, down = channel_chunks(w_gu[:, :FF]), channel_chunks(w_gu[:, FF:]), w_down.reshape(FT, P, D)
    order = [gate[0], up[0]]
    for j in range(1, FT):
        order += [gate[j], up[j], down[j - 1]]
    return order + [down[FT - 1]]


def mix_chunks(w_in, w_out):
    import numpy as np
    cut = np.cumsum([AW, AW, BW, XB * P, HEADS, 2 * CW])[:-1]
    gate, rec, z, xbc, dt, uv = np.split(w_in, cut, axis=1)
    gate = channel_chunks(gate)
    rows = w_out.reshape(KD, P, D)
    return ([np.zeros((P, CH), w_in.dtype)] + list(channel_chunks(rec)) + list(channel_chunks(xbc)) + list(region(dt)) + [gate[0]]
            + list(region(uv)) + [gate[1], gate[2]] + list(region(z)) + [rows[k] for k in OUT_ORDER])


def per_partition(v):
    return v.reshape(-1, P).T


def across(v):
    import numpy as np
    return np.broadcast_to(v.reshape(1, -1), (P, v.size))


def taps(w):
    return w.reshape(w.shape[0], -1, P).transpose(2, 1, 0).reshape(P, -1)


def diagonal(w):
    import numpy as np
    out = np.zeros((P, AB, P), w.dtype)
    for h in range(w.shape[0]):
        r = HD * (h % 2)
        out[r:r + HD, h // 2, r:r + HD] = w[h]
    return out.reshape(P, -1)


def mix_params(a, l):
    import numpy as np
    parts = [per_partition(a["mix_pre_g"][l]), taps(a["lru_conv_w"][l]), per_partition(a["lru_conv_b"][l]),
             taps(a["ssd_conv_w"][l]), per_partition(a["ssd_conv_b"][l]), per_partition(a["lru_b_r"][l]),
             per_partition(a["lru_b_i"][l]), per_partition(a["lru_lambda"][l]), diagonal(a["lru_w_r"][l]), diagonal(a["lru_w_i"][l]),
             across(a["mix_post_g"][l]), across(a["ssd_norm_g"][l]), across(a["sgu_ln_g"][l]), across(a["sgu_ln_b"][l]),
             across(a["ssd_dt_bias"][l]), across(a["ssd_a_log"][l]), across(a["ssd_d"][l]), a["sgu_b_s"][l].T,
             a["sgu_w_s"][l].transpose(2, 0, 1).reshape(P, -1)]
    return np.concatenate(parts, axis=1)


def mix2_chunks(a):
    import numpy as np
    w = a["w_in_2"][0]
    cut = np.cumsum([512, 512, 512, 512, 512] + [P] * 6 + [24])
    u, c_b, c_c, c_x, q, kc, vc, ks, vs, kw, vw, ng, mg = np.split(w, cut, axis=1)
    twice = [channel_chunks(np.concatenate([v[:, h * HD:(h + 1) * HD]] * 2, axis=1))[0] for v in (kc, vc) for h in range(2)]
    u, c_b, c_c, c_x, mg = [channel_chunks(v) for v in (u, c_b, c_c, c_x, mg)]
    b = np.zeros((4, P, 4, 2, P), w.dtype)
    for g in range(32):
        k, r, j = g // 8, g // 2 % 4, g % 2
        for i, name in enumerate(("ssm_b_re_2", "ssm_b_im_2")):
            b[k, 16 * (g % 8):16 * (g % 8) + 16, r, i, HD * j:HD * (j + 1)] = a[name][0, g].T
    b = b.reshape(4, P, CH)
    chunks = {}
    conv = [v for k in range(4) for v in (c_c[k], c_x[k], c_b[k])]
    chunks.update(zip(D_CONV, conv))
    chunks.update(zip(D_B, b))
    parts = list(region(q)) + twice + list(region(ng)) + [u[0], u[1], u[2]] + list(region(np.concatenate([ks, kw, vs, vw], axis=1))) + [u[3]]
    parts += [c for i in range(2) for c in region(a["cmp_w1_2"][0, i])]
    parts += [mg[b * KD + i] for i, b in EARLY]
    parts += [chunks[c] for c in range(D_ROUNDS, D_ROUNDS + 16)]

    def half(v, i):
        return v[:, i * P:(i + 1) * P].reshape(4, P, P).transpose(1, 0, 2).reshape(P, -1)

    glu, conv_out, w_o = a["ssm_w_glu_2"][0], a["conv_w_out_2"][0], a["nsa_w_o_2"][0]
    for i in range(KD):
        parts += [mg[b * KD + i] for b in range(3) if (i, b) not in EARLY]
        parts += [np.concatenate([half(glu, i), half(glu, KD + i)], axis=1), np.concatenate([half(conv_out, i), half(w_o, i)], axis=1)]
    parts += list(a["w_out_2"][0].reshape(KD, P, D))
    assert len(parts) == MIX2_CHUNKS
    return parts


def mix2_params(a):
    import numpy as np
    c = np.zeros((P, 16, 2, 32), a["ssm_c_re_2"].dtype)
    for g in range(32):
        j = g % 2
        for i, name in enumerate(("ssm_c_re_2", "ssm_c_im_2")):
            c[HD * j:HD * (j + 1), g // 2, i, 16 * j:16 * (j + 1)] = a[name][0, g].T
    states = lambda v: v.reshape(16, P).T
    pe = a["cmp_pe_2"][0].reshape(2, 16, 2 * HD).transpose(2, 0, 1).reshape(P, -1)
    w2 = a["cmp_w2_2"][0].reshape(2, 2, P, HD).transpose(2, 0, 1, 3).reshape(P, -1)
    parts = [taps(a["conv_w_2"][0]), per_partition(a["ssm_d_2"][0]), states(a["ssm_lam_re_2"][0]),
             states(a["ssm_lam_im_2"][0]), states(np.repeat(a["ssm_log_dt_2"][0], HD)), c.reshape(P, -1), across(a["q_norm_g_2"][0]),
             across(a["k_norm_g_2"][0].reshape(-1)), pe, w2, per_partition(a["ffn_norm_g_2"][0])]
    return np.concatenate(parts, axis=1)


def kernel(**inputs):
    import numpy as np
    import concourse.bacc as bacc
    from concourse.bass_utils import run_bass_kernel_spmd as run

    a = {k: np.asarray(v) for k, v in inputs.items()}
    parts = []
    for l in range(LAYERS):
        parts += ffn_chunks(a["ffn1_w_gu"][l], a["ffn1_w_down"][l])
        parts += mix_chunks(a["mix_w_in"][l], a["mix_w_out"][l])
        parts += ffn_chunks(a["ffn2_w_gu"][l], a["ffn2_w_down"][l])
    parts += mix2_chunks(a)
    parts += ffn_chunks(a["ffn_w_gate_up_2"][0], a["ffn_w_down_2"][0])
    ffn_par = lambda pre, post: np.concatenate([per_partition(pre), across(post)], axis=1)
    g3 = a["mix_norm_g_2"][0]
    arrays = {
        "stream": np.stack(parts),
        "x_in": a["x"].reshape(S, D),
        "pf_a": np.stack([ffn_par(a["ffn1_pre_g"][l], a["ffn1_post_g"][l]) for l in range(LAYERS)] + [ffn_par(g3, np.zeros_like(g3))]),
        "pf_b": np.stack([ffn_par(a["ffn2_pre_g"][l], a["ffn2_post_g"][l]) for l in range(LAYERS)]),
        "pm": np.stack([mix_params(a, l) for l in range(LAYERS)]),
        "pm2": mix2_params(a),
    }
    arrays = {k: np.ascontiguousarray(v) for k, v in arrays.items()}
    nc = bacc.Bacc("TRN2", target_bir_lowering=False, num_devices=1)
    args = [nc.dram_tensor(k, v.shape, F32, kind="ExternalInput").ap() for k, v in arrays.items()]
    out = nc.dram_tensor("out", (S, D), F32, kind="ExternalOutput").ap()
    block_program(nc, *args, out)
    r = run(nc, [arrays], core_ids=[0])
    return r.results[0]["out"].reshape(1, S, D)
```
